# Optimizing a Trainium2 kernel written in Bass

```python
import math
import jax
import jax.numpy as jnp
from jax import lax
import numpy as np

D_MODEL = 1024
BATCH = 1
SEQ = 512
DEPTH = 2
DEC_BATCH = 8
DEC_SEQ = 1
PAST_LEN = 256
PAGE_SIZE = 128

N_HEADS = 16
HEAD_DIM = D_MODEL // N_HEADS
N_KV = 4
HPG = N_HEADS // N_KV
N_BRANCH = 3
CMP_BLOCK = 32
CMP_HIDDEN = HEAD_DIM
SEL_BLOCK = 64
TOP_N = 16
WINDOW = 512
N_BUCKETS = 32
MAX_EXACT = N_BUCKETS // 2
MAX_DISTANCE = 1024
CONV_W = 3
D_FF = 256 * ((8 * D_MODEL // 3 + 255) // 256)
N_A = DEPTH // 2
N_B = DEPTH - N_A
Q_BLOCK = 32
EPS = 1e-6

kernel_name = 'yoco_shortconv_nsa_decoder_step'

def rmsnorm(x, g):
    xf = x.astype(jnp.float32)
    y = xf * lax.rsqrt(jnp.mean(xf * xf, axis=-1, keepdims=True) + EPS)
    return (y * g.astype(jnp.float32)).astype(x.dtype)

def modulated_norm(x, c, w_mod, b_mod, g):
    shift, scale, gate = jnp.split(c @ w_mod + b_mod, 3, axis=-1)
    h = rmsnorm(x, g) * (1 + scale[:, None, :]) + shift[:, None, :]
    return h, gate[:, None, :]

def causal_conv(x, prev, w, b):
    L = x.shape[1]
    xx = jnp.concatenate([prev.astype(x.dtype), x], axis=1)
    y = sum(w[j] * xx[:, j:j + L] for j in range(CONV_W)) + b
    return y, xx[:, L:]

def short_conv_mixer(h, prev, w_in, conv_w, conv_b, w_out):
    bg, cg, u = jnp.split(h @ w_in, 3, axis=-1)
    y, st = causal_conv(cg * u, prev, conv_w, conv_b)
    return (bg * y) @ w_out, st

def conv_ffn(h, prev, w_up, conv_w, conv_b, w_down):
    up, st = causal_conv(h @ w_up, prev, conv_w, conv_b)
    u, g = jnp.split(up, 2, axis=-1)
    return (jax.nn.silu(g) * u) @ w_down, st

def t5_bucket(n):
    n = jnp.maximum(n, 0)
    nf = jnp.maximum(n, 1).astype(jnp.float32)
    large = MAX_EXACT + (jnp.log(nf / MAX_EXACT) / math.log(MAX_DISTANCE / MAX_EXACT)
                         * (N_BUCKETS - MAX_EXACT)).astype(jnp.int32)
    return jnp.where(n < MAX_EXACT, n, jnp.minimum(large, N_BUCKETS - 1))

def masked_softmax(s, mask):
    s = jnp.where(mask, s, -jnp.inf)
    m = jnp.max(s, axis=-1, keepdims=True)
    m = jnp.where(jnp.isfinite(m), m, 0.0)
    p = jnp.exp(s - m)
    d = jnp.sum(p, axis=-1, keepdims=True)
    return p / jnp.where(d > 0, d, 1.0)

def compress_blocks(rows, pe, w1, w2):
    B, Lp = rows.shape[0], rows.shape[1]
    nb = Lp // CMP_BLOCK
    blk = rows.reshape(B, nb, CMP_BLOCK, N_KV, HEAD_DIM) + pe[None, None, :, None, :]
    flat = blk.transpose(0, 1, 3, 2, 4).reshape(B, nb, N_KV, CMP_BLOCK * HEAD_DIM)
    return jax.nn.gelu(flat @ w1) @ w2

def nsa_attend(q, gates, k_cb, v_cb, k_sel, v_sel, k_win, v_win, q_pos0, win_pos0, rel_bias):
    f32 = jnp.float32
    B, Q = q.shape[0], q.shape[1]
    n_cb = k_cb.shape[1]
    n_sb = k_sel.shape[1] // SEL_BLOCK
    n_sel = min(TOP_N, n_sb)
    qc_len = Q_BLOCK if Q % Q_BLOCK == 0 else Q
    n_chunks = Q // qc_len
    n_kw = WINDOW + qc_len - 1
    k_sb = k_sel.reshape(B, n_sb, SEL_BLOCK, N_KV, HEAD_DIM).transpose(0, 3, 1, 2, 4)
    v_sb = v_sel.reshape(B, n_sb, SEL_BLOCK, N_KV, HEAD_DIM).transpose(0, 3, 1, 2, 4)
    pad_w = ((0, 0), (WINDOW, 0), (0, 0), (0, 0))
    kw_pad = jnp.pad(k_win, pad_w)
    vw_pad = jnp.pad(v_win, pad_w)
    tab = rel_bias.astype(f32)
    tab_g = tab.T.reshape(N_KV, HPG, N_BUCKETS)
    cmp_end = jnp.arange(n_cb) * CMP_BLOCK + (CMP_BLOCK - 1)
    blk = jnp.arange(n_sb)

    def head_bias(d):
        return tab[t5_bucket(d)].reshape(d.shape[0], d.shape[1], N_KV, HPG).transpose(0, 2, 3, 1)

    def sel_group(q_g, ksb_g, vsb_g, idx_g, bkt_g, ok_g, tab_h):
        kg = jax.vmap(lambda kb, ix: kb[ix])(ksb_g, idx_g).reshape(B, qc_len, n_sel * SEL_BLOCK, HEAD_DIM)
        vg = jax.vmap(lambda vb, ix: vb[ix])(vsb_g, idx_g).reshape(B, qc_len, n_sel * SEL_BLOCK, HEAD_DIM)
        s = jnp.einsum('bqhd,bqkd->bqhk', q_g, kg.astype(f32)) + jnp.moveaxis(tab_h[:, bkt_g], 0, 2)
        p = masked_softmax(s, ok_g[:, :, None, :])
        return jnp.einsum('bqhk,bqkd->bqhd', p, vg.astype(f32))

    def chunk(ci):
        start = ci * qc_len
        qs = q_pos0 + start
        qc = lax.dynamic_slice_in_dim(q, start, qc_len, axis=1).astype(f32)
        gc = lax.dynamic_slice_in_dim(gates, start, qc_len, axis=1).astype(f32)
        t = qs + jnp.arange(qc_len)
        d_c = t[:, None] - cmp_end[None, :]
        s_c = jnp.einsum('bqghd,bngd->bqghn', qc, k_cb.astype(f32)) + head_bias(d_c)
        p_c = masked_softmax(s_c, (d_c >= 0)[:, None, None, :])
        o_c = jnp.einsum('bqghn,bngd->bqghd', p_c, v_cb.astype(f32))
        imp = p_c.sum(axis=3).reshape(B, qc_len, N_KV, n_sb, SEL_BLOCK // CMP_BLOCK).sum(axis=-1)
        cur = (t // SEL_BLOCK)[:, None]
        valid = blk[None, :] <= cur
        forced = (blk[None, :] == 0) | (blk[None, :] == cur) | (blk[None, :] == cur - 1)
        score = jnp.where((valid & forced)[None, :, None, :], jnp.inf,
                          jnp.where(valid[None, :, None, :], imp, -jnp.inf))
        top_val, top_idx = lax.top_k(score, n_sel)
        pos = top_idx[..., None] * SEL_BLOCK + jnp.arange(SEL_BLOCK)
        ok = (top_val > -jnp.inf)[..., None] & (pos <= t[None, :, None, None, None])
        pos = pos.reshape(B, qc_len, N_KV, n_sel * SEL_BLOCK)
        ok = ok.reshape(B, qc_len, N_KV, n_sel * SEL_BLOCK)
        bkt = t5_bucket(t[None, :, None, None] - pos)
        o_s = jax.vmap(sel_group, in_axes=(2, 1, 1, 2, 2, 2, 0), out_axes=2)(
            qc, k_sb, v_sb, top_idx, bkt, ok, tab_g)
        w0 = qs - win_pos0 + 1
        kw = lax.dynamic_slice_in_dim(kw_pad, w0, n_kw, axis=1).astype(f32)
        vw = lax.dynamic_slice_in_dim(vw_pad, w0, n_kw, axis=1).astype(f32)
        s_pos = qs - WINDOW + 1 + jnp.arange(n_kw)
        d_w = t[:, None] - s_pos[None, :]
        ok_w = (d_w >= 0) & (d_w < WINDOW) & (s_pos[None, :] >= win_pos0)
        s_w = jnp.einsum('bqghd,bkgd->bqghk', qc, kw) + head_bias(d_w)
        p_w = masked_softmax(s_w, ok_w[:, None, None, :])
        o_w = jnp.einsum('bqghk,bkgd->bqghd', p_w, vw)
        o = gc[..., 0:1] * o_c + gc[..., 1:2] * o_s + gc[..., 2:3] * o_w
        return o.astype(q.dtype)

    out = lax.map(chunk, jnp.arange(n_chunks))
    return jnp.moveaxis(out, 0, 1).reshape(B, Q, N_KV, HPG, HEAD_DIM)

def nsa_mixer(h, shared, pos0, w_qg, w_out, rel_bias):
    B, S = h.shape[0], h.shape[1]
    nq = N_HEADS * HEAD_DIM
    qg = h @ w_qg
    q = (qg[..., :nq] * HEAD_DIM ** -0.5).reshape(B, S, N_KV, HPG, HEAD_DIM)
    gates = jax.nn.sigmoid(qg[..., nq:].astype(jnp.float32)).reshape(B, S, N_KV, HPG, N_BRANCH)
    k_cb, v_cb, k_sel, v_sel, k_win, v_win, win_pos0 = shared
    o = nsa_attend(q, gates, k_cb, v_cb, k_sel, v_sel, k_win, v_win, pos0, win_pos0, rel_bias)
    return o.reshape(B, S, nq) @ w_out

def shared_kv(x, c, past_kv, past_win, page_table, kv_mod_w, kv_mod_b, kv_norm_g, w_kv,
              cmp_pe, cmp_w1, cmp_w2):
    Bn, S = x.shape[0], x.shape[1]
    shift, scale = jnp.split(c @ kv_mod_w + kv_mod_b, 2, axis=-1)
    hk = rmsnorm(x, kv_norm_g) * (1 + scale[:, None, :]) + shift[:, None, :]
    kv = (hk @ w_kv).reshape(Bn, S, 6, N_KV, HEAD_DIM)
    rows, win_rows = kv[:, :, :4], kv[:, :, 4:]
    if past_kv is None:
        full, wfull, win_pos0, keep = rows, win_rows, 0, min(WINDOW, S)
    else:
        past = past_kv[page_table].reshape(Bn, PAST_LEN, 4, N_KV, HEAD_DIM).astype(rows.dtype)
        full = jnp.concatenate([past, rows], axis=1)
        keep = past_win.shape[1]
        wfull = jnp.concatenate([past_win.astype(rows.dtype), win_rows], axis=1)
        win_pos0 = PAST_LEN - keep
    pad = (-full.shape[1]) % SEL_BLOCK
    full = jnp.pad(full, ((0, 0), (0, pad), (0, 0), (0, 0), (0, 0)))
    k_cb = compress_blocks(full[:, :, 0], cmp_pe[0], cmp_w1[0], cmp_w2[0])
    v_cb = compress_blocks(full[:, :, 1], cmp_pe[1], cmp_w1[1], cmp_w2[1])
    shared = (k_cb, v_cb, full[:, :, 2], full[:, :, 3], wfull[:, :, 0], wfull[:, :, 1], win_pos0)
    return shared, rows, wfull[:, wfull.shape[1] - keep:]

def setup_inputs(seed: int = 0) -> dict:
    key = jax.random.key(seed)
    ks = iter(jax.random.split(key, 40))
    D = D_MODEL

    def nrm(shape, scale):
        return jax.random.normal(next(ks), shape, jnp.float32) * scale

    n_pages = PAST_LEN // PAGE_SIZE
    n_used = DEC_BATCH * n_pages
    n_pool = n_used + n_used // 4
    win_buf = min(WINDOW, PAST_LEN)
    return {
        'x_prompt': nrm((BATCH, SEQ, D), 1.0),
        'x_sample': nrm((DEC_BATCH, DEC_SEQ, D), 1.0),
        'c_prompt': nrm((BATCH, D), 1.0),
        'c_sample': nrm((DEC_BATCH, D), 1.0),
        'cache_kv': nrm((n_pool, PAGE_SIZE, 4, N_KV, HEAD_DIM), 1.0),
        'cache_win': nrm((DEC_BATCH, win_buf, 2, N_KV, HEAD_DIM), 1.0),
        'state_conv_a': nrm((N_A, DEC_BATCH, CONV_W - 1, D), 1.0),
        'state_ffn_conv': nrm((DEPTH, DEC_BATCH, CONV_W - 1, 2 * D_FF), 1.0),
        'page_table': jax.random.permutation(next(ks), n_pool)[:n_used].reshape(DEC_BATCH, n_pages).astype(jnp.int32),
        'mod_w': nrm((DEPTH, 2, D, 3 * D), 0.5 * D ** -0.5),
        'mod_b': nrm((DEPTH, 2, 3 * D), 0.01),
        'norm_g': 1.0 + nrm((DEPTH, 4, D), 0.05),
        'a_w_in': nrm((N_A, D, 3 * D), D ** -0.5),
        'a_conv_w': nrm((N_A, CONV_W, D), CONV_W ** -0.5),
        'a_conv_b': nrm((N_A, D), 0.01),
        'a_w_out': nrm((N_A, D, D), D ** -0.5),
        'kv_mod_w': nrm((D, 2 * D), 0.5 * D ** -0.5),
        'kv_mod_b': nrm((2 * D,), 0.01),
        'kv_norm_g': 1.0 + nrm((D,), 0.05),
        'w_kv': nrm((D, 6 * N_KV * HEAD_DIM), D ** -0.5),
        'cmp_pe': nrm((2, CMP_BLOCK, HEAD_DIM), 0.1),
        'cmp_w1': nrm((2, CMP_BLOCK * HEAD_DIM, CMP_HIDDEN), (CMP_BLOCK * HEAD_DIM) ** -0.5),
        'cmp_w2': nrm((2, CMP_HIDDEN, HEAD_DIM), CMP_HIDDEN ** -0.5),
        'b_w_qg': nrm((N_B, D, N_HEADS * HEAD_DIM + N_BRANCH * N_HEADS), D ** -0.5),
        'b_w_out': nrm((N_B, N_HEADS * HEAD_DIM, D), (N_HEADS * HEAD_DIM) ** -0.5),
        'rel_bias': nrm((N_BUCKETS, N_HEADS), 0.5),
        'ffn_w_up': nrm((DEPTH, D, 2 * D_FF), D ** -0.5),
        'ffn_conv_w': nrm((DEPTH, CONV_W, 2 * D_FF), CONV_W ** -0.5),
        'ffn_conv_b': nrm((DEPTH, 2 * D_FF), 0.01),
        'ffn_w_down': nrm((DEPTH, D_FF, D), D_FF ** -0.5),
    }

def reference(x_prompt, x_sample, c_prompt, c_sample, cache_kv, cache_win, state_conv_a,
              state_ffn_conv, page_table, mod_w, mod_b, norm_g, a_w_in, a_conv_w, a_conv_b,
              a_w_out, kv_mod_w, kv_mod_b, kv_norm_g, w_kv, cmp_pe, cmp_w1, cmp_w2, b_w_qg,
              b_w_out, rel_bias, ffn_w_up, ffn_conv_w, ffn_conv_b, ffn_w_down):

    def trunk(x, c, conv_a_prev, ffn_prev, past_kv, past_win, pos0):
        conv_a_new, ffn_new = [], []
        shared, kv_rows, win_state = None, None, None
        for l in range(DEPTH):
            h, gate = modulated_norm(x, c, mod_w[l, 0], mod_b[l, 0], norm_g[l, 0])
            if l < N_A:
                o, st = short_conv_mixer(h, conv_a_prev[l], a_w_in[l], a_conv_w[l], a_conv_b[l], a_w_out[l])
                conv_a_new.append(st)
            else:
                if shared is None:
                    shared, kv_rows, win_state = shared_kv(
                        x, c, past_kv, past_win, page_table, kv_mod_w, kv_mod_b, kv_norm_g, w_kv,
                        cmp_pe, cmp_w1, cmp_w2)
                o = nsa_mixer(h, shared, pos0, b_w_qg[l - N_A], b_w_out[l - N_A], rel_bias)
            x = x + gate * rmsnorm(o, norm_g[l, 1])
            h, gate = modulated_norm(x, c, mod_w[l, 1], mod_b[l, 1], norm_g[l, 2])
            o, st = conv_ffn(h, ffn_prev[l], ffn_w_up[l], ffn_conv_w[l], ffn_conv_b[l], ffn_w_down[l])
            ffn_new.append(st)
            x = x + gate * rmsnorm(o, norm_g[l, 3])
        return x, kv_rows, win_state, jnp.stack(conv_a_new), jnp.stack(ffn_new)

    bp = x_prompt.shape[0]
    zeros_a = jnp.zeros((N_A, bp, CONV_W - 1, D_MODEL), x_prompt.dtype)
    zeros_f = jnp.zeros((DEPTH, bp, CONV_W - 1, 2 * D_FF), x_prompt.dtype)
    y_prompt, kv_p, win_p, conv_a_p, ffn_p = trunk(x_prompt, c_prompt, zeros_a, zeros_f, None, None, 0)
    y_sample, kv_s, win_s, conv_a_s, ffn_s = trunk(x_sample, c_sample, state_conv_a, state_ffn_conv,
                                                   cache_kv, cache_win, PAST_LEN)
    return (y_prompt, y_sample, kv_p, kv_s, win_p, win_s, conv_a_p, conv_a_s, ffn_p, ffn_s)


_drawn_inputs = setup_inputs


def setup_inputs(seed=0):
    import zlib

    import numpy as np

    out = dict(_drawn_inputs(seed))
    spreads = {}
    factors = {'a_conv_b': 8.0, 'kv_mod_b': 4.819, 'ffn_conv_b': 8.0}
    for name, (base, spread) in spreads.items():
        noise = np.random.default_rng([zlib.crc32(name.encode()), seed]).standard_normal(out[name].shape)
        drawn = base * np.exp(spread * noise) if base else spread * noise
        out[name] = jnp.asarray(drawn.astype(out[name].dtype))
    for name, factor in factors.items():
        out[name] = (out[name] * factor).astype(out[name].dtype)
    return out
```

```python
import math
from contextlib import ExitStack

import numpy as np
import concourse.bass as bass
from concourse import mybir

D = 1024
NP = 512
NS = 8
NT = NP + NS
HALF = NT // 2
KT = D // 128
FF = 2816
FT = FF // 128
FH = FT // 2
NC9 = NS + 1
HD = 64
PAST = 256
EPS = 1e-6
NEG = -1.0e30
FLOOR = -1.0e29
PSO = 512 - HALF
R_MODB, R_KVG, R_ACB = 0, 112, 120
R_NG, R_ACW = 128, 192
R_FCB, R_FCW = 256, 384
R_STA, R_STF = 768, 896
R_C, R_XS = 2304, 2432
PT_TILES = 20
UNITS = [("mix_in", 24), ("mix_out", 8), ("up00", 22), ("down00", 8), ("up01", 22), ("down01", 8),
         ("kv", 12), ("q", 8), ("attn_out", 8), ("up10", 22), ("down10", 8), ("up11", 22), ("down11", 8)]
UBASE, _n = {}, 0
for _name, _c in UNITS:
    UBASE[_name] = _n
    _n += _c
KV_SLOTS = [0, 1, 3, 5, 2, 4]
MOD_CHUNKS = 28


S_ITEMS, N_TABLES = [], 14
for _u in range(2):
    S_ITEMS += [(_u, None), (_u, None)]
    S_ITEMS += [(_u, (16 * _u + 8 * f + 4 * br + 3 - i, f, br, i)) for f in range(2) for br in range(2)
                for i in (3, 2, 1, 0)]


NSI = len(S_ITEMS)


def bucket(d):
    if d < 16:
        return max(d, 0)
    f = np.float32(np.log(np.float32(d) / np.float32(16)))
    return min(16 + int(np.float32(f / np.float32(math.log(64)) * np.float32(16))), 31)


def constants():
    ident = np.eye(128, dtype=np.float32)
    line = np.zeros((33, 1024), np.float32)
    for x in range(1024):
        if x < 512:
            line[32, x] = NEG
        else:
            line[bucket(x - 512), x] = 1
    srow = np.zeros((32, 328), np.float32)
    for j in range(256):
        srow[bucket(256 - j), j] = 1
    srow[0, 256:264] = 1
    for b in range(8):
        for n in range(8):
            srow[bucket(256 - 32 * n - 31), 264 + 8 * b + n] = 1
    smask = np.zeros((128, 72), np.float32)
    for r in range(128):
        for b in range(8):
            if b != r % 8:
                smask[r, b] = NEG
                smask[r, 8 + 8 * b:16 + 8 * b] = NEG
    rep = np.tile(np.eye(16, dtype=np.float32), (1, 8))
    blk = np.kron(np.eye(8, dtype=np.float32), np.ones((16, 1), np.float32))
    return dict(c_ident=ident, c_line=line, c_srow=srow, c_smask=smask, c_rep=rep, c_blk=blk)


def decoder_step(nc, A, O):
    f32 = mybir.dt.float32
    f32r = mybir.dt.float32r
    i32 = mybir.dt.int32
    ALU = mybir.AluOpType
    ACT = mybir.ActivationFunctionType
    AX = mybir.AxisListType

    ctx = ExitStack()
    with ctx:
        base = (nc.sbuf_base + 63) // 64 * 64
        at = [base]

        def place(name, shape, dt=f32, offset=None):
            n = int(np.prod(shape[1:])) * 4
            if offset is None:
                offset = at[0]
                at[0] += (n + 31) // 32 * 32
            t = nc.alloc_sbuf_tensor_at(name, list(shape), dt, offset=offset)
            return t, offset

        def keep(name, *shape, dt=f32):
            return place(name, shape, dt)[0]

        x = keep("x", 128, KT, NT)
        o, o_at = place("o", (128, KT, NT))
        h_hi, h_at = place("h_hi", (128, KT, NT), f32r)
        h_lo = keep("h_lo", 128, KT, NT, dt=f32r)
        w_raw = [keep(f"w_raw{s}", 128, FH, 128) for s in range(2)]
        w_hi = [keep(f"w_hi{s}", 128, FH, 128, dt=f32r) for s in range(2)]
        w_lo = [keep(f"w_lo{s}", 128, FH, 128, dt=f32r) for s in range(2)]
        PT = keep("PT", 128, PT_TILES * 128)
        modT = keep("modT", 128, 4 * MOD_CHUNKS, NC9)
        ident = keep("ident", 128, 128)
        ones = keep("ones", 128, 128)
        srow = keep("srow", 32, 328)
        smask = keep("smask", 128, 72)
        rep = keep("rep", 16, 128)
        blk = keep("blk", 128, 8)
        tab = keep("tab", 33, 16)
        tabr = keep("tabr", 32, 128)
        tabp = keep("tabp", 33, 16)
        sca = keep("sca", 128, KT, NS)
        scf = keep("scf", 128, 2, 2 * FT, NS)
        up10 = keep("up10", 128, 10, 2 * FT)
        z10 = keep("z10", 128, 10, KT)
        zflag = keep("zflag", 128, 1)
        hemb = keep("hemb", 128, 1)
        pti = keep("pti", 1, 16, dt=i32)
        n_at = at[0]
        rstd = keep("rstd", 128, NT)
        sq = keep("sq", 128, NT)
        sqt = [keep(f"sqt{s}", 128, NT) for s in range(2)]
        nt = [keep(f"nt{s}", 128, NT) for s in range(2)]
        hf = [keep(f"hf{s}", 128, NT) for s in range(2)]
        n_end = at[0]
        ts = keep("ts", 128, KT, NS)
        st = keep("st", 88, 5, 128)
        st_z = keep("st_z", 80, 128)
        z_at = at[0]

        def layer(start):
            pos = [start]

            def put(name, *shape, dt=f32):
                t, off = place(name, shape, dt, pos[0])
                pos[0] += (int(np.prod(shape[1:])) * 4 + 31) // 32 * 32
                assert pos[0] <= nc.sbuf_usable_end, (name, pos[0])
                return t
            put.pos = pos
            return put

        put = layer(z_at)
        act_hi = put("act_hi", 128, FH, NT, dt=f32r)
        act_lo = put("act_lo", 128, FH, NT, dt=f32r)
        ub = [put(f"ub{s}", 128, NT + 2) for s in range(2)]
        yb = [put(f"yb{s}", 128, NT) for s in range(2)]
        sg = put("sg", 128, NT)
        af = put("af", 128, NT)
        put = layer(z_at)
        mw = [put(f"mw{s}", 128, KT, 512) for s in range(3)]
        mrow = [put(f"mrow{s}", NC9, 512) for s in range(2)]
        put = layer(h_at)
        xs = put("xs", 128, 4, D)
        PR = put("PR", 128, PT_TILES, 128)
        line = put("line", 33, 1024)
        lrow = place("lrow", (16, 1024), f32, n_end - 4160)[0]
        put = layer(z_at)
        kT = put("kT", 128, 4, NT)
        kvt = put("kvt", 128, 4, 1536)
        kvs = put("kvs", NS, 1536)
        cb = put("cb", 128, 4, 16, 16)
        sc = put("sc", 128, 4, 16, 16)
        gat = put("gat", 128, 4, 48)
        gts = put("gts", 128, 48)
        gr = put("gr", 128, 3)
        kcT = put("kcT", 128, 2, 80)
        vcp = put("vcp", 16, 256)
        vcs = put("vcs", 64, 256)
        w2b = put("w2b", 128, 2, 128)
        a_at = put.pos[0]
        w1b = put("w1b", 128, 32, 128)
        put = layer(a_at)
        Hb = [put(f"Hb{s}", 128, 512) for s in range(4)]
        qT = [put(f"qT{s}", 128, NT) for s in range(2)]
        qs = put("qs", 128, KT, NS)
        wg_hi = put("wg_hi", 128, KT, 48, dt=f32r)
        wg_lo = put("wg_lo", 128, KT, 48, dt=f32r)
        mx = put("mx", 128, 4)
        nm = put("nm", 128, 4)
        den = put("den", 128, 8)
        cf = put("cf", 128, 4)
        put = layer(n_at)
        Ss = [put(f"Ss{s}", 128, 512) for s in range(2)]
        Pb = [put(f"Pb{s}", 128, 512) for s in range(4)]
        PTb = [put(f"PTb{s}", 128, 512) for s in range(2)]
        assert put.pos[0] <= n_end
        put = layer(n_at + NT * 4)
        hx = put("hx", 128, 2, 80)
        hy = put("hy", 128, 2, 80)
        hz = put("hz", 128, 2, 80)
        per_ = put("per_", 32, 128)
        put = layer(h_at)
        RT = put("RT", 128, 2, 2592)
        pgc = [put(f"pgc{s}", 128, 2, 256) for s in range(2)]
        assert put.pos[0] <= h_at + 2 * KT * NT * 4
        okv = place("okv", (128, KT, NT), f32, o_at)[0]
        wg_raw = place("wg_raw", (128, KT, 48), f32, n_at + 3 * NT * 4)[0]
        line2 = place("line2", (33, 1024), f32, n_end - 4160)[0]
        Oacc = place("Oacc", (128, 4, D), f32, o_at)[0]
        put = layer(a_at)
        vblk = put("vblk", 128, 2, 512)
        cm = put("cm", 128, 64)
        cd = put("cd", 128, 64)
        put = layer(n_at)
        pcT = [put(f"pcT{s}", 128, 128) for s in range(2)]
        put = layer(z_at + 16512)
        ld = [put(f"ld{s}", 128, 4, 256) for s in range(2)]
        put = layer(n_at + 1216)
        ksT = put("ksT", 128, 2, 512)
        bias_s = put("bias_s", 128, 328)
        ST = put("ST", 128, 4, 128)
        STn = put("STn", 64, 3, 128)
        Sa = put("Sa", 128, 592)
        assert put.pos[0] <= n_end, (put.pos[0], n_end)
        qb = place("qb", (128, KT), f32, z_at + 8320)[0]
        put = layer(z_at + 8320 + 64)
        pT = put("pT", 128, 4, 128)
        pTn = put("pTn", 64, 3, 128)
        pb = put("pb", 128, 4, 16)
        oS = put("oS", 128, KT, NS)
        oS2 = put("oS2", 128, KT, NS)
        smx = put("smx", 128, 4)
        sden = put("sden", 128, 4)
        scof = put("scf_", 128, 4)
        put = layer(z_at)
        yt = [put(f"yt{s}", 128, D) for s in range(2)]
        yts = put("yts", NS, D)

        pu = [ctx.enter_context(nc.psum_tensor(f"pu{s}", [128, 1024], f32)) for s in range(2)]
        pn = ctx.enter_context(nc.psum_tensor("pn", [128, 1024], f32))
        pm = [ctx.enter_context(nc.psum_tensor(f"pm{s}", [128, 512], f32))[:, :] for s in range(2)]
        prod = [p[:, PSO:PSO + NT] for p in pu]
        pnb = [pn[:, 0:512], pn[:, 512:1024]]

        lines_d = nc.dram_tensor("lines_d", [16, 1024], f32).ap()
        gates_d = nc.dram_tensor("gates_d", [8, 48], f32).ap()

        sems = {}

        def sem(name):
            if name not in sems:
                sems[name] = ctx.enter_context(nc.semaphore(name))
            return sems[name]

        def PTv(row, n):
            return PT[:, row:row + n]

        def site(k):
            b0 = 24 * k
            return modT[:, b0:b0 + 8, :], modT[:, b0 + 8:b0 + 16, :], modT[:, b0 + 16:b0 + 24, :] if k < 4 else None


        def turns(e, count, body, first=False):
            if first:
                body(0, True)
            with e.Fori(1 if first else 0, count) as i:
                body(i, False)

        def hold(e, semaphore, value):
            e.wait_ge(semaphore, value)
            e.sem_inc(S["passed"], 1)

        class Chain:

            def __init__(self, e, s):
                self.e, self.s, self.n, self.off = e, s, 0, 0

            def mark(self, ins):
                ins.then_inc(self.s, 1)
                self.n += 1

            def settle(self):
                self.e.wait_ge(self.s, self.off + self.n)

            def link(self, ins):
                self.mark(ins)
                self.settle()

            def turns(self, count, per, body, first=False):
                if first:
                    body(0, True)
                start = 1 if first else 0
                k0 = self.n
                with self.e.Fori(start, count) as i:
                    self.n, self.off = 0, k0 + (i - start) * per
                    body(i, False)
                    assert self.n == per, (self.n, per)
                self.off, self.n = 0, k0 + (count - start) * per

        names = """passed consts_in tables_in x_in tr_done tr_taken_a tr_taken_v ones_set tab_set prep_done
            lines_out mod_landed0 mod_landed1 mod_landed2 mod_done mod_row mod_t mod_t_taken mod_set
            w_landed0 w_landed1 w_hi_ready w_lo_ready unit_done out_taken
            sq_ready sq_added norm_done rs_ready rstd_ready
            t_ready hf_ready hhi_ready hlo_ready x_updated dve_seq pool_seq act_seq
            mix_in_sb z_made mixed mix_hi mix_lo z10_kept ub_zero
            up_in_sb conv_done silu_done af_ready act_hi_done act_lo_done up10_kept
            o_in_sb half_added s_tr s_taken s_out
            kv_in_sb kv_tr kv_tok kv_out mod_coef lrow_set pe_in cmpw_in pages_in0 pages_in1
            w1_zero page_tr page_rows rt_rest hid_done hid_act hid_lin hid_tanh cmp_done cmp_kept pe_tr line_in
            cb_done cb_kept gate_w_in wg_hi_s wg_lo_s g_done g_kept g_sent g_back g_rt
            H_in0 H_in1 H_in2 H_in3 head_used q_in_sb q_kept sc_done sc_kept
            S_done S_biased nm_ready P_ready PT_done PT_kept_a PT_kept_v O_done O_kept
            c_max c_exp c_prob c_tr c_trk vrep_done v_blk c_out c_added
            sk_in0 sk_in1 sk_tr sk_sb qb_set s_sc s_sck sn_done sn_kept sS_tr sS_bias s_exp s_p sP_tr sP_kept
            sv_in0 sv_in1 pb_set sv_done sv_kept sv_all oS_done oT_tr oT_kept oh_ready olo_ready
            y_tr y_kept y_out0 y_out1 ys_out win_out kvp_out""".split()
        S = {n: sem(n) for n in names}

        w_mod = A["mod_w"].rearrange("l s (k p) n -> (l s) p k n", p=128)
        w_kvm = A["kv_mod_w"].rearrange("(k p) n -> p k n", p=128)
        w_ain = A["a_w_in"][0].rearrange("(k p) n -> p k n", p=128)
        w_aout = A["a_w_out"][0].rearrange("(k p) n -> p k n", p=128)
        w_up = A["ffn_w_up"].rearrange("l (k p) n -> l p k n", p=128)
        w_down = A["ffn_w_down"].rearrange("l (h k p) n -> (l h) p k n", p=128, h=2)
        w_kv = A["w_kv"].rearrange("(k p) n -> p k n", p=128)
        w_qg = A["b_w_qg"][0].rearrange("(k p) n -> p k n", p=128)
        w_bout = A["b_w_out"][0].rearrange("(g f p d) n -> f d g p n", g=2, f=2, p=4)

        block = ctx.enter_context(nc.Block())

        def w_wait(e, phase, i, s):
            e.wait_ge(S[f"w_landed{s}"], W0[phase] + WI[phase] * (i + 1))

        WI = {n: {"q": 32, "attn_out": 64}.get(n, 16) for n, _ in UNITS}
        W0, c0 = {}, 0
        for n, c in UNITS:
            W0[n] = c0
            c0 += WI[n] * (c // 2)
        NEXT = {n: m for (n, _), (m, _) in zip(UNITS, UNITS[1:]) if m not in ("q", "attn_out")}
        KOF = {n: FH if n.startswith("down") else KT for n, _ in UNITS}
        valid = [128, 88, 88, 128, 128, 8] + [128] * 12 + [72, 64]

        @block.sync
        def _(sp):
            for t, n in ((ident, "c_ident"), (srow, "c_srow"), (smask, "c_smask"), (rep, "c_rep"), (blk, "c_blk"),
                         (line, "c_line")):
                sp.dma_start(t[:, :], A[n]).then_inc(S["consts_in"], 16)
            sp.dma_start(tab[0:32, :], A["rel_bias"]).then_inc(S["consts_in"], 16)
            sp.dma_start(pti[:, :], A["page_table"].rearrange("a b -> (a b)").unsqueeze(0)).then_inc(S["consts_in"], 16)
            n_tab = 0
            for row, src in ((R_MODB, A["mod_b"].rearrange("l s (t c) -> (l s t) c", c=128)),
                             (96, A["kv_mod_b"].rearrange("(t c) -> t c", c=128)),
                             (R_KVG, A["kv_norm_g"].rearrange("(t c) -> t c", c=128)),
                             (R_ACB, A["a_conv_b"].rearrange("l (t c) -> (l t) c", c=128)),
                             (R_NG, A["norm_g"].rearrange("l s (t c) -> (l s t) c", c=128)),
                             (R_ACW, A["a_conv_w"].rearrange("l j (t c) -> (l j t) c", c=128)),
                             (R_FCB, A["ffn_conv_b"].rearrange("l (t c) -> (l t) c", c=128)),
                             (R_FCW, A["ffn_conv_w"].rearrange("l j (t c) -> (l j t) c", c=128)),
                             (R_STA, A["state_conv_a"].rearrange("l b j (t c) -> (l b j t) c", c=128)),
                             (R_STF, A["state_ffn_conv"].rearrange("l b j (t c) -> (l b j t) c", c=128)),
                             (R_C, A["c_prompt"].rearrange("b (t c) -> (b t) c", c=128)),
                             (R_C + 8, A["c_sample"].rearrange("b (t c) -> (b t) c", c=128)),
                             (R_XS, A["x_sample"].rearrange("b s (t c) -> (b s t) c", c=128))):
                n, k = src.shape[0], 0
                while k < n:
                    t, p = divmod(row + k, 128)
                    full = (n - k) // 128 if p == 0 else 0
                    if full:
                        sp.dma_start(PR[:, t:t + full, :], src[k:k + 128 * full, :].rearrange("(t p) c -> p t c", p=128))\
                          .then_inc(S["tables_in"], 16)
                        k += 128 * full
                    else:
                        m = min(128 - p, n - k)
                        sp.dma_start(PR[p:p + m, t, :], src[k:k + m, :]).then_inc(S["tables_in"], 16)
                        k += m
                    n_tab += 1
            assert n_tab == N_TABLES, n_tab
            sp.dma_start(xs[:, :, :], A["x_prompt"][0].rearrange("(i p) n -> p i n", p=128)).then_inc(S["x_in"], 16)

            def set_chunks(s, first):
                for c in range(6):
                    if not (first and c < 3):
                        hold(sp, S["mod_done"], 6 * s + c - 2)
                    src = w_mod[bass.ds(s, 1), :, :, 512 * c:512 * c + 512].rearrange("o p k n -> (o p) k n")
                    sp.dma_start(mw[c % 3][:, :, :], src).then_inc(S[f"mod_landed{c % 3}"], 16)
            turns(sp, 4, set_chunks, first=True)
            for c in range(4):
                hold(sp, S["mod_done"], 24 + c - 2)
                sp.dma_start(mw[c % 3][:, :, :], w_kvm[:, :, 512 * c:512 * c + 512]).then_inc(S[f"mod_landed{c % 3}"], 16)

            def weights(phase, i, s, src, first=False):
                if not first:
                    hold(sp, S["w_lo_ready"], UBASE[phase] + 2 * i + s - 1)
                k = KOF[phase]
                sp.dma_start(w_raw[s][:, 0:k, :], src).then_inc(S[f"w_landed{s}"], 16)

            def mix_in_w(i, first):
                for u in range(6):
                    part = (1, 2, 0)[u % 3]
                    col = part * D + (2 * i + u // 3) * 128
                    if not (first and u < 2):
                        hold(sp, S["w_lo_ready"], 6 * i + u - 1)
                    sp.dma_start(w_raw[u % 2][:, 0:KT, :], w_ain[:, :, bass.ds(col, 128)]).then_inc(S[f"w_landed{u % 2}"], 16)
            turns(sp, 4, mix_in_w, first=True)

            def out_w(phase, view):
                def body(i, first):
                    for s in range(2):
                        weights(phase, i, s, view[:, :, bass.ds(256 * i + 128 * s, 128)])
                turns(sp, 4, body)

            def up_w(phase, l, hh):
                def body(i, first):
                    for s in range(2):
                        weights(phase, i, s, w_up[l, :, :, bass.ds((hh * FH + i) * 128 + s * FF, 128)])
                turns(sp, FH, body)

            def ffn_w(l):
                for hh in range(2):
                    up_w(f"up{l}{hh}", l, hh)
                    out_w(f"down{l}{hh}", w_down[2 * l + hh])

            out_w("mix_out", w_aout)
            ffn_w(0)
            for c, slot in enumerate(KV_SLOTS):
                for s in range(2):
                    weights("kv", c, s, w_kv[:, :, 256 * slot + 128 * s:256 * slot + 128 * s + 128])

            for c in range(2):
                if c == 0:
                    sp.wait_ge(S["w1_zero"], 1)
                    hold(sp, S["unit_done"], UBASE["q"])
                else:
                    sp.wait_ge(S["hid_done"], 1)
                    sp.wait_ge(S["cmp_done"], 1)
                for f in range(2):
                    sp.dma_start(w1b[64 * f:64 * f + 64, :, 64 * f:64 * f + 64],
                                 A["cmp_w1"][c].rearrange("(r d) n -> d r n", d=64)).then_inc(S["cmpw_in"], 16)
                    sp.dma_start(w2b[64 * f:64 * f + 64, c, 64 * f:64 * f + 64], A["cmp_w2"][c]).then_inc(S["cmpw_in"], 16)
                    sp.dma_start(per_[:, 64 * f:64 * f + 64], A["cmp_pe"][c]).then_inc(S["pe_in"], 16)

                def cached(i, first):
                    for s in range(2):
                        if not (first and c == 0):
                            hold(sp, S["page_tr"], 8 * c + 2 * i + s - 1)
                        for g in range(2):
                            v = sp.value_load(pti[0:1, bass.ds(4 * i + 2 * s + g, 1)], min_val=0, max_val=19)
                            src = A["cache_kv"][bass.ds(v, 1), :, c].rearrange("o p g d -> (o p) (g d)")
                            sp.dma_start(pgc[s][:, g, :], src).then_inc(S[f"pages_in{s}"], 16)
                turns(sp, 4, cached, first=True)
            sp.wait_ge(S["pe_tr"], 2)
            sp.wait_ge(S["hid_done"], 2)
            sp.dma_start(line2[:, :], A["c_line"]).then_inc(S["line_in"], 16)
            sp.dma_start(wg_raw[:, :, :], w_qg[:, :, 1024:1072]).then_inc(S["gate_w_in"], 16)

            sp.wait_ge(S["lines_out"], 16)
            for gp in range(2):
                def heads(it, first):
                    for u in range(2):
                        hold(sp, S["w_lo_ready"], UBASE["q"] + 4 * gp + 2 * it + u - 1)
                        for f in range(2):
                            col = (8 * gp + 4 * f + 2 * it + u) * 64
                            sp.dma_start(w_raw[u][:, 0:KT, 64 * f:64 * f + 64], w_qg[:, :, bass.ds(col, 64)])\
                              .then_inc(S[f"w_landed{u}"], 16)
                    for u in range(2):
                        for f in range(2):
                            k = 2 * u + f
                            if not (gp == 0 and first):
                                hold(sp, S["head_used"], 8 * gp + 4 * it + k - 3)
                            row = 8 * gp + 4 * f + 2 * it + u
                            src = bass.AP(lines_d.tensor, row * 1024 + 385, [[1, 128], [1, 512]])
                            sp.dma_start(Hb[k][:, :], src).then_inc(S[f"H_in{k}"], 16)
                turns(sp, 2, heads, first=(gp == 0))

            for part, done in (("k", "sk_tr"), ("v", "sv_done")):
                kv = 0 if part == "k" else 1
                if part == "k":
                    sp.wait_ge(S["c_added"], 8)
                    sp.wait_ge(S["kvp_out"], 16 * 4)
                else:
                    sp.wait_ge(S["sk_tr"], 8)

                def cached_rows(i, first):
                    for s in range(2):
                        if not first:
                            hold(sp, S[done], 2 * i + s - 1)
                        for g in range(2):
                            v = sp.value_load(pti[0:1, bass.ds(4 * i + 2 * s + g, 1)], min_val=0, max_val=19)
                            src = A["cache_kv"][bass.ds(v, 1), :, 2 + kv].rearrange("o p g d -> (o p) (g d)")
                            sp.dma_start(ld[s][:, g, :], src).then_inc(S[f"s{part}_in{s}"], 16)
                        src = A["cache_win"][bass.ds(2 * i + s, 1), :, kv].rearrange("o (g p) h d -> (o p) g (h d)", p=128)
                        sp.dma_start(ld[s][:, 2:4, :], src).then_inc(S[f"s{part}_in{s}"], 16)
                turns(sp, 4, cached_rows, first=True)

            def bout(i, first):
                for s in range(2):
                    hold(sp, S["w_lo_ready"], UBASE["attn_out"] + 2 * i + s - 1)
                    for f in range(2):
                        for g in range(2):
                            sp.dma_start(w_raw[s][64 * f:64 * f + 64, 4 * g:4 * g + 4, :],
                                         w_bout[f][:, g, :, bass.ds(256 * i + 128 * s, 128)]).then_inc(S[f"w_landed{s}"], 16)
            turns(sp, 4, bout)
            ffn_w(1)

            for i in range(4):
                hold(sp, S["y_kept"], 2 * i + 2)
                sp.dma_start(O["y_prompt"][0, 128 * i:128 * i + 128, :], yt[i % 2][:, :]).then_inc(S[f"y_out{i % 2}"], 16)
            sp.wait_ge(S["y_kept"], 10)
            sp.dma_start(O["y_sample"].rearrange("b s n -> (b s) n"), yts[:, :]).then_inc(S["ys_out"], 16)
            sp.wait_ge(S["y_out0"], 32)
            sp.wait_ge(S["y_out1"], 32)
            sp.wait_ge(S["ys_out"], 16)

        @block.tensor
        def _(pe):
            mm = nc.tensor.matmul
            banks = [pnb[0], pnb[1], pm[0], pm[1]]
            group = [0]

            def tr_group(tiles):
                t = group[0]
                if t >= 4:
                    pe.wait_ge(S["tr_taken_a" if t % 2 == 0 else "tr_taken_v"], (t - 4) // 2 + 1)
                col = 0
                for src in tiles:
                    k, n = src.shape[0], src.free_size()
                    last = nc.tensor.transpose(banks[t % 4][0:n, col:col + k], src, ident[0:k, 0:k])
                    col += k
                last.then_inc(S["tr_done"], 1)
                group[0] += 1

            pe.wait_ge(S["consts_in"], 16 * 8)
            pe.wait_ge(S["tables_in"], 16 * N_TABLES)
            for g in range(5):
                tr_group([PR[0:valid[t], t, :] for t in range(4 * g, 4 * g + 4)])
            pe.wait_ge(S["x_in"], 16)
            for i in range(4):
                for kk in range(2):
                    tr_group([xs[:, i, 128 * k:128 * k + 128] for k in range(4 * kk, 4 * kk + 4)])
            pe.wait_ge(S["tab_set"], 1)
            for c in range(2):
                t = group[0]
                pe.wait_ge(S["tr_taken_a" if t % 2 == 0 else "tr_taken_v"], (t - 4) // 2 + 1)
                mm(banks[t % 4][0:16, :], tab[:, :], line[:, 512 * c:512 * c + 512], start=True, stop=True)\
                    .then_inc(S["tr_done"], 1)
                group[0] += 1

            def norm_sum(m):
                pe.wait_ge(S["sq_added"], 8 * (m + 1))
                if m == 0:
                    pe.wait_ge(S["ones_set"], 1)
                for hh in range(2):
                    last = mm(pn[:, PSO + HALF * hh:PSO + HALF * (hh + 1)], ones[:, :], sq[:, HALF * hh:HALF * (hh + 1)],
                              start=True, stop=True)
                last.then_inc(S["norm_done"], 1)

            pe.wait_ge(S["prep_done"], 1)
            pe.wait_ge(S["tr_taken_a"], 8)
            pe.wait_ge(S["tr_taken_v"], 7)

            def mod_product(q, c, use):
                if c is not None:
                    pe.wait_ge(S[f"mod_landed{c % 3}"], 16 * (use + 1))
                pe.wait_ge(S["mod_row"], q - 1)
                for k in range(KT):
                    last = mm(pm[c % 2][0:NC9, :], PT[:, R_C + k:R_C + 72:8], mw[c % 3][:, k, :],
                              start=(k == 0), stop=(k == KT - 1))
                last.then_inc(S["mod_done"], 1)

            def mod_transpose(q, c, early=False):
                hold(pe, S["mod_row"], q + 1)
                if not early:
                    hold(pe, S["mod_t_taken"], q - 1)
                for t in range(4):
                    last = nc.tensor.transpose(pnb[c % 2][:, NC9 * t:NC9 * t + NC9], mrow[c % 2][:, 128 * t:128 * t + 128],
                                               ident[0:NC9, 0:NC9])
                last.then_inc(S["mod_t"], 1)

            def mod_set(s, first):
                for c in range(6):
                    if first and c < 2:
                        pe.wait_ge(S[f"mod_landed{c}"], 16)
                        for k in range(KT):
                            last = mm(pm[c][0:NC9, :], PT[:, R_C + k:R_C + 72:8], mw[c][:, k, :],
                                      start=(k == 0), stop=(k == KT - 1))
                        last.then_inc(S["mod_done"], 1)
                    else:
                        mod_product(6 * s + c, c, 2 * s + c // 3)
                    mod_transpose(6 * s + c, c, early=(first and c < 2))
            turns(pe, 4, mod_set, first=True)
            for c in range(4):
                mod_product(24 + c, c, 8 + c // 3)
                mod_transpose(24 + c, c)
            pe.wait_ge(S["mod_t_taken"], MOD_CHUNKS)

            def unit(phase, i, s, hi, lo, slot=None, waits=()):
                n = UBASE[phase] + 2 * i + s
                pe.wait_ge(S["w_lo_ready"], n + 1)
                if slot is None:
                    slot = s
                    if not (isinstance(n, int) and n < 2):
                        pe.wait_ge(S["out_taken"], n - 1)
                else:
                    pe.wait_ge(S["out_taken"], n)
                kk = KOF[phase]
                for k in range(kk):
                    for name, value in waits:
                        pe.wait_ge(S[name], value + k)
                    for w, hs in ((w_hi[s], (hi, lo)), (w_lo[s], (hi,))):
                        for h in hs:
                            for c in range(2):
                                last = mm(pu[slot][:, PSO + HALF * c:PSO + HALF * (c + 1)], w[:, k, :],
                                          h[:, k, HALF * c:HALF * (c + 1)],
                                          start=(k == 0 and w is w_hi[s] and h is hi),
                                          stop=(k == kk - 1 and w is w_lo[s]))
                last.then_inc(S["unit_done"], 1)

            def phase(name, hi, lo, per=2, waits=()):
                def body(i, first):
                    for u in range(per):
                        unit(name, (per // 2) * i + u // 2, u % 2, hi, lo, waits=waits if first and u == 0 else ())
                turns(pe, dict(UNITS)[name] // per, body, first=True)

            def ffn(l, q):
                for hh in range(2):
                    phase(f"up{l}{hh}", h_hi, h_lo, waits=[("hlo_ready", 9 * q + 2)] if hh == 0 else ())
                    phase(f"down{l}{hh}", act_hi, act_lo, waits=[("act_lo_done", FH * (2 * l + hh) + 1)])

            def kept_rows(p):
                pe.wait_ge(S["up10_kept"], 44 * (p + 1))
                for k in range(5):
                    bank = pm[0] if k < 4 else pm[1]
                    last = nc.tensor.transpose(bank[0:88, 128 * (k % 4):128 * (k % 4) + 128],
                                               up10[:, 2 * k:2 * k + 2, :].rearrange("p a b -> p (a b)"), ident[:, :])
                last.then_inc(S["s_tr"], 1)

            norm_sum(0)
            phase("mix_in", h_hi, h_lo, per=6, waits=[("hlo_ready", 2)])
            phase("mix_out", act_hi, act_lo, waits=[("mix_lo", 1)])
            pe.wait_ge(S["z10_kept"], KT)
            nc.tensor.transpose(pm[0][0:80, 0:128], z10[:, :, :].rearrange("p a b -> p (a b)"), ident[:, :])\
                .then_inc(S["s_tr"], 1)
            norm_sum(1)
            norm_sum(2)
            ffn(0, 1)
            norm_sum(3)
            pe.wait_ge(S["s_taken"], 1)
            kept_rows(0)
            norm_sum(4)
            phase("kv", h_hi, h_lo, waits=[("hlo_ready", 9 * 2 + 2)])

            pe.wait_ge(S["out_taken"], UBASE["q"])
            pe.wait_ge(S["s_taken"], 2)
            tiles = [okv[:, m, :] for m in range(8)] + [kT[:, m, :] for m in range(4)]
            ordered = [tiles[2 * KV_SLOTS.index(sl) + g] for sl in range(6) for g in range(2)]
            for s3 in range(3):
                for i in range(4):
                    tr_group([ordered[4 * s3 + k][:, 128 * i:128 * i + 128] for k in range(4)])
            for s3 in range(3):
                t = group[0]
                pe.wait_ge(S["tr_taken_a" if t % 2 == 0 else "tr_taken_v"], (t - 4) // 2 + 1)
                for k in range(4):
                    last = nc.tensor.transpose(banks[t % 4][0:NS, 128 * k:128 * k + 128], ordered[4 * s3 + k][:, NP:NT],
                                               ident[:, :])
                last.then_inc(S["tr_done"], 1)
                group[0] += 1
            pe.wait_ge(S["tr_taken_a"], 15)
            pe.wait_ge(S["tr_taken_v"], 15)

            for c in range(2):
                def page(i, first):
                    for s in range(2):
                        n = 8 * c + 2 * i + s
                        pe.wait_ge(S[f"pages_in{s}"], 128 * c + 32 * (i + 1))
                        if not (c == 0 and first):
                            pe.wait_ge(S["page_rows"], n - 1)
                        for gp in range(2):
                            for g in range(2):
                                last = nc.tensor.transpose(pm[s][:, 256 * gp + 128 * g:256 * gp + 128 * g + 128],
                                                           pgc[s][:, g, 128 * gp:128 * gp + 128], ident[:, :])
                        last.then_inc(S["page_tr"], 1)
                turns(pe, 4, page, first=(c == 0))
                pe.wait_ge(S["pe_in"], 32 * (c + 1))
                if c == 1:
                    pe.wait_ge(S["cmp_kept"], 1)
                nc.tensor.transpose(pnb[1][:, 0:32], per_[:, :], ident[0:32, 0:32]).then_inc(S["pe_tr"], 1)
                pe.wait_ge(S["cmpw_in"], 64 * (c + 1))
                pe.wait_ge(S["rt_rest"], 3 * (c + 1))
                pe.wait_ge(S["page_rows"], 8 * (c + 1))
                for r in range(32):
                    last = mm(pn[:, 0:162], w1b[:, r, :], RT[:, :, r:2592:32], start=(r == 0), stop=(r == 31))
                last.then_inc(S["hid_done"], 1)
                pe.wait_ge(S["hid_act"], c + 1)
                if c == 0:
                    mm(pnb[1][:, 0:160], w2b[:, 0, :], hx[:, :, :], start=True, stop=True).then_inc(S["cmp_done"], 1)
                else:
                    for gp in range(2):
                        mm(pnb[1][0:16, 128 * gp:128 * gp + 128], hx[:, gp, 0:16], w2b[:, 1, :], start=True, stop=True)
                        last = mm(pnb[0][0:64, 128 * gp:128 * gp + 128], hx[:, gp, 16:80], w2b[:, 1, :], start=True, stop=True)
                    last.then_inc(S["cmp_done"], 1)
            pe.wait_ge(S["cmp_kept"], 2)

            pe.wait_ge(S["line_in"], 16)
            for i in range(4):
                for n in range(16):
                    x0 = 128 * i - 32 * n + 481
                    last = mm(pn[:, 256 * i + 16 * n:256 * i + 16 * n + 16], line2[:, x0:x0 + 128], tabp[:, :],
                              start=True, stop=True)
            last.then_inc(S["cb_done"], 1)

            pe.wait_ge(S["hlo_ready"], 9 * 4)
            pe.wait_ge(S["wg_lo_s"], 1)
            for t, c0 in enumerate((0, 128, 256, 384, NT - 128)):
                for k in range(KT):
                    for h, w in ((h_hi, wg_hi), (h_hi, wg_lo), (h_lo, wg_hi)):
                        last = mm(pm[0][:, 48 * t:48 * t + 48], h[:, k, c0:c0 + 128], w[:, k, :],
                                  start=(k == 0 and h is h_hi and w is wg_hi), stop=(k == KT - 1 and h is h_lo))
            last.then_inc(S["g_done"], 1)
            pe.wait_ge(S["g_kept"], 1)
            pe.wait_ge(S["cb_kept"], 1)

            for gp in range(2):
                def heads(it, first):
                    T = 2 * gp + it
                    for u in range(2):
                        unit("q", T, u, h_hi, h_lo, slot=0)

                    def scores(step):
                        u, item = S_ITEMS[step]
                        nS = NSI * T + step
                        if item is None or S_ITEMS[step - 1][1] is None:
                            pe.wait_ge(S["q_in_sb"], 2 * T + u + 1)
                        if not (gp == 0 and first and step < 2):
                            pe.wait_ge(S["S_biased"], nS - 1)
                        if item is None:
                            f = step % 2
                            for i in range(4):
                                last = mm(pnb[f][:, 16 * i:16 * i + 16], qT[u][64 * f:64 * f + 64, 128 * i:128 * i + 128],
                                          kcT[64 * f:64 * f + 64, gp, 0:16], start=True, stop=True)
                        else:
                            _, f, br, i = item
                            W = 128 * (i + 1)
                            last = mm(pnb[step % 2][:, 0:W], qT[u][64 * f:64 * f + 64, 128 * i:128 * i + 128],
                                      kT[64 * f:64 * f + 64, 2 * br + gp, 0:W], start=True, stop=True)
                        last.then_inc(S["S_done"], 1)

                    def flip(step):
                        _, item = S_ITEMS[step]
                        m, f, br, i = item
                        pe.wait_ge(S["P_ready"], 32 * T + m + 1)
                        if not (gp == 0 and first and m < 2):
                            pe.wait_ge(S["PT_kept_a" if m % 2 == 0 else "PT_kept_v"], 16 * T + m // 2)
                        for j in range(i + 1):
                            last = nc.tensor.transpose(pm[m % 2][:, 128 * j:128 * j + 128],
                                                       Pb[m % 4][:, 128 * j:128 * j + 128], ident[:, :])
                        last.then_inc(S["PT_done"], 1)

                    def weigh(step):
                        _, item = S_ITEMS[step]
                        m, f, br, i = item
                        pe.wait_ge(S["PT_kept_a" if m % 2 == 0 else "PT_kept_v"], 16 * T + m // 2 + 1)
                        if not (gp == 0 and first and m < 2):
                            pe.wait_ge(S["O_kept"], 32 * T + m - 1)
                        col = (3 if br == 0 else 5) * 256 + (2 * gp + f) * 64
                        for j in range(i + 1):
                            last = mm(pu[1][:, 512 * (m % 2):512 * (m % 2) + 64], PTb[m % 2][:, 128 * j:128 * j + 128],
                                      kvt[:, j, col:col + 64], start=(j == 0), stop=(j == i))
                        last.then_inc(S["O_done"], 1)

                    for step in range(len(S_ITEMS) + 3):
                        if step < len(S_ITEMS):
                            scores(step)
                        if 0 <= step - 2 < len(S_ITEMS) and S_ITEMS[step - 2][1] is not None:
                            flip(step - 2)
                        if 0 <= step - 3 < len(S_ITEMS) and S_ITEMS[step - 3][1] is not None:
                            weigh(step - 3)
                turns(pe, 2, heads, first=(gp == 0))
            pe.wait_ge(S["O_kept"], 128)
            pe.wait_ge(S["PT_kept_a"], 64)
            pe.wait_ge(S["PT_kept_v"], 64)

            for gp in range(2):
                mm(pm[gp][:, 0:128], rep[:, :], vcp[:, 128 * gp:128 * gp + 128], start=True, stop=True)\
                    .then_inc(S["vrep_done"], 1)
            pe.wait_ge(S["c_prob"], 1)
            pe.wait_ge(S["v_blk"], 2)
            for n in range(9):
                if n < 8:
                    i, gp = divmod(n, 2)
                    if n >= 2:
                        pe.wait_ge(S["c_trk"], n - 1)
                    nc.tensor.transpose(pm[n % 2][:, 0:128], sc[:, i, 8 * gp:8 * gp + 8, :].rearrange("p e n -> p (e n)"),
                                        ident[:, :]).then_inc(S["c_tr"], 1)
                if n >= 1:
                    k = n - 1
                    pe.wait_ge(S["c_trk"], k + 1)
                    if k >= 2:
                        pe.wait_ge(S["c_added"], k - 1)
                    mm(pnb[k % 2][:, :], pcT[k % 2][:, :], vblk[:, k % 2, :], start=True, stop=True)\
                        .then_inc(S["c_out"], 1)

            def sample_keys(i, first):
                for s in range(2):
                    b = 2 * i + s
                    pe.wait_ge(S[f"sk_in{s}"], 48 * (i + 1))
                    if not (first and s == 0):
                        pe.wait_ge(S["sk_sb"], 2 * b)
                    for gp in range(2):
                        for j in range(4):
                            last = nc.tensor.transpose(pm[gp][:, 128 * j:128 * j + 128],
                                                       ld[s][:, j, 128 * gp:128 * gp + 128], ident[:, :])
                    last.then_inc(S["sk_tr"], 1)
                    pe.wait_ge(S["sk_sb"], 2 * b + 2)
                    pe.wait_ge(S["qb_set"], b + 1)
                    if not (first and s == 0):
                        pe.wait_ge(S["s_sck"], b)
                    for g in range(4):
                        gp, f = divmod(g, 2)
                        for j in range(4):
                            last = mm(pnb[f][:, 8 * j + 4 * gp:8 * j + 4 * gp + 4],
                                      ksT[64 * f:64 * f + 64, gp, 128 * j:128 * j + 128],
                                      qb[64 * f:64 * f + 64, 4 * gp:4 * gp + 4], start=True, stop=True)
                    last.then_inc(S["s_sc"], 1)
            pe.wait_ge(S["c_added"], 8)
            pe.wait_ge(S["c_trk"], 8)
            turns(pe, 4, sample_keys, first=True)
            pe.wait_ge(S["s_sck"], 8)
            pe.wait_ge(S["sk_sb"], 16)
            for g in range(4):
                gp, f = divmod(g, 2)
                rhs = qs[64 * f:64 * f + 64, 4 * gp:4 * gp + 4, :]
                bank = (pm[0], pnb[1])[f]
                for br in range(2):
                    mm(bank[0:8, 64 * br + 32 * gp:64 * br + 32 * gp + 32], kT[64 * f:64 * f + 64, 2 * br + gp, NP:NT], rhs,
                       start=True, stop=True)
                last = mm(bank[0:64, 128 + 32 * gp:128 + 32 * gp + 32], kcT[64 * f:64 * f + 64, gp, 16:80], rhs,
                          start=True, stop=True)
            mm(pnb[0][:, 0:328], tabr[:, :], srow[:, :], start=True, stop=True).then_inc(S["sn_done"], 1)
            pe.wait_ge(S["sn_kept"], 3)
            for j in range(4):
                nc.tensor.transpose(pm[1][:, 128 * j:128 * j + 128], ST[:, j, :], ident[:, :])
            for br in range(2):
                nc.tensor.transpose(pnb[1][:, 8 * br:8 * br + 8], STn[0:8, br, :], ident[0:8, 0:8])
            nc.tensor.transpose(pnb[1][:, 16:80], STn[0:64, 2, :], ident[0:64, 0:64]).then_inc(S["sS_tr"], 1)
            pe.wait_ge(S["s_p"], 1)
            for j, c0 in enumerate((0, 128, 264, 392)):
                nc.tensor.transpose(pm[0][:, 128 * j:128 * j + 128], Sa[:, c0:c0 + 128], ident[:, :])
            for j, c0 in enumerate((256, 520)):
                nc.tensor.transpose(pm[1][0:8, 128 * j:128 * j + 128], Sa[:, c0:c0 + 8], ident[:, :])
            nc.tensor.transpose(pm[1][0:64, 256:384], Sa[:, 528:592], ident[:, :]).then_inc(S["sP_tr"], 1)
            pe.wait_ge(S["sP_kept"], 3)

            def sample_values(i, first):
                for s in range(2):
                    b = 2 * i + s
                    pe.wait_ge(S[f"sv_in{s}"], 48 * (i + 1))
                    pe.wait_ge(S["pb_set"], b + 1)
                    if not (first and s == 0):
                        pe.wait_ge(S["sv_kept"], b)
                    for g in range(4):
                        gp, f = divmod(g, 2)
                        for j in range(4):
                            last = mm(pnb[0][64 * f:64 * f + 64, 4 * gp:4 * gp + 4], ld[s][:, j, 64 * g:64 * g + 64],
                                      pb[:, j, 4 * g:4 * g + 4], start=(j == 0), stop=(j == 3))
                    last.then_inc(S["sv_done"], 1)
            turns(pe, 4, sample_values, first=True)
            for g in range(4):
                gp, f = divmod(g, 2)
                out = pm[1][64 * f:64 * f + 64, 32 * gp:32 * gp + 32]
                mm(out, kvs[:, 768 + 64 * g:768 + 64 * g + 64], pTn[0:8, 0, 32 * g:32 * g + 32], start=True, stop=False)
                mm(out, kvs[:, 1280 + 64 * g:1280 + 64 * g + 64], pTn[0:8, 1, 32 * g:32 * g + 32], start=False, stop=False)
                last = mm(out, vcs[:, 64 * g:64 * g + 64], pTn[0:64, 2, 32 * g:32 * g + 32], start=False, stop=True)
            last.then_inc(S["sv_all"], 1)

            for n in range(8):
                i, kk = divmod(n, 2)
                if n >= 2:
                    pe.wait_ge(S["olo_ready"], n - 1)
                bank = (pm[0], pnb[1])[n % 2]
                for t in range(4):
                    last = nc.tensor.transpose(bank[:, 128 * t:128 * t + 128],
                                               Oacc[:, i, 512 * kk + 128 * t:512 * kk + 128 * t + 128], ident[:, :])
                last.then_inc(S["oT_tr"], 1)
            pe.wait_ge(S["olo_ready"], 9)
            phase("attn_out", h_hi, h_lo)
            norm_sum(5)
            norm_sum(6)
            ffn(1, 4)
            norm_sum(7)
            kept_rows(1)
            pe.wait_ge(S["s_taken"], 3)
            pe.wait_ge(S["x_updated"], 9 * 4)
            for n in range(10):
                if n >= 4:
                    pe.wait_ge(S["y_kept"], n - 3)
                for k in range(4):
                    kk = 4 * (n % 2) + k
                    if n < 8:
                        i = n // 2
                        last = nc.tensor.transpose(banks[n % 4][:, 128 * k:128 * k + 128],
                                                   x[:, kk, 128 * i:128 * i + 128], ident[:, :])
                    else:
                        last = nc.tensor.transpose(banks[n % 4][0:NS, 128 * k:128 * k + 128], x[:, kk, NP:NT], ident[:, :])
                last.then_inc(S["y_tr"], 1)

        @block.scalar
        def _(act):
            fn = nc.scalar.activation
            banks = [pnb[0], pnb[1], pm[0], pm[1]]
            ch = Chain(act, S["act_seq"])

            def split_hi(phase, i, s, first=False):
                w_wait(act, phase, i, s)
                if not first:
                    act.wait_ge(S["unit_done"], UBASE[phase] + 2 * i + s - 1)
                k = KOF[phase]
                fn(w_hi[s][:, 0:k, :], w_raw[s][:, 0:k, :], ACT.Copy).then_inc(S["w_hi_ready"], 1)

            def squares(m, tiles, waits):
                for k in range(KT):
                    for name, value in waits(k):
                        act.wait_ge(S[name], value)
                    if 8 * m + k >= 2:
                        act.wait_ge(S["sq_added"], 8 * m + k - 1)
                    fn(sqt[k % 2][:, :], tiles[:, k, :], ACT.Square).then_inc(S["sq_ready"], 1)

            def root(m):
                act.wait_ge(S["rs_ready"], m + 1)
                fn(rstd[:, :], rstd[:, :], ACT.Sqrt).then_inc(S["rstd_ready"], 1)

            def affine(q, scale, shift):
                for k in range(KT):
                    act.wait_ge(S["t_ready"], 8 * q + k + 1)
                    if 8 * q + k >= 2:
                        act.wait_ge(S["hlo_ready"], 9 * ((8 * q + k - 2) // 8) + (8 * q + k - 2) % 8 + 2)
                    fn(hf[k % 2][:, 0:NP], nt[k % 2][:, 0:NP], ACT.Identity, bias=shift[:, k, 0:1], scale=scale[:, k, 0:1])\
                        .then_inc(S["hf_ready"], 1)

            for t in range(0, 13, 2):
                act.wait_ge(S["tr_done"], t + 1)
                bank = banks[t % 4]
                if t < 5:
                    col = 0
                    for tile in range(4 * t, 4 * t + 4):
                        n = valid[tile]
                        last = fn(PT[:, 128 * tile:128 * tile + n], bank[:, col:col + n], ACT.Copy)
                        col += n
                else:
                    i, kk = divmod(t - 5, 2)
                    last = fn(x[:, 4 * kk:4 * kk + 4, 128 * i:128 * i + 128], bank.rearrange("p (k c) -> p k c", k=4), ACT.Copy)
                last.then_inc(S["tr_taken_a"], 1)
            act.wait_ge(S["tr_done"], 15)
            fn(lrow[:, 512:1024], banks[2][0:16, :], ACT.Copy).then_inc(S["tr_taken_a"], 1)
            act.wait_ge(S["tr_taken_a"], 8)
            act.wait_ge(S["tr_taken_v"], 7)
            act.dma_start(lines_d, lrow[:, :]).then_inc(S["lines_out"], 16)
            squares(0, x, lambda k: [("prep_done", 1)] if k == 0 else [])

            def mod_rows(s, first, count=6, base=0):
                for c in range(count):
                    q = base + 6 * s + c
                    act.wait_ge(S["mod_done"], q + 1)
                    if not (first and c < 2):
                        act.wait_ge(S["mod_t"], q - 1)
                    fn(mrow[c % 2][:, :], pm[c % 2][0:NC9, :], ACT.Copy).then_inc(S["mod_row"], 1)
            turns(act, 4, mod_rows, first=True)
            mod_rows(0, False, count=4, base=24)

            act.wait_ge(S["mod_done"], MOD_CHUNKS)
            for b in range(NS):
                act.dma_start(O["new_win_sample"][b, 0:PAST - 1].rearrange("t a g d -> t (a g d)"),
                              A["cache_win"][b, 1:PAST].rearrange("t a g d -> t (a g d)")).then_inc(S["win_out"], 16)
            for l in range(2):
                act.dma_start(O["new_ffn_conv_sample"][l, :, 0, :], A["state_ffn_conv"][l, :, 1, :]).then_inc(S["win_out"], 16)
            act.dma_start(O["new_conv_a_sample"][0, :, 0, :], A["state_conv_a"][0, :, 1, :]).then_inc(S["win_out"], 16)

            root(0)
            act.wait_ge(S["lines_out"], 16)
            split_hi("mix_in", 0, 0, first=True)
            split_hi("mix_in", 0, 1, first=True)
            sh, s_, _ = site(0)
            affine(0, s_, sh)

            def mix_in(i, first, last_turn=False):
                for u in range(6):
                    j, part = 2 * i + u // 3, u % 3
                    n = 6 * i + u
                    act.wait_ge(S["unit_done"], n + 1)
                    if not (first and u < 3):
                        act.wait_ge(S["z_made" if part < 2 else "mixed"], j)
                    fn((sg, yb[0], af)[part][:, :], prod[u % 2], ACT.Copy).then_inc(S["out_taken"], 1)
                    if part == 2:
                        hold(act, S["mixed"], j + 1)
                        fn(act_hi[:, bass.ds(j, 1), :].rearrange("p o n -> p (o n)"), hf[0][:, :], ACT.Copy).then_inc(S["mix_hi"], 1)
                    if not last_turn or u < 4:
                        split_next(i, u)
                    else:
                        split_hi("mix_out", 0, u % 2)

            def split_next(i, u):
                s = u % 2
                k = 3 * i + u // 2 + 1
                w_wait(act, "mix_in", k, s)
                act.wait_ge(S["unit_done"], 2 * k + s - 1)
                fn(w_hi[s][:, 0:KT, :], w_raw[s][:, 0:KT, :], ACT.Copy).then_inc(S["w_hi_ready"], 1)
            act.wait_ge(S["hlo_ready"], 9)
            mix_in(0, True)
            with act.Fori(1, 3) as i:
                mix_in(i, False)
            mix_in(3, False, last_turn=True)

            def out_phase(name, m, second=False, halves=0):
                if name == "attn_out":
                    split_hi(name, 0, 0)
                    split_hi(name, 0, 1)

                def body(i, first, last_turn=False):
                    for s in range(2):
                        n, k = UBASE[name] + 2 * i + s, 2 * i + s
                        act.wait_ge(S["unit_done"], n + 1)
                        if second:
                            act.wait_ge(S["half_added"], 8 * halves + k)
                            fn(nt[0][:, :], prod[s], ACT.Copy).then_inc(S["out_taken"], 1)
                        else:
                            act.sem_inc(S["passed"], 1)
                            fn(o[:, bass.ds(k, 1), :].rearrange("p a n -> p (a n)"), prod[s], ACT.Copy).then_inc(S["out_taken"], 1)
                        if not last_turn:
                            split_hi(name, i + 1, s)
                        elif name in NEXT:
                            split_hi(NEXT[name], 0, s)
                        if m is not None:
                            act.wait_ge(S["sq_added"], 8 * m + k - 1)
                            if second:
                                hold(act, S["half_added"], 8 * halves + k + 1)
                            else:
                                hold(act, S["out_taken"], n + 1)
                            fn(sqt[s][:, :], o[:, bass.ds(k, 1), :].rearrange("p a n -> p (a n)"), ACT.Square)\
                                .then_inc(S["sq_ready"], 1)
                body(0, True)
                with act.Fori(1, 3) as i:
                    body(i, False)
                body(3, False, last_turn=True)

            def up_phase(name, half):

                def body(i, first, last_turn=False):
                    for s in range(2):
                        n = UBASE[name] + 2 * i + s
                        act.wait_ge(S["unit_done"], n + 1)
                        if not (half == 0 and first):
                            act.wait_ge(S["conv_done"], 2 * (FH * half + i) - 1 + s)
                            act.wait_ge(S["up10_kept"], 2 * (FH * half + i) - 1 + s)
                        elif half == 0:
                            act.wait_ge(S["ub_zero"], 1)
                        fn(ub[s][:, 2:2 + NT], prod[s], ACT.Copy).then_inc(S["out_taken"], 1)
                        if not last_turn:
                            split_hi(name, i + 1, s)
                        else:
                            split_hi(NEXT[name], 0, s)
                    j = FH * half + i
                    act.wait_ge(S["conv_done"], 2 * j + 2)
                    fn(sg[:, :], yb[1][:, :], ACT.Silu).then_inc(S["silu_done"], 1)
                    hold(act, S["af_ready"], j + 1)
                    fn(act_hi[:, bass.ds(i, 1), :].rearrange("p o n -> p (o n)"), af[:, :], ACT.Copy)\
                        .then_inc(S["act_hi_done"], 1)
                body(0, True)
                with act.Fori(1, FH - 1) as i:
                    body(i, False)
                body(FH - 1, False, last_turn=True)

            def ffn(l, q):
                sh, s_, _ = site(2 * l + 1)
                affine(q, s_, sh)
                if l == 1:
                    act.wait_ge(S["ub_zero"], 2)
                up_phase(f"up{l}0", 2 * l)
                out_phase(f"down{l}0", None)
                up_phase(f"up{l}1", 2 * l + 1)
                out_phase(f"down{l}1", 4 * l + 3, second=True, halves=l)

            def history_out(l):
                act.wait_ge(S["s_tr"], 2 + l)
                if l == 1:
                    act.wait_ge(S["s_out"], 16 * 5)
                fn(st[:, 0:4, :], pm[0][0:88, :].rearrange("p (a c) -> p a c", a=4), ACT.Copy)
                fn(st[:, 4, :], pm[1][0:88, 0:128], ACT.Copy).then_inc(S["s_taken"], 1)
                act.wait_ge(S["s_taken"], 2 + l)
                act.dma_start(O["new_ffn_conv_prompt"][l, 0].rearrange("j (t c) -> (j t) c", c=128), st[:, 0, :])\
                   .then_inc(S["s_out"], 16)
                for f in range(2):
                    dst = O["new_ffn_conv_sample"][l, :, 1, :].rearrange("(a f) (t c) -> f t a c", f=2, c=128)
                    act.dma_start(dst[f], st[44 * f:44 * f + 44, 1:5, :]).then_inc(S["s_out"], 16)

            out_phase("mix_out", 1)
            act.wait_ge(S["s_tr"], 1)
            fn(st_z[:, :], pm[0][0:80, 0:128], ACT.Copy).then_inc(S["s_taken"], 1)
            act.wait_ge(S["s_taken"], 1)
            act.dma_start(O["new_conv_a_prompt"][0, 0].rearrange("j (t c) -> (j t) c", c=128), st_z[0:16, :])\
               .then_inc(S["s_out"], 16)
            act.dma_start(O["new_conv_a_sample"][0, :, 1, :].rearrange("b (t c) -> b t c", c=128), st_z[16:80, :])\
               .then_inc(S["s_out"], 16)
            root(1)
            squares(2, x, lambda k: [("x_updated", k + 2)])
            root(2)
            ffn(0, 1)
            root(3)
            history_out(0)
            squares(4, x, lambda k: [("x_updated", 9 + k + 2)])
            root(4)

            sh, s_, _ = site(4)
            affine(2, s_, sh)
            for c in range(6):
                for s in range(2):
                    m = 2 * c + s
                    act.wait_ge(S["unit_done"], UBASE["kv"] + m + 1)
                    dst = okv[:, m, :] if m < 8 else kT[:, m - 8, :]
                    if m == 8:
                        act.wait_ge(S["hlo_ready"], 27)
                    fn(dst, prod[s], ACT.Copy).then_inc(S["out_taken"], 1)
                    if c < 5:
                        split_hi("kv", c + 1, s)
            for n in range(15):
                t = 15 + n
                if t % 2:
                    continue
                act.wait_ge(S["tr_done"], t + 1)
                if n < 12:
                    dst, src = kvt[:, n % 4, 512 * (n // 4):512 * (n // 4) + 512], banks[t % 4]
                else:
                    dst, src = kvs[:, 512 * (n - 12):512 * (n - 12) + 512], banks[t % 4][0:NS, :]
                fn(dst, src, ACT.Copy).then_inc(S["tr_taken_a"], 1)
            act.wait_ge(S["tr_taken_a"], 15)
            act.wait_ge(S["tr_taken_v"], 15)
            act.dma_start(O["new_kv_prompt"][0].rearrange("(i p) s g d -> p i (s g d)", p=128), kvt[:, :, 0:1024])\
               .then_inc(S["kvp_out"], 16)
            act.dma_start(O["new_win_prompt"][0].rearrange("(i p) s g d -> p i (s g d)", p=128), kvt[:, :, 1024:1536])\
               .then_inc(S["kvp_out"], 16)
            act.dma_start(O["new_kv_sample"].rearrange("b o s g d -> (b o) (s g d)"), kvs[:, 0:1024]).then_inc(S["kvp_out"], 16)
            act.dma_start(O["new_win_sample"][:, PAST - 1].rearrange("b s g d -> b (s g d)"), kvs[:, 1024:1536])\
               .then_inc(S["kvp_out"], 16)

            for c in range(2):
                def rows(i, first):
                    for s in range(2):
                        hold(act, S["page_tr"], 8 * c + 2 * i + s + 1)
                        fn(RT[:, :, bass.ds(NP + 512 * i + 256 * s, 256)], pm[s][:, :].rearrange("p (g n) -> p g n", g=2),
                           ACT.Copy).then_inc(S["page_rows"], 1)
                if c == 1:
                    act.wait_ge(S["hid_done"], 1)
                turns(act, 4, rows)
                act.wait_ge(S["pe_tr"], c + 1)
                for g in range(2):
                    last = fn(RT[:, g, 2560:2592], pnb[1][:, 0:32], ACT.Copy)
                last.then_inc(S["rt_rest"], 1)
                act.wait_ge(S["hid_lin"], c + 1)
                fn(hz[:, :, :], hy[:, :, :], ACT.Tanh, scale=math.sqrt(2.0 / math.pi)).then_inc(S["hid_tanh"], 1)
                act.wait_ge(S["cmp_done"], c + 1)
                if c == 0:
                    fn(kcT[:, :, :], pnb[1][:, 0:160].rearrange("p (g n) -> p g n", g=2), ACT.Copy).then_inc(S["cmp_kept"], 1)
                else:
                    fn(vcp[:, :], pnb[1][0:16, 0:256], ACT.Copy)
                    fn(vcs[:, :], pnb[0][0:64, 0:256], ACT.Copy).then_inc(S["cmp_kept"], 1)
            act.wait_ge(S["cb_done"], 1)
            for c in range(2):
                last = fn(cb[:, 2 * c:2 * c + 2, :, :].rearrange("p i e n -> p i n e"),
                          pnb[c].rearrange("p (i n e) -> p i n e", i=2, n=16), ACT.Copy)
            last.then_inc(S["cb_kept"], 1)

            act.wait_ge(S["gate_w_in"], 16)
            fn(wg_hi[:, :, :], wg_raw[:, :, :], ACT.Copy).then_inc(S["wg_hi_s"], 1)
            sh, s_, _ = site(2)
            affine(3, s_, sh)
            split_hi("q", 0, 0)
            split_hi("q", 0, 1)
            act.wait_ge(S["g_done"], 1)
            fn(gat[:, :, :], pm[0][:, 0:192].rearrange("p (i n) -> p i n", i=4), ACT.Exp, scale=-1.0)
            fn(gts[:, :], pm[0][:, 192:240], ACT.Exp, scale=-1.0).then_inc(S["g_kept"], 1)
            act.wait_ge(S["g_rt"], 1)
            act.dma_start(gates_d, gts[120:128, :]).then_inc(S["g_sent"], 16)
            act.wait_ge(S["g_sent"], 16)
            act.dma_start(gr[:, :], bass.AP(gates_d.tensor, 0, [[3, 16], [48, 8], [1, 3]])).then_inc(S["g_back"], 16)

            for gp in range(2):
                def heads(it, first, last_turn=False):
                    T = 2 * gp + it
                    for u in range(2):
                        n = UBASE["q"] + 2 * T + u
                        act.wait_ge(S["unit_done"], n + 1)
                        if not (gp == 0 and first):
                            act.wait_ge(S["S_done"], NSI * T)
                        fn(qT[u][:, :], prod[0], ACT.Copy, scale=0.125).then_inc(S["out_taken"], 1)
                        hold(act, S["out_taken"], n + 1)
                        fn(qs[:, bass.ds(2 * T + u, 1), :].rearrange("p o b -> p (o b)"), qT[u][:, NP:NT], ACT.Copy)\
                            .then_inc(S["q_in_sb"], 1)
                        if not last_turn:
                            split_hi("q", T + 1, u)

                    def expo(step):
                        m, f, br, i = S_ITEMS[step][1]
                        act.wait_ge(S["nm_ready"], 32 * T + m + 1)
                        if not (gp == 0 and first and m < 4):
                            act.wait_ge(S["PT_done"], 32 * T + m - 3)
                            if not (gp == 0 and first and m < 8):
                                act.wait_ge(S["O_kept"], 32 * T + m - 7)
                        W = 128 * (i + 1)
                        fn(Pb[m % 4][:, 0:W], Ss[m % 2][:, 0:W], ACT.Exp, bias=nm[:, m % 4:m % 4 + 1],
                           accum_out=den[:, m % 8:m % 8 + 1]).then_inc(S["P_ready"], 1)

                    def keep_t(step):
                        m, f, br, i = S_ITEMS[step][1]
                        if m % 2:
                            return
                        act.wait_ge(S["PT_done"], 32 * T + m + 1)
                        if not (gp == 0 and first and m < 2):
                            act.wait_ge(S["O_done"], 32 * T + m - 1)
                        W = 128 * (i + 1)
                        fn(PTb[0][:, 0:W], pm[0][:, 0:W], ACT.Copy).then_inc(S["PT_kept_a"], 1)

                    for step in range(len(S_ITEMS) + 2):
                        if step < len(S_ITEMS) and S_ITEMS[step][1] is not None:
                            expo(step)
                        if step >= 2 and S_ITEMS[step - 2][1] is not None:
                            keep_t(step - 2)
                heads(0, gp == 0)
                heads(1, False, last_turn=(gp == 1))

            act.wait_ge(S["c_max"], 1)
            fn(sc[:, :, :, :].rearrange("p i e n -> p (i e n)"), sc[:, :, :, :].rearrange("p i e n -> p (i e n)"), ACT.Exp)\
                .then_inc(S["c_exp"], 1)
            for n in range(8):
                act.wait_ge(S["c_tr"], n + 1)
                if n >= 2:
                    act.wait_ge(S["c_out"], n - 1)
                fn(pcT[n % 2][:, :], pm[n % 2][:, 0:128], ACT.Copy).then_inc(S["c_trk"], 1)

            def sample_keys(i, first):
                for s in range(2):
                    b = 2 * i + s
                    act.wait_ge(S["sk_tr"], b + 1)
                    if not (first and s == 0):
                        act.wait_ge(S["s_sc"], b)
                    for gp in range(2):
                        last = fn(ksT[:, gp, :], pm[gp][:, :], ACT.Copy)
                    last.then_inc(S["sk_sb"], 2)
                    hold(act, S["s_sc"], b + 1)
                    for f in range(2):
                        STv = ST[:, :, bass.ds(b, 16, step=8)].rearrange("p j (g f q) -> p j g f q", g=2, f=2)
                        last = fn(STv[:, :, :, f], pnb[f][:, 0:32].rearrange("p (j g q) -> p j g q", j=4, g=2), ACT.Copy)
                    last.then_inc(S["s_sck"], 1)
            act.wait_ge(S["c_added"], 8)
            turns(act, 4, sample_keys, first=True)
            act.wait_ge(S["sn_done"], 1)
            for f, bank in enumerate((pm[0], pnb[1])):
                STv = STn[:, :, :].rearrange("p k (g f r) -> p k g f r", g=2, f=2)
                fn(STv[0:8, 0:2, :, f], bank[0:8, 0:128].rearrange("p (k g r) -> p k g r", k=2, g=2), ACT.Copy)
                fn(STv[0:64, 2, :, f], bank[0:64, 128:192].rearrange("p (g r) -> p g r", g=2), ACT.Copy).then_inc(S["sn_kept"], 1)
            fn(bias_s[:, :], pnb[0][:, 0:328], ACT.Copy).then_inc(S["sn_kept"], 1)
            act.wait_ge(S["sS_bias"], 1)
            for br, c0, n in ((0, 0, 264), (1, 264, 264), (2, 528, 64)):
                last = fn(Sa[:, c0:c0 + n], Sa[:, c0:c0 + n], ACT.Exp, bias=smx[:, br:br + 1], accum_out=sden[:, br:br + 1])
            last.then_inc(S["s_exp"], 1)
            act.wait_ge(S["sP_tr"], 1)
            fn(pT[:, :, :], pm[0][:, :].rearrange("p (j r) -> p j r", j=4), ACT.Copy).then_inc(S["sP_kept"], 1)
            fn(pTn[0:8, 0:2, :], pm[1][0:8, 0:256].rearrange("p (k r) -> p k r", k=2), ACT.Copy).then_inc(S["sP_kept"], 1)
            fn(pTn[0:64, 2, :], pm[1][0:64, 256:384], ACT.Copy).then_inc(S["sP_kept"], 1)

            for n in range(8):
                i, kk = divmod(n, 2)
                act.wait_ge(S["oT_tr"], n + 1)
                bank = (pm[0], pnb[1])[n % 2]
                fn(h_hi[:, 4 * kk:4 * kk + 4, 128 * i:128 * i + 128], bank.rearrange("p (t c) -> p t c", t=4), ACT.Copy)\
                    .then_inc(S["oh_ready"], 1)
            act.wait_ge(S["oS_done"], 1)
            fn(h_hi[:, :, NP:NT], oS[:, :, :], ACT.Copy).then_inc(S["oh_ready"], 1)

            act.wait_ge(S["olo_ready"], 9)
            out_phase("attn_out", 5)
            root(5)
            squares(6, x, lambda k: [("x_updated", 18 + k + 2)])
            root(6)
            ffn(1, 4)
            root(7)
            history_out(1)
            for n in range(10):
                act.wait_ge(S["y_tr"], n + 1)
                if n < 8:
                    i = n // 2
                    if i >= 2:
                        act.wait_ge(S[f"y_out{i % 2}"], 16)
                    fn(yt[i % 2][:, 512 * (n % 2):512 * (n % 2) + 512], banks[n % 4], ACT.Copy).then_inc(S["y_kept"], 1)
                else:
                    fn(yts[:, 512 * (n % 2):512 * (n % 2) + 512], banks[n % 4][0:NS, :], ACT.Copy).then_inc(S["y_kept"], 1)
            act.wait_ge(S["win_out"], 16 * 11)
            act.wait_ge(S["kvp_out"], 16 * 4)
            act.wait_ge(S["s_out"], 16 * 8)

        @block.vector
        def _(dve):
            v = nc.vector
            banks = [pnb[0], pnb[1], pm[0], pm[1]]
            ch = Chain(dve, S["dve_seq"])

            def wide(ap, n):
                return ap.unsqueeze(2).to_broadcast([ap.shape[0], ap.shape[1], n])

            v.memset(ones[:, :], 1.0).then_inc(S["ones_set"], 1)
            v.memset(tab[32:33, :], 1.0).then_inc(S["tab_set"], 1)
            dve.wait_ge(S["consts_in"], 16 * 8)
            dve.wait_ge(S["tab_set"], 1)
            v.tensor_copy(tabp[:, :].rearrange("t (g q f) -> t g q f", g=2, q=4),
                          tab[:, :].rearrange("t (g f q) -> t g q f", g=2, f=2))
            v.tensor_copy(tabr[:, :].rearrange("t (h b) -> t h b", b=NS), wide(tab[0:32, :], NS))

            for t in range(1, 15, 2):
                dve.wait_ge(S["tr_done"], t + 1)
                bank = banks[t % 4]
                if t < 5:
                    col = 0
                    for tile in range(4 * t, 4 * t + 4):
                        n = valid[tile]
                        last = v.tensor_copy(PT[:, 128 * tile:128 * tile + n], bank[:, col:col + n])
                        col += n
                elif t < 13:
                    i, kk = divmod(t - 5, 2)
                    last = v.tensor_copy(x[:, 4 * kk:4 * kk + 4, 128 * i:128 * i + 128], bank.rearrange("p (k c) -> p k c", k=4))
                else:
                    last = v.tensor_copy(lrow[:, 0:512], banks[1][0:16, :])
                last.then_inc(S["tr_taken_v"], 1)

            dve.wait_ge(S["tr_taken_a"], 7)
            dve.wait_ge(S["tr_taken_v"], 7)
            ch.link(v.tensor_copy(x[:, :, NP:NT], PTv(R_XS, 64).rearrange("p (b k) -> p k b", k=KT)))

            def history(out, state, w, n, tmp):
                st_ = state.rearrange("p (b j k) -> p j k b", b=NS, j=2)
                ch.mark(v.tensor_tensor(out, st_[:, 0], wide(w[:, 0:n], NS), ALU.mult))
                ch.link(v.tensor_tensor(tmp, st_[:, 1], wide(w[:, n:2 * n], NS), ALU.mult))
                ch.link(v.tensor_tensor(out, out, tmp, ALU.add))
            history(sca[:, :, :], PTv(R_STA, 128), PTv(R_ACW, 24), KT, ts[:, :, :])
            for l in range(2):
                history(scf[:, l], PTv(R_STF + 704 * l, 704), PTv(R_FCW + 132 * l, 132), 2 * FT,
                        nt[0][:, 0:352].rearrange("p (k b) -> p k b", b=NS))
            v.tensor_copy(st_z[0:1, 0:1], ones[0:1, 0:1]).then_inc(S["prep_done"], 1)

            def mods(s, first, count=6, base=0):
                for c in range(count):
                    q = base + 6 * s + c
                    dve.wait_ge(S["mod_t"], q + 1)
                    ft = 4 * q if isinstance(q, int) else 24 * s + 4 * c
                    v.tensor_tensor(modT[:, bass.ds(ft, 4), :], pnb[c % 2][:, 0:36].rearrange("p (t r) -> p t r", t=4),
                                    wide(PT[:, bass.ds(ft, 4)], NC9), ALU.add).then_inc(S["mod_t_taken"], 1)
            turns(dve, 4, mods)
            mods(0, False, count=4, base=24)
            dve.wait_ge(S["mod_t_taken"], MOD_CHUNKS)
            for k in range(5):
                sh, s_, gate = site(k)
                g = PTv(R_NG + 16 * k, 8) if k < 4 else PTv(R_KVG, 8)
                ch.mark(v.scalar_tensor_tensor(s_, s_, 1.0, wide(g, NC9), ALU.add, ALU.mult))
                if k < 4:
                    ch.mark(v.tensor_tensor(gate, gate, wide(PTv(R_NG + 16 * k + 8, 8), NC9), ALU.mult))
            ch.settle()

            def mean(m):
                dve.wait_ge(S["norm_done"], m + 1)
                ch.link(v.tensor_scalar(rstd[:, :], pn[:, PSO:PSO + NT], 1.0 / D, EPS, ALU.mult, ALU.add))
                v.reciprocal(rstd[:, :], rstd[:, :]).then_inc(S["rs_ready"], 1)
                dve.wait_ge(S["rstd_ready"], m + 1)

            rs_s = rstd[:, NP:NT].unsqueeze(1).to_broadcast([128, KT, NS])

            def modulate(q, scale, shift):
                if q > 0:
                    dve.wait_ge(S["hlo_ready"], 9 * q)
                ch.link(v.tensor_tensor(ts[:, :, :], x[:, :, NP:NT], rs_s, ALU.mult))
                ch.link(v.tensor_tensor(ts[:, :, :], ts[:, :, :], scale[:, :, 1:NC9], ALU.mult))
                ch.link(v.tensor_tensor(ts[:, :, :], ts[:, :, :], shift[:, :, 1:NC9], ALU.add))
                v.tensor_copy(h_hi[:, :, NP:NT], ts[:, :, :]).then_inc(S["hhi_ready"], 1)
                for k in range(KT + 1):
                    if k < KT:
                        if 8 * q + k >= 2:
                            dve.wait_ge(S["hf_ready"], 8 * q + k - 1)
                        v.tensor_tensor(nt[k % 2][:, 0:NP], x[:, k, 0:NP], rstd[:, 0:NP], ALU.mult).then_inc(S["t_ready"], 1)
                    if k > 0:
                        dve.wait_ge(S["hf_ready"], 8 * q + k)
                        v.tensor_copy(h_hi[:, k - 1, 0:NP], hf[(k - 1) % 2][:, 0:NP]).then_inc(S["hhi_ready"], 1)

            def update(p, gate):
                ch.link(v.tensor_tensor(ts[:, :, :], o[:, :, NP:NT], rs_s, ALU.mult))
                ch.link(v.tensor_tensor(ts[:, :, :], ts[:, :, :], gate[:, :, 1:NC9], ALU.mult))
                v.tensor_tensor(x[:, :, NP:NT], x[:, :, NP:NT], ts[:, :, :], ALU.add).then_inc(S["x_updated"], 1)
                for k in range(KT):
                    ch.link(v.tensor_tensor(nt[k % 2][:, 0:NP], o[:, k, 0:NP], rstd[:, 0:NP], ALU.mult))
                    v.scalar_tensor_tensor(x[:, k, 0:NP], nt[k % 2][:, 0:NP], gate[:, k, 0:1], x[:, k, 0:NP], ALU.mult, ALU.add)\
                     .then_inc(S["x_updated"], 1)
                dve.wait_ge(S["x_updated"], 9 * (p + 1))

            def conv(y, u, w, b, history_term):
                ch.link(v.tensor_scalar(y[:, :], u[:, 2:2 + NT], w[2], b, ALU.mult, ALU.add))
                ch.mark(v.tensor_tensor(y[:, NP:NT], y[:, NP:NT], history_term, ALU.add))
                ch.link(v.scalar_tensor_tensor(y[:, 0:NP], u[:, 1:1 + NP], w[1], y[:, 0:NP], ALU.mult, ALU.add))
                return v.scalar_tensor_tensor(y[:, 0:NP], u[:, 0:NP], w[0], y[:, 0:NP], ALU.mult, ALU.add)

            mean(0)
            sh, s_, _ = site(0)
            modulate(0, s_, sh)

            def mix(i, first):
                for e in range(2):
                    j = 2 * i + e
                    dve.wait_ge(S["out_taken"], 6 * i + 3 * e + 2)
                    if first and e == 0:
                        dve.wait_ge(S["ub_zero"], 1)
                    else:
                        dve.wait_ge(S["z10_kept"], j)
                    ch.link(v.tensor_tensor(ub[0][:, 2:2 + NT], sg[:, :], yb[0][:, :], ALU.mult))
                    v.tensor_copy(zflag[:, 0:1], ub[0][:, 2:3]).then_inc(S["z_made"], 1)
                    w = [PT[:, bass.ds(R_ACW + 8 * t + j, 1)] for t in range(3)]
                    ch.link(conv(yb[1], ub[0], w, PT[:, bass.ds(R_ACB + j, 1)],
                                 sca[:, bass.ds(j, 1), :].rearrange("p o b -> p (o b)")))
                    dve.wait_ge(S["out_taken"], 6 * i + 3 * e + 3)
                    if first and e == 0:
                        dve.wait_ge(S["hlo_ready"], 9)
                    else:
                        dve.wait_ge(S["mix_lo"], j)
                    v.tensor_tensor(hf[0][:, :], yb[1][:, :], af[:, :], ALU.mult).then_inc(S["mixed"], 1)
            ch.turns(4, 10, mix, first=True)

            mean(1)
            update(0, site(0)[2])
            mean(2)

            def ffn_pairs(l, half, half_l):
                def body(i, first):
                    j = FH * half + i
                    for s in range(2):
                        n = UBASE[f"up{l}{half_l}"] + 2 * i + s
                        dve.wait_ge(S["out_taken"], n + 1)
                        if not (half == 0 and first):
                            dve.wait_ge(S["silu_done" if s else "af_ready"], j)
                        ft = FH * half_l + i + FT * s
                        w = [PT[:, bass.ds(R_FCW + 132 * l + 44 * t + ft, 1)] for t in range(3)]
                        conv(yb[s], ub[s], w, PT[:, bass.ds(R_FCB + 44 * l + ft, 1)],
                             scf[:, l, bass.ds(ft, 1), :].rearrange("p o b -> p (o b)")).then_inc(S["conv_done"], 1)
                    dve.wait_ge(S["silu_done"], j + 1)
                    dve.wait_ge(S["conv_done"], 2 * j + 1)
                    if not (half == 0 and first):
                        dve.wait_ge(S["act_lo_done"], j)
                    v.tensor_tensor(af[:, :], sg[:, :], yb[0][:, :], ALU.mult).then_inc(S["af_ready"], 1)
                ch.turns(FH, 6, body, first=(half == 0))

            def add_halves(l):
                def body(i, first):
                    for s in range(2):
                        dve.wait_ge(S["out_taken"], UBASE[f"down{l}1"] + 2 * i + s + 1)
                        ok = o[:, bass.ds(2 * i + s, 1), :].rearrange("p a n -> p (a n)")
                        v.tensor_tensor(ok, ok, nt[0][:, :], ALU.add).then_inc(S["half_added"], 1)
                turns(dve, 4, body)

            def ffn(l, q):
                sh, s_, _ = site(2 * l + 1)
                modulate(q, s_, sh)
                ffn_pairs(l, 2 * l, 0)
                ffn_pairs(l, 2 * l + 1, 1)
                add_halves(l)

            ffn(0, 1)
            mean(3)
            update(1, site(1)[2])
            mean(4)
            sh, s_, _ = site(4)
            modulate(2, s_, sh)

            for n in range(15):
                t = 15 + n
                if t % 2 == 0:
                    continue
                dve.wait_ge(S["tr_done"], t + 1)
                if n < 12:
                    dst, src = kvt[:, n % 4, 512 * (n // 4):512 * (n // 4) + 512], banks[t % 4]
                else:
                    dst, src = kvs[:, 512 * (n - 12):512 * (n - 12) + 512], banks[t % 4][0:NS, :]
                v.tensor_copy(dst, src).then_inc(S["tr_taken_v"], 1)

            for c in range(2):
                dve.wait_ge(S["hid_done"], c + 1)
                if c == 1:
                    dve.wait_ge(S["cmp_done"], 1)
                hid = pn[:, 0:162].rearrange("p (g n) -> p g n", g=2)
                ch.link(v.tensor_copy(hemb[:, :], pn[:, 80:81]))
                ch.link(v.tensor_scalar(hx[:, :, :], hid[:, :, 0:80], hemb[:, 0:1], None, ALU.add))
                ch.link(v.tensor_tensor(hy[:, :, :], hx[:, :, :], hx[:, :, :], ALU.mult))
                ch.link(v.tensor_tensor(hy[:, :, :], hy[:, :, :], hx[:, :, :], ALU.mult))
                v.scalar_tensor_tensor(hy[:, :, :], hy[:, :, :], 0.044715, hx[:, :, :], ALU.mult, ALU.add)\
                    .then_inc(S["hid_lin"], 1)
                dve.wait_ge(S["hid_tanh"], c + 1)
                ch.link(v.tensor_scalar(hz[:, :, :], hz[:, :, :], 1.0, 0.5, ALU.add, ALU.mult))
                v.tensor_tensor(hx[:, :, :], hx[:, :, :], hz[:, :, :], ALU.mult).then_inc(S["hid_act"], 1)

            dve.wait_ge(S["cb_kept"], 1)
            dve.wait_ge(S["wg_hi_s"], 1)
            v.tensor_tensor(wg_lo[:, :, :], wg_raw[:, :, :], wg_hi[:, :, :].bitcast(f32), ALU.subtract).then_inc(S["wg_lo_s"], 1)
            sh, s_, _ = site(2)
            modulate(3, s_, sh)
            dve.wait_ge(S["g_kept"], 1)
            ch.mark(v.tensor_scalar_add(gat[:, :, :], gat[:, :, :], 1.0))
            ch.link(v.tensor_scalar_add(gts[:, :], gts[:, :], 1.0))
            ch.mark(v.reciprocal(gat[:, :, :], gat[:, :, :]))
            v.reciprocal(gts[:, :], gts[:, :]).then_inc(S["g_rt"], 1)
            ch.settle()

            for gp in range(2):
                def heads(it, first):
                    T = 2 * gp + it

                    def bias(step):
                        u, item = S_ITEMS[step]
                        dve.wait_ge(S["S_done"], NSI * T + step + 1)
                        if item is None:
                            e = 8 * gp + 4 * it + 2 * u + step % 2
                            v.tensor_tensor(sc[:, :, bass.ds(e, 1), :].rearrange("p i o n -> p i (o n)"),
                                            pnb[step % 2][:, 0:64].rearrange("p (i n) -> p i n", i=4),
                                            cb[:, :, bass.ds(e, 1), :].rearrange("p i o n -> p i (o n)"), ALU.add)\
                                .then_inc(S["S_biased"], 1)
                            return
                        m, f, br, i = item
                        W = 128 * (i + 1)
                        if not (gp == 0 and first and m < 2):
                            dve.wait_ge(S["P_ready"], 32 * T + m - 1)
                        hold(dve, S[f"H_in{2 * u + f}"], 16 * (T + 1))
                        v.tensor_tensor_reduce(out=Ss[m % 2][:, 0:W], in0=pnb[step % 2][:, 0:W],
                                               in1=Hb[2 * u + f][:, 0:W][:, ::-1], scale=1.0, scalar=-3.0e38,
                                               op0=ALU.add, op1=ALU.max, accum_out=mx[:, m % 4:m % 4 + 1])\
                            .then_inc(S["S_biased"], 1)
                        dve.wait_ge(S["S_biased"], NSI * T + step + 1)
                        ins = v.tensor_scalar(nm[:, m % 4:m % 4 + 1], mx[:, m % 4:m % 4 + 1], -1.0, None, ALU.mult)
                        ins.then_inc(S["nm_ready"], 1)
                        if br == 1 and i == 0:
                            v.tensor_copy(zflag[:, 0:1], ones[:, 0:1]).then_inc(S["head_used"], 1)

                    def keep_t(step):
                        m, f, br, i = S_ITEMS[step][1]
                        if m % 2 == 0:
                            return
                        dve.wait_ge(S["PT_done"], 32 * T + m + 1)
                        if not (gp == 0 and first and m < 2):
                            dve.wait_ge(S["O_done"], 32 * T + m - 1)
                        W = 128 * (i + 1)
                        v.tensor_copy(PTb[1][:, 0:W], pm[1][:, 0:W]).then_inc(S["PT_kept_v"], 1)

                    def gather(step):
                        u = S_ITEMS[step][0]
                        m, f, br, i = S_ITEMS[step][1]
                        dve.wait_ge(S["P_ready"], 32 * T + m + 1)
                        c = cf[:, m % 4:m % 4 + 1]
                        ch.link(v.reciprocal(c, den[:, m % 8:m % 8 + 1]))
                        gcol = 3 * (8 * gp + 4 * f + 2 * it + u) + 1 + br
                        ch.link(v.tensor_tensor(c, c, gat[:, i, bass.ds(gcol, 1)], ALU.mult))
                        dve.wait_ge(S["O_done"], 32 * T + m + 1)
                        dst = Oacc[:, i, bass.ds(64 * (8 * gp + 4 * it + 2 * u + f), 64)]
                        O_ = pu[1][:, 512 * (m % 2):512 * (m % 2) + 64]
                        if br == 0:
                            ins = v.tensor_scalar(dst, O_, c, None, ALU.mult)
                        else:
                            ins = v.scalar_tensor_tensor(dst, O_, c, dst, ALU.mult, ALU.add)
                        ins.then_inc(S["O_kept"], 1)

                    for step in range(len(S_ITEMS) + 4):
                        if step < len(S_ITEMS):
                            bias(step)
                        if 2 <= step < len(S_ITEMS) + 2 and S_ITEMS[step - 2][1] is not None:
                            keep_t(step - 2)
                        if step >= 4 and S_ITEMS[step - 4][1] is not None:
                            gather(step - 4)
                ch.turns(2, 2 * 32, heads, first=(gp == 0))
            dve.wait_ge(S["O_kept"], 128)

            rows = sc[:, :, :, :].rearrange("p i e n -> p (i e) n")
            ch.link(v.tensor_reduce(cm[:, :], rows, AX.X, ALU.max))
            ch.link(v.tensor_scalar(cm[:, :], cm[:, :], FLOOR, None, ALU.max))
            v.tensor_tensor(rows, rows, wide(cm[:, :], 16), ALU.subtract).then_inc(S["c_max"], 1)
            for gp in range(2):
                dve.wait_ge(S["vrep_done"], gp + 1)
                for q in range(4):
                    e = 2 * q
                    last = v.tensor_tensor(vblk[:, gp, 128 * q:128 * q + 128].rearrange("p (f d) -> p f d", f=2),
                                           pm[gp][:, 0:128].rearrange("p (f d) -> p f d", f=2), wide(blk[:, e:e + 2], 64), ALU.mult)
                last.then_inc(S["v_blk"], 1)
            dve.wait_ge(S["c_exp"], 1)
            ch.link(v.tensor_reduce(cd[:, :], rows, AX.X, ALU.add))
            ch.link(v.tensor_scalar(cd[:, :], cd[:, :], 1.0e-30, None, ALU.max))
            ch.link(v.reciprocal(cd[:, :], cd[:, :]))
            gq = gat[:, :, :].rearrange("p i (g f q b) -> p i g q f b", g=2, f=2, q=4)
            cdv = cd[:, :].rearrange("p (i g q f) -> p i g q f", i=4, g=2, q=4)
            for i in range(4):
                for g in range(2):
                    ch.mark(v.tensor_tensor(cdv[:, i, g], cdv[:, i, g], gq[:, i, g, :, :, 0], ALU.mult))
            ch.settle()
            v.tensor_tensor(rows, rows, wide(cd[:, :], 16), ALU.mult).then_inc(S["c_prob"], 1)
            for n in range(8):
                i, g = divmod(n, 2)
                dve.wait_ge(S["c_out"], n + 1)
                dst = Oacc[:, i, 512 * g:512 * g + 512]
                v.tensor_tensor(dst, dst, pnb[n % 2], ALU.add).then_inc(S["c_added"], 1)

            def queries(i, first):
                for s in range(2):
                    b = 2 * i + s
                    if not (first and s == 0):
                        dve.wait_ge(S["s_sc"], b)
                    v.tensor_copy(qb[:, :], qs[:, :, bass.ds(b, 1)].rearrange("p t o -> p (t o)")).then_inc(S["qb_set"], 1)
            dve.wait_ge(S["c_added"], 8)
            dve.wait_ge(S["kvp_out"], 16 * 4)
            turns(dve, 4, queries, first=True)
            dve.wait_ge(S["sS_tr"], 1)
            dve.wait_ge(S["sn_kept"], 3)
            for k, c0 in enumerate((0, 264)):
                ch.mark(v.tensor_tensor(Sa[:, c0:c0 + 256], pm[1][:, 256 * k:256 * k + 256], bias_s[:, 0:256], ALU.add))
                ch.mark(v.tensor_tensor(Sa[:, c0 + 256:c0 + 264], pnb[1][:, 8 * k:8 * k + 8], bias_s[:, 256:264], ALU.add))
            ch.link(v.tensor_tensor(Sa[:, 528:592], pnb[1][:, 16:80], bias_s[:, 264:328], ALU.add))
            for c0, n, m0 in ((256, 8, 0), (520, 8, 0), (528, 64, 8)):
                ch.mark(v.tensor_tensor(Sa[:, c0:c0 + n], Sa[:, c0:c0 + n], smask[:, m0:m0 + n], ALU.add))
            ch.settle()
            for br, c0, n in ((0, 0, 264), (1, 264, 264), (2, 528, 64)):
                ch.mark(v.tensor_reduce(smx[:, br:br + 1], Sa[:, c0:c0 + n], AX.X, ALU.max))
            ch.settle()
            v.tensor_scalar(smx[:, 0:3], smx[:, 0:3], -1.0, None, ALU.mult).then_inc(S["sS_bias"], 1)
            dve.wait_ge(S["s_exp"], 1)
            dve.wait_ge(S["g_back"], 16)
            ch.link(v.reciprocal(scof[:, 0:3], sden[:, 0:3]))
            for br, gcol in ((0, 1), (1, 2), (2, 0)):
                ch.mark(v.tensor_tensor(scof[:, br:br + 1], scof[:, br:br + 1], gr[:, gcol:gcol + 1], ALU.mult))
            ch.settle()
            for br, c0, n in ((0, 0, 264), (1, 264, 264), (2, 528, 64)):
                last = v.tensor_scalar(Sa[:, c0:c0 + n], Sa[:, c0:c0 + n], scof[:, br:br + 1], None, ALU.mult)
            last.then_inc(S["s_p"], 1)
            dve.wait_ge(S["sP_kept"], 3)

            def values(i, first):
                for s in range(2):
                    b = 2 * i + s
                    if not (first and s == 0):
                        dve.wait_ge(S["sv_done"], b)
                    v.tensor_copy(pb[:, :, :], pT[:, :, bass.ds(b, 16, step=8)]).then_inc(S["pb_set"], 1)
                    dve.wait_ge(S["sv_done"], b + 1)
                    v.tensor_copy(oS[:, :, bass.ds(b, 1)].rearrange("p t o -> p (t o)"), pnb[0][:, 0:8]).then_inc(S["sv_kept"], 1)
            turns(dve, 4, values, first=True)
            dve.wait_ge(S["sv_all"], 1)
            dve.wait_ge(S["sv_kept"], 8)
            v.tensor_tensor(oS[:, :, :].rearrange("p t b -> p (t b)"), oS[:, :, :].rearrange("p t b -> p (t b)"), pm[1][:, 0:64],
                            ALU.add).then_inc(S["oS_done"], 1)

            for n in range(8):
                i, kk = divmod(n, 2)
                dve.wait_ge(S["oh_ready"], n + 1)
                bank = (pm[0], pnb[1])[n % 2].rearrange("p (t c) -> p t c", t=4)
                v.tensor_tensor(h_lo[:, 4 * kk:4 * kk + 4, 128 * i:128 * i + 128], bank,
                                h_hi[:, 4 * kk:4 * kk + 4, 128 * i:128 * i + 128].bitcast(f32), ALU.subtract)\
                    .then_inc(S["olo_ready"], 1)
            dve.wait_ge(S["oh_ready"], 9)
            dve.wait_ge(S["oS_done"], 1)
            v.tensor_tensor(h_lo[:, :, NP:NT], oS[:, :, :], h_hi[:, :, NP:NT].bitcast(f32), ALU.subtract)\
                .then_inc(S["olo_ready"], 1)

            mean(5)
            update(2, site(2)[2])
            mean(6)
            ffn(1, 4)
            mean(7)
            update(3, site(3)[2])

        @block.gpsimd
        def _(pool):
            g = nc.gpsimd

            def split_lo(phase, i, s):
                n, k = UBASE[phase] + 2 * i + s, KOF[phase]
                pool.wait_ge(S["w_hi_ready"], n + 1)
                g.tensor_tensor(w_lo[s][:, 0:k, :], w_raw[s][:, 0:k, :], w_hi[s][:, 0:k, :].bitcast(f32), ALU.subtract)\
                    .then_inc(S["w_lo_ready"], 1)

            def add_square(m, k, s, first):
                pool.wait_ge(S["sq_ready"], 8 * m + k + 1)
                if first:
                    if m > 0:
                        pool.wait_ge(S["norm_done"], m)
                    g.tensor_copy(sq[:, :], sqt[s][:, :]).then_inc(S["sq_added"], 1)
                else:
                    pool.wait_ge(S["sq_added"], 8 * m + k)
                    g.tensor_tensor(sq[:, :], sq[:, :], sqt[s][:, :], ALU.add).then_inc(S["sq_added"], 1)

            def trail(q):
                for k in range(KT + 1):
                    pool.wait_ge(S["hhi_ready"], 9 * q + k + 1)
                    if k == 0:
                        dst, full, hi = h_lo[:, :, NP:NT], ts[:, :, :], h_hi[:, :, NP:NT]
                    else:
                        dst, full, hi = h_lo[:, k - 1, 0:NP], hf[(k - 1) % 2][:, 0:NP], h_hi[:, k - 1, 0:NP]
                    g.tensor_tensor(dst, full, hi.bitcast(f32), ALU.subtract).then_inc(S["hlo_ready"], 1)

            for k in range(KT):
                add_square(0, k, k % 2, k == 0)
            split_lo("mix_in", 0, 0)
            split_lo("mix_in", 0, 1)
            trail(0)
            pool.wait_ge(S["mod_done"], MOD_CHUNKS)
            for s in range(2):
                last = g.memset(ub[s][:, 0:2], 0.0)
            last.then_inc(S["ub_zero"], 1)

            def mix(i, first, last_turn=False):
                for u in range(6):
                    j, part = 2 * i + u // 3, u % 3
                    if part == 1:
                        pool.wait_ge(S["z_made"], j + 1)
                        g.tensor_copy(z10[:, :, bass.ds(j, 1)].rearrange("p t o -> p (t o)"), ub[0][:, NP:NP + 10])\
                            .then_inc(S["z10_kept"], 1)
                    if part == 2:
                        pool.wait_ge(S["mix_hi"], j + 1)
                        g.tensor_tensor(act_lo[:, bass.ds(j, 1), :].rearrange("p o n -> p (o n)"), hf[0][:, :],
                                        act_hi[:, bass.ds(j, 1), :].rearrange("p o n -> p (o n)").bitcast(f32), ALU.subtract)\
                            .then_inc(S["mix_lo"], 1)
                    if not last_turn or u < 4:
                        s = u % 2
                        pool.wait_ge(S["w_hi_ready"], 6 * i + u + 3)
                        g.tensor_tensor(w_lo[s][:, 0:KT, :], w_raw[s][:, 0:KT, :], w_hi[s][:, 0:KT, :].bitcast(f32), ALU.subtract)\
                            .then_inc(S["w_lo_ready"], 1)
                    else:
                        split_lo("mix_out", 0, u % 2)
            mix(0, True)
            with pool.Fori(1, 3) as i:
                mix(i, False)
            mix(3, False, last_turn=True)

            def out_phase(name, m):
                if name == "attn_out":
                    split_lo(name, 0, 0)
                    split_lo(name, 0, 1)

                def body(i, first, last_turn=False):
                    for s in range(2):
                        if not last_turn:
                            split_lo(name, i + 1, s)
                        elif name in NEXT:
                            split_lo(NEXT[name], 0, s)
                        if m is not None:
                            add_square(m, 2 * i + s, s, first and s == 0)
                body(0, True)
                with pool.Fori(1, 3) as i:
                    body(i, False)
                body(3, False, last_turn=True)

            def up_phase(name, half, half_l):
                def body(i, first, last_turn=False):
                    j = FH * half + i
                    for s in range(2):
                        if not last_turn:
                            split_lo(name, i + 1, s)
                        else:
                            split_lo(NEXT[name], 0, s)
                        pool.wait_ge(S["out_taken"], UBASE[name] + 2 * i + s + 1)
                        g.tensor_copy(up10[:, :, bass.ds(FH * half_l + i + FT * s, 1)].rearrange("p t o -> p (t o)"),
                                      ub[s][:, NP:NP + 10]).then_inc(S["up10_kept"], 1)
                    pool.wait_ge(S["act_hi_done"], j + 1)
                    g.tensor_tensor(act_lo[:, bass.ds(i, 1), :].rearrange("p o n -> p (o n)"), af[:, :],
                                    act_hi[:, bass.ds(i, 1), :].rearrange("p o n -> p (o n)").bitcast(f32), ALU.subtract)\
                        .then_inc(S["act_lo_done"], 1)
                body(0, True)
                with pool.Fori(1, FH - 1) as i:
                    body(i, False)
                body(FH - 1, False, last_turn=True)

            def ffn(l, q):
                trail(q)
                up_phase(f"up{l}0", 2 * l, 0)
                out_phase(f"down{l}0", None)
                up_phase(f"up{l}1", 2 * l + 1, 1)
                out_phase(f"down{l}1", 4 * l + 3)

            out_phase("mix_out", 1)
            for k in range(KT):
                add_square(2, k, k % 2, k == 0)
            ffn(0, 1)
            for k in range(KT):
                add_square(4, k, k % 2, k == 0)
            trail(2)
            for c in range(1, 6):
                for s in range(2):
                    split_lo("kv", c, s)
            pool.wait_ge(S["unit_done"], UBASE["kv"] + 1)
            g.memset(w1b[:, :, :], 0.0)
            g.memset(w2b[:, :, :], 0.0).then_inc(S["w1_zero"], 1)
            for c in range(2):
                pool.wait_ge(S["out_taken"], UBASE["q"])
                pool.wait_ge(S["unit_done"], UBASE["q"])
                if c == 1:
                    pool.wait_ge(S["hid_done"], 1)
                for gp in range(2):
                    g.tensor_copy(RT[:, gp, 0:NP], okv[:, 2 * c + gp, 0:NP]).then_inc(S["rt_rest"], 1)
            trail(3)
            split_lo("q", 0, 0)
            split_lo("q", 0, 1)
            for T in range(3):
                for u in range(2):
                    split_lo("q", T + 1, u)
            out_phase("attn_out", 5)
            for k in range(KT):
                add_square(6, k, k % 2, k == 0)
            for s in range(2):
                last = g.memset(ub[s][:, 0:2], 0.0)
            last.then_inc(S["ub_zero"], 1)
            ffn(1, 4)


_INS = ['x_prompt', 'x_sample', 'c_prompt', 'c_sample', 'cache_kv', 'cache_win', 'state_conv_a', 'state_ffn_conv',
        'page_table', 'mod_w', 'mod_b', 'norm_g', 'a_w_in', 'a_conv_w', 'a_conv_b', 'a_w_out', 'kv_mod_w', 'kv_mod_b',
        'kv_norm_g', 'w_kv', 'cmp_pe', 'cmp_w1', 'cmp_w2', 'b_w_qg', 'b_w_out', 'rel_bias', 'ffn_w_up', 'ffn_conv_w',
        'ffn_conv_b', 'ffn_w_down']
_OUTS = [('y_prompt', (1, 512, 1024)), ('y_sample', (8, 1, 1024)), ('new_kv_prompt', (1, 512, 4, 4, 64)),
         ('new_kv_sample', (8, 1, 4, 4, 64)), ('new_win_prompt', (1, 512, 2, 4, 64)), ('new_win_sample', (8, 256, 2, 4, 64)),
         ('new_conv_a_prompt', (1, 1, 2, 1024)), ('new_conv_a_sample', (1, 8, 2, 1024)),
         ('new_ffn_conv_prompt', (2, 1, 2, 5632)), ('new_ffn_conv_sample', (2, 8, 2, 5632))]


def kernel(**inputs):
    import numpy as _np
    import concourse.bacc as _bacc
    from concourse import mybir as _mybir
    from concourse.bass_utils import run_bass_kernel_spmd as _run

    nc = _bacc.Bacc("TRN2", target_bir_lowering=False, num_devices=1)
    arrays, ins, outs = {}, {}, {}
    tables = constants()
    for name in _INS + list(tables):
        a = _np.ascontiguousarray(inputs[name] if name in inputs else tables[name])
        arrays[f"in_{name}"] = a
        ins[name] = nc.dram_tensor(f"in_{name}", a.shape, _mybir.dt.from_np(a.dtype), kind="ExternalInput").ap()
    for name, shape in _OUTS:
        outs[name] = nc.dram_tensor(f"out_{name}", shape, _mybir.dt.float32, kind="ExternalOutput").ap()
    decoder_step(nc, ins, outs)
    r = _run(nc, [arrays], core_ids=[0])
    return tuple(r.results[0][f"out_{name}"] for name, _ in _OUTS)
```

```python
import math
from contextlib import ExitStack

import numpy as np
import concourse.bass as bass
from concourse import mybir

D = 1024
NP = 512
NS = 8
NT = NP + NS
HALF = NT // 2
KT = D // 128
FF = 2816
FT = FF // 128
FH = FT // 2
NC9 = NS + 1
HD = 64
PAST = 256
EPS = 1e-6
NEG = -1.0e30
FLOOR = -1.0e29
PSO = 512 - HALF
R_MODB, R_KVG, R_ACB = 0, 112, 120
R_NG, R_ACW = 128, 192
R_FCB, R_FCW = 256, 384
R_STA, R_STF = 768, 896
R_C, R_XS = 2304, 2432
PT_TILES = 20
UNITS = [("mix_in", 24), ("mix_out", 8), ("up00", 22), ("down00", 8), ("up01", 22), ("down01", 8),
         ("kv", 12), ("q", 8), ("attn_out", 8), ("up10", 22), ("down10", 8), ("up11", 22), ("down11", 8)]
UBASE, _n = {}, 0
for _name, _c in UNITS:
    UBASE[_name] = _n
    _n += _c
KV_SLOTS = [0, 1, 3, 5, 2, 4]
MODS = ([(0, c, z) for c, z in enumerate(("z2", "z0", "z1", "z2", "z0", "z1"))]
        + [(1, c, z) for c, z in enumerate(("h0", "h1", "z0", "z1", "z0", "z1"))]
        + [(4, c, z) for c, z in enumerate(("h0", "h1", "z0", "z1"))]
        + [(2, c, z) for c, z in enumerate(("w0", "w1", "w0", "w1", "w0", "w1"))]
        + [(3, c, z) for c, z in enumerate(("z0", "z1", "h0", "h1", "z0", "z1"))])
MOD_AT = {k: [m[0] for m in MODS].index(k) for k in range(5)}


S_ITEMS, N_TABLES = [], 14
for _u in range(2):
    S_ITEMS += [(_u, None), (_u, None)]
    S_ITEMS += [(_u, (16 * _u + 8 * f + 4 * br + 3 - i, f, br, i)) for f in range(2) for br in range(2)
                for i in (3, 2, 1, 0)]


NSI = len(S_ITEMS)


def bucket(d):
    if d < 16:
        return max(d, 0)
    f = np.float32(np.log(np.float32(d) / np.float32(16)))
    return min(16 + int(np.float32(f / np.float32(math.log(64)) * np.float32(16))), 31)


def constants():
    ident = np.eye(128, dtype=np.float32)
    line = np.zeros((33, 1024), np.float32)
    for x in range(1024):
        if x < 512:
            line[32, x] = NEG
        else:
            line[bucket(x - 512), x] = 1
    srow = np.zeros((32, 328), np.float32)
    for j in range(256):
        srow[bucket(256 - j), j] = 1
    srow[0, 256:264] = 1
    for b in range(8):
        for n in range(8):
            srow[bucket(256 - 32 * n - 31), 264 + 8 * b + n] = 1
    smask = np.zeros((128, 72), np.float32)
    for r in range(128):
        for b in range(8):
            if b != r % 8:
                smask[r, b] = NEG
                smask[r, 8 + 8 * b:16 + 8 * b] = NEG
    rep = np.tile(np.eye(16, dtype=np.float32), (1, 8))
    blk = np.kron(np.eye(8, dtype=np.float32), np.ones((16, 1), np.float32))
    return dict(c_ident=ident, c_line=line, c_srow=srow, c_smask=smask, c_rep=rep, c_blk=blk)


def decoder_step(nc, A, O):
    f32 = mybir.dt.float32
    f32r = mybir.dt.float32r
    i32 = mybir.dt.int32
    ALU = mybir.AluOpType
    ACT = mybir.ActivationFunctionType
    AX = mybir.AxisListType

    ctx = ExitStack()
    with ctx:
        base = (nc.sbuf_base + 63) // 64 * 64
        at = [base]

        def place(name, shape, dt=f32, offset=None):
            n = int(np.prod(shape[1:])) * 4
            if offset is None:
                offset = at[0]
                at[0] += (n + 31) // 32 * 32
            t = nc.alloc_sbuf_tensor_at(name, list(shape), dt, offset=offset)
            return t, offset

        def keep(name, *shape, dt=f32):
            return place(name, shape, dt)[0]

        x = keep("x", 128, KT, NT)
        o, o_at = place("o", (128, KT, NT))
        h_hi, h_at = place("h_hi", (128, KT, NT), f32r)
        h_lo = keep("h_lo", 128, KT, NT, dt=f32r)
        w_at = at[0]
        w_raw = [keep(f"w_raw{s}", 128, FH, 128) for s in range(2)]
        w_hi = [keep(f"w_hi{s}", 128, FH, 128, dt=f32r) for s in range(2)]
        w_lo = [keep(f"w_lo{s}", 128, FH, 128, dt=f32r) for s in range(2)]
        PT = keep("PT", 128, PT_TILES * 128)
        modT = keep("modT", 128, 4 * len(MODS), NC9)
        ident = keep("ident", 128, 128)
        ones = keep("ones", 128, 128)
        srow = keep("srow", 32, 328)
        smask = keep("smask", 128, 72)
        rep = keep("rep", 16, 128)
        blk = keep("blk", 128, 8)
        tab = keep("tab", 33, 16)
        tabr = keep("tabr", 32, 128)
        tabp = keep("tabp", 33, 16)
        sca = keep("sca", 128, KT, NS)
        scf = keep("scf", 128, 2, 2 * FT, NS)
        up10 = keep("up10", 128, 10, 2 * FT)
        z10 = keep("z10", 128, 10, KT)
        zflag = keep("zflag", 128, 1)
        hemb = keep("hemb", 128, 1)
        pti = keep("pti", 1, 16, dt=i32)
        n_at = at[0]
        rstd = keep("rstd", 128, NT)
        sq = keep("sq", 128, NT)
        sqt = [keep(f"sqt{s}", 128, NT) for s in range(2)]
        nt = [keep(f"nt{s}", 128, NT) for s in range(2)]
        hf = [keep(f"hf{s}", 128, NT) for s in range(2)]
        n_end = at[0]
        ts = keep("ts", 128, KT, NS)
        st = keep("st", 88, 5, 128)
        st_z = keep("st_z", 80, 128)
        z_at = at[0]

        def layer(start):
            pos = [start]

            def put(name, *shape, dt=f32):
                t, off = place(name, shape, dt, pos[0])
                pos[0] += (int(np.prod(shape[1:])) * 4 + 31) // 32 * 32
                assert pos[0] <= nc.sbuf_usable_end, (name, pos[0])
                return t
            put.pos = pos
            return put

        put = layer(z_at)
        act_hi = put("act_hi", 128, FH, NT, dt=f32r)
        act_lo = put("act_lo", 128, FH, NT, dt=f32r)
        ub = [put(f"ub{s}", 128, NT + 2) for s in range(2)]
        yb = [put(f"yb{s}", 128, NT) for s in range(2)]
        sg = put("sg", 128, NT)
        af = put("af", 128, NT)
        mw = {}
        for where, start, count in (("z", z_at, 3), ("h", h_at, 2), ("w", w_at, 2)):
            put = layer(start)
            for s in range(count):
                mw[f"{where}{s}"] = put(f"mw_{where}{s}", 128, KT, 512)
        put = layer(h_at)
        xs = put("xs", 128, 4, D)
        PR = put("PR", 128, PT_TILES, 128)
        line = put("line", 33, 1024)
        lrow = place("lrow", (16, 1024), f32, n_end - 4160)[0]
        put = layer(z_at)
        kT = put("kT", 128, 4, NT)
        kvt = put("kvt", 128, 4, 1536)
        kvs = put("kvs", NS, 1536)
        cb = put("cb", 128, 4, 16, 16)
        sc = put("sc", 128, 4, 16, 16)
        gat = put("gat", 128, 4, 48)
        gts = put("gts", NS, 48)
        gr = put("gr", 128, 3)
        kcT = put("kcT", 128, 2, 80)
        vcp = put("vcp", 16, 256)
        vcs = put("vcs", 64, 256)
        w2b = put("w2b", 128, 2, 128)
        a_at = put.pos[0]
        w1b = put("w1b", 128, 32, 128)
        put = layer(a_at)
        Hb = [put(f"Hb{s}", 128, 512) for s in range(4)]
        qT = [put(f"qT{s}", 128, NT) for s in range(2)]
        qs = put("qs", 128, KT, NS)
        wg_hi = put("wg_hi", 128, KT, 48, dt=f32r)
        wg_lo = put("wg_lo", 128, KT, 48, dt=f32r)
        mx = put("mx", 128, 4)
        nm = put("nm", 128, 4)
        den = put("den", 128, 8)
        cf = put("cf", 128, 4)
        put = layer(n_at)
        Ss = [put(f"Ss{s}", 128, 512) for s in range(2)]
        Pb = [put(f"Pb{s}", 128, 512) for s in range(4)]
        PTb = [put(f"PTb{s}", 128, 512) for s in range(2)]
        assert put.pos[0] <= n_end
        put = layer(n_at + NT * 4)
        hx = put("hx", 128, 2, 80)
        hy = put("hy", 128, 2, 80)
        hz = put("hz", 128, 2, 80)
        per_ = put("per_", 32, 128)
        put = layer(h_at)
        RT = put("RT", 128, 2, 2592)
        pgc = [put(f"pgc{s}", 128, 2, 256) for s in range(4)]
        assert put.pos[0] <= h_at + 2 * KT * NT * 4
        okv = place("okv", (128, KT, NT), f32, o_at)[0]
        wg_raw = place("wg_raw", (128, KT, 48), f32, n_at + 3 * NT * 4)[0]
        line2 = place("line2", (33, 1024), f32, n_end - 4160)[0]
        gT = place("gT", (48, NT), f32, o_at)[0]
        Oacc = place("Oacc", (128, 4, D), f32, o_at)[0]
        put = layer(a_at)
        vblk = put("vblk", 128, 2, 512)
        cm = put("cm", 128, 64)
        cd = put("cd", 128, 64)
        put = layer(n_at)
        pcT = [put(f"pcT{s}", 128, 128) for s in range(2)]
        put = layer(z_at + 16512)
        ld = [put(f"ld{s}", 128, 4, 256) for s in range(2)]
        put = layer(n_at + 1216)
        ksT = put("ksT", 128, 2, 512)
        bias_s = put("bias_s", 128, 328)
        ST = put("ST", 128, 4, 128)
        STn = put("STn", 64, 3, 128)
        Sa = put("Sa", 128, 592)
        assert put.pos[0] <= n_end, (put.pos[0], n_end)
        qb = place("qb", (128, KT), f32, z_at + 8320)[0]
        put = layer(z_at + 8320 + 64)
        pT = put("pT", 128, 4, 128)
        pTn = put("pTn", 64, 3, 128)
        pb = put("pb", 128, 4, 16)
        oS = put("oS", 128, KT, NS)
        oS2 = put("oS2", 128, KT, NS)
        smx = put("smx", 128, 4)
        sden = put("sden", 128, 4)
        scof = put("scf_", 128, 4)
        put = layer(z_at)
        yt = [put(f"yt{s}", 128, D) for s in range(2)]
        yts = put("yts", NS, D)

        pu = [ctx.enter_context(nc.psum_tensor(f"pu{s}", [128, 1024], f32)) for s in range(2)]
        pn = ctx.enter_context(nc.psum_tensor("pn", [128, 1024], f32))
        pm = [ctx.enter_context(nc.psum_tensor(f"pm{s}", [128, 512], f32))[:, :] for s in range(2)]
        prod = [p[:, PSO:PSO + NT] for p in pu]
        pnb = [pn[:, 0:512], pn[:, 512:1024]]

        def mod_places(q):
            k, c, _ = MODS[q]
            if k in (0, 1, 3) and c >= 4:
                out, tr = pm[q % 2], pnb[q % 2]
            else:
                out, tr = pu[q % 2][:, 0:512], pu[q % 2][:, 512:1024]
            row = (nt if k in (0, 2) else hf if k == 4 or c < 4 else sqt)[q % 2][0:NC9, 0:512]
            return out[0:NC9, :], row, tr[:, 0:4 * NC9]

        lines_d = nc.dram_tensor("lines_d", [16, 1024], f32).ap()
        gates_d = nc.dram_tensor("gates_d", [8, 48], f32).ap()

        sems = {}

        def sem(name):
            if name not in sems:
                sems[name] = ctx.enter_context(nc.semaphore(name))
            return sems[name]

        def PTv(row, n):
            return PT[:, row:row + n]

        def site(k):
            b0 = 24 * k
            return modT[:, b0:b0 + 8, :], modT[:, b0 + 8:b0 + 16, :], modT[:, b0 + 16:b0 + 24, :] if k < 4 else None


        def turns(e, count, body, first=False):
            if first:
                body(0, True)
            with e.Fori(1 if first else 0, count) as i:
                body(i, False)

        def hold(e, semaphore, value):
            e.wait_ge(semaphore, value)
            e.sem_inc(S["passed"], 1)

        class Chain:

            def __init__(self, e, s):
                self.e, self.s, self.n, self.off = e, s, 0, 0

            def mark(self, ins):
                ins.then_inc(self.s, 1)
                self.n += 1

            def settle(self):
                self.e.wait_ge(self.s, self.off + self.n)

            def link(self, ins):
                self.mark(ins)
                self.settle()

            def turns(self, count, per, body, first=False):
                if first:
                    body(0, True)
                start = 1 if first else 0
                k0 = self.n
                with self.e.Fori(start, count) as i:
                    self.n, self.off = 0, k0 + (i - start) * per
                    body(i, False)
                    assert self.n == per, (self.n, per)
                self.off, self.n = 0, k0 + (count - start) * per

        names = """passed consts_in tables_in x_in tr_done tr_taken_a tr_taken_v ones_set tab_set prep_done
            lines_out mod_in_z0 mod_in_z1 mod_in_z2 mod_in_h0 mod_in_h1 mod_in_w0 mod_in_w1 mod_done mod_row mod_t mod_kept
            w_landed0 w_landed1 w_hi_ready w_lo_ready unit_done out_taken
            sq_ready sq_added norm_done rs_ready rstd_ready
            t_ready hf_ready hhi_ready hlo_ready x_updated dve_seq pool_seq act_seq
            mix_in_sb z_made mixed mix_hi mix_lo z10_kept ub_zero
            up_in_sb conv_done silu_done af_ready act_hi_done act_lo_done up10_kept
            o_in_sb half_added s_tr s_taken s_out
            kv_in_sb kv_tr kv_tok kv_out pe_in cmpw_in pages_in0 pages_in1 pages_in2 pages_in3
            w1_zero page_tr page_rows rt_rest hid_done hid_act hid_lin hid_tanh cmp_done cmp_kept pe_tr line_in
            cb_done cb_kept gate_w_in wg_hi_s wg_lo_s g_done g_tr g_kept g_sent g_back g_rt
            H_in0 H_in1 H_in2 H_in3 head_used q_in_sb q_kept sc_done sc_kept
            S_done S_biased nm_ready P_ready PT_done PT_kept_a PT_kept_v O_done O_kept
            c_max c_exp c_prob c_tr c_trk vrep_done v_blk c_out c_added
            sk_in0 sk_in1 sk_tr sk_sb qb_set s_sc s_sck sn_done sn_kept sS_tr sS_bias s_exp s_p sP_tr sP_kept
            sv_in0 sv_in1 pb_set sv_done sv_kept sv_all oS_done oT_tr oT_kept oh_ready olo_ready
            y_tr y_kept y_out0 y_out1 ys_out win_out kvp_out""".split()
        S = {n: sem(n) for n in names}

        w_mod = A["mod_w"].rearrange("l s (k p) n -> (l s) p k n", p=128)
        w_kvm = A["kv_mod_w"].rearrange("(k p) n -> p k n", p=128)
        w_ain = A["a_w_in"][0].rearrange("(k p) n -> p k n", p=128)
        w_aout = A["a_w_out"][0].rearrange("(k p) n -> p k n", p=128)
        w_up = A["ffn_w_up"].rearrange("l (k p) n -> l p k n", p=128)
        w_down = A["ffn_w_down"].rearrange("l (h k p) n -> (l h) p k n", p=128, h=2)
        w_kv = A["w_kv"].rearrange("(k p) n -> p k n", p=128)
        w_qg = A["b_w_qg"][0].rearrange("(k p) n -> p k n", p=128)
        w_bout = A["b_w_out"][0].rearrange("(g f p d) n -> f d g p n", g=2, f=2, p=4)

        block = ctx.enter_context(nc.Block())

        def w_wait(e, phase, i, s):
            e.wait_ge(S[f"w_landed{s}"], W0[phase] + WI[phase] * (i + 1))

        WI = {n: {"q": 32, "attn_out": 64}.get(n, 16) for n, _ in UNITS}
        W0, c0 = {}, 0
        for n, c in UNITS:
            W0[n] = c0
            c0 += WI[n] * (c // 2)
        NEXT = {n: m for (n, _), (m, _) in zip(UNITS, UNITS[1:]) if m not in ("q", "attn_out")}
        KOF = {n: FH if n.startswith("down") else KT for n, _ in UNITS}
        valid = [128, 88, 88, 128, 128, 8] + [128] * 12 + [72, 64]

        @block.sync
        def _(sp):
            for t, n in ((ident, "c_ident"), (srow, "c_srow"), (smask, "c_smask"), (rep, "c_rep"), (blk, "c_blk"),
                         (line, "c_line")):
                sp.dma_start(t[:, :], A[n]).then_inc(S["consts_in"], 16)
            sp.dma_start(tab[0:32, :], A["rel_bias"]).then_inc(S["consts_in"], 16)
            sp.dma_start(pti[:, :], A["page_table"].rearrange("a b -> (a b)").unsqueeze(0)).then_inc(S["consts_in"], 16)
            n_tab = 0
            for row, src in ((R_MODB, A["mod_b"].rearrange("l s (t c) -> (l s t) c", c=128)),
                             (96, A["kv_mod_b"].rearrange("(t c) -> t c", c=128)),
                             (R_KVG, A["kv_norm_g"].rearrange("(t c) -> t c", c=128)),
                             (R_ACB, A["a_conv_b"].rearrange("l (t c) -> (l t) c", c=128)),
                             (R_NG, A["norm_g"].rearrange("l s (t c) -> (l s t) c", c=128)),
                             (R_ACW, A["a_conv_w"].rearrange("l j (t c) -> (l j t) c", c=128)),
                             (R_FCB, A["ffn_conv_b"].rearrange("l (t c) -> (l t) c", c=128)),
                             (R_FCW, A["ffn_conv_w"].rearrange("l j (t c) -> (l j t) c", c=128)),
                             (R_STA, A["state_conv_a"].rearrange("l b j (t c) -> (l b j t) c", c=128)),
                             (R_STF, A["state_ffn_conv"].rearrange("l b j (t c) -> (l b j t) c", c=128)),
                             (R_C, A["c_prompt"].rearrange("b (t c) -> (b t) c", c=128)),
                             (R_C + 8, A["c_sample"].rearrange("b (t c) -> (b t) c", c=128)),
                             (R_XS, A["x_sample"].rearrange("b s (t c) -> (b s t) c", c=128))):
                n, k = src.shape[0], 0
                while k < n:
                    t, p = divmod(row + k, 128)
                    full = (n - k) // 128 if p == 0 else 0
                    if full:
                        sp.dma_start(PR[:, t:t + full, :], src[k:k + 128 * full, :].rearrange("(t p) c -> p t c", p=128))\
                          .then_inc(S["tables_in"], 16)
                        k += 128 * full
                    else:
                        m = min(128 - p, n - k)
                        sp.dma_start(PR[p:p + m, t, :], src[k:k + m, :]).then_inc(S["tables_in"], 16)
                        k += m
                    n_tab += 1
            assert n_tab == N_TABLES, n_tab
            sp.dma_start(xs[:, :, :], A["x_prompt"][0].rearrange("(i p) n -> p i n", p=128)).then_inc(S["x_in"], 16)

            def mod_weights(q):
                k, c, where = MODS[q]
                last = [p for p in range(q) if MODS[p][2] == where]
                if last:
                    sp.wait_ge(S["mod_done"], last[-1] + 1)
                src = w_kvm if k == 4 else w_mod[k]
                sp.dma_start(mw[where][:, :, :], src[:, :, 512 * c:512 * c + 512]).then_inc(S[f"mod_in_{where}"], 16)

            for q in range(3):
                mod_weights(q)

            def weights(phase, i, s, src, first=False):
                if not first:
                    hold(sp, S["w_lo_ready"], UBASE[phase] + 2 * i + s - 1)
                k = KOF[phase]
                sp.dma_start(w_raw[s][:, 0:k, :], src).then_inc(S[f"w_landed{s}"], 16)

            def mix_in_w(i, first, units=range(6)):
                for u in units:
                    part = (1, 2, 0)[u % 3]
                    col = part * D + (2 * i + u // 3) * 128
                    if not (first and u < 2):
                        hold(sp, S["w_lo_ready"], 6 * i + u - 1)
                    sp.dma_start(w_raw[u % 2][:, 0:KT, :], w_ain[:, :, bass.ds(col, 128)]).then_inc(S[f"w_landed{u % 2}"], 16)
            mix_in_w(0, True, units=range(2))
            for q in range(3, 6):
                mod_weights(q)
            mix_in_w(0, True, units=range(2, 6))
            with sp.Fori(1, 4) as i:
                mix_in_w(i, False)

            def out_w(phase, view):
                def body(i, first):
                    for s in range(2):
                        weights(phase, i, s, view[:, :, bass.ds(256 * i + 128 * s, 128)])
                turns(sp, 4, body)

            def up_w(phase, l, hh, between=None):
                def body(i, first):
                    for s in range(2):
                        weights(phase, i, s, w_up[l, :, :, bass.ds((hh * FH + i) * 128 + s * FF, 128)])
                body(0, True)
                if between is not None:
                    between()
                with sp.Fori(1, FH) as i:
                    body(i, False)

            def ffn_w(l, between):
                for hh in range(2):
                    up_w(f"up{l}{hh}", l, hh, between if hh == 0 else None)
                    out_w(f"down{l}{hh}", w_down[2 * l + hh])

            out_w("mix_out", w_aout)
            sp.wait_ge(S["unit_done"], UBASE["mix_out"])
            for q in range(6, 8):
                mod_weights(q)

            def mods_ffn0():
                sp.wait_ge(S["unit_done"], UBASE["up00"])
                for q in range(8, 12):
                    mod_weights(q)
            ffn_w(0, mods_ffn0)
            sp.wait_ge(S["unit_done"], UBASE["down01"])
            for q in range(12, 14):
                mod_weights(q)
            for c, slot in enumerate(KV_SLOTS):
                if c == 1:
                    sp.wait_ge(S["unit_done"], UBASE["kv"])
                    for q in range(14, 16):
                        mod_weights(q)
                for s in range(2):
                    weights("kv", c, s, w_kv[:, :, 256 * slot + 128 * s:256 * slot + 128 * s + 128])

            sp.wait_ge(S["unit_done"], UBASE["q"])
            for c in range(2):
                def cached(i, first):
                    for s in range(4):
                        if not (first and c == 0):
                            hold(sp, S["page_tr"], 8 * c + 4 * i + s - 3)
                        for g in range(2):
                            v = sp.value_load(pti[0:1, bass.ds(8 * i + 2 * s + g, 1)], min_val=0, max_val=19)
                            src = A["cache_kv"][bass.ds(v, 1), :, c].rearrange("o p g d -> (o p) (g d)")
                            sp.dma_start(pgc[s][:, g, :], src).then_inc(S[f"pages_in{s}"], 16)
                turns(sp, 2, cached, first=(c == 0))
                if c == 0:
                    sp.wait_ge(S["w1_zero"], 1)
                else:
                    sp.wait_ge(S["hid_done"], 1)
                    sp.wait_ge(S["cmp_done"], 1)
                for f in range(2):
                    sp.dma_start(w1b[64 * f:64 * f + 64, :, 64 * f:64 * f + 64],
                                 A["cmp_w1"][c].rearrange("(r d) n -> d r n", d=64)).then_inc(S["cmpw_in"], 16)
                    sp.dma_start(w2b[64 * f:64 * f + 64, c, 64 * f:64 * f + 64], A["cmp_w2"][c]).then_inc(S["cmpw_in"], 16)
                    sp.dma_start(per_[:, 64 * f:64 * f + 64], A["cmp_pe"][c]).then_inc(S["pe_in"], 16)
                if c == 0:
                    sp.dma_start(line2[:, :], A["c_line"]).then_inc(S["line_in"], 16)
                    sp.dma_start(wg_raw[:, :, :], w_qg[:, :, 1024:1072]).then_inc(S["gate_w_in"], 16)
                for q in ((16, 17), (18, 19, 20, 21))[c]:
                    mod_weights(q)
            sp.wait_ge(S["mod_done"], 22)
            sp.wait_ge(S["lines_out"], 16)
            for gp in range(2):
                def heads(it, first):
                    for u in range(2):
                        hold(sp, S["w_lo_ready"], UBASE["q"] + 4 * gp + 2 * it + u - 1)
                        for f in range(2):
                            col = (8 * gp + 4 * f + 2 * it + u) * 64
                            sp.dma_start(w_raw[u][:, 0:KT, 64 * f:64 * f + 64], w_qg[:, :, bass.ds(col, 64)])\
                              .then_inc(S[f"w_landed{u}"], 16)
                    for u in range(2):
                        for f in range(2):
                            k = 2 * u + f
                            if not (gp == 0 and first):
                                hold(sp, S["head_used"], 8 * gp + 4 * it + k - 3)
                            row = 8 * gp + 4 * f + 2 * it + u
                            src = bass.AP(lines_d.tensor, row * 1024 + 385, [[1, 128], [1, 512]])
                            sp.dma_start(Hb[k][:, :], src).then_inc(S[f"H_in{k}"], 16)
                turns(sp, 2, heads, first=(gp == 0))

            for part, done in (("k", "sk_tr"), ("v", "sv_done")):
                kv = 0 if part == "k" else 1
                if part == "k":
                    sp.wait_ge(S["c_added"], 8)
                    sp.wait_ge(S["kvp_out"], 16 * 4)
                else:
                    sp.wait_ge(S["sk_tr"], 8)

                def cached_rows(i, first):
                    for s in range(2):
                        if not first:
                            hold(sp, S[done], 2 * i + s - 1)
                        for g in range(2):
                            v = sp.value_load(pti[0:1, bass.ds(4 * i + 2 * s + g, 1)], min_val=0, max_val=19)
                            src = A["cache_kv"][bass.ds(v, 1), :, 2 + kv].rearrange("o p g d -> (o p) (g d)")
                            sp.dma_start(ld[s][:, g, :], src).then_inc(S[f"s{part}_in{s}"], 16)
                        src = A["cache_win"][bass.ds(2 * i + s, 1), :, kv].rearrange("o (g p) h d -> (o p) g (h d)", p=128)
                        sp.dma_start(ld[s][:, 2:4, :], src).then_inc(S[f"s{part}_in{s}"], 16)
                turns(sp, 4, cached_rows, first=True)

            def bout(i, first):
                for s in range(2):
                    hold(sp, S["w_lo_ready"], UBASE["attn_out"] + 2 * i + s - 1)
                    for f in range(2):
                        for g in range(2):
                            sp.dma_start(w_raw[s][64 * f:64 * f + 64, 4 * g:4 * g + 4, :],
                                         w_bout[f][:, g, :, bass.ds(256 * i + 128 * s, 128)]).then_inc(S[f"w_landed{s}"], 16)
            turns(sp, 4, bout)
            sp.wait_ge(S["unit_done"], UBASE["attn_out"] + 1)
            for q in range(22, 24):
                mod_weights(q)

            def mods_ffn1():
                sp.wait_ge(S["unit_done"], UBASE["up10"])
                for q in range(24, 28):
                    mod_weights(q)
            ffn_w(1, mods_ffn1)

            for i in range(4):
                hold(sp, S["y_kept"], 2 * i + 2)
                sp.dma_start(O["y_prompt"][0, 128 * i:128 * i + 128, :], yt[i % 2][:, :]).then_inc(S[f"y_out{i % 2}"], 16)
            sp.wait_ge(S["y_kept"], 10)
            sp.dma_start(O["y_sample"].rearrange("b s n -> (b s) n"), yts[:, :]).then_inc(S["ys_out"], 16)
            sp.wait_ge(S["y_out0"], 32)
            sp.wait_ge(S["y_out1"], 32)
            sp.wait_ge(S["ys_out"], 16)

        @block.tensor
        def _(pe):
            mm = nc.tensor.matmul
            banks = [pnb[0], pnb[1], pm[0], pm[1]]
            group = [0]

            def tr_group(tiles):
                t = group[0]
                if t >= 4:
                    pe.wait_ge(S["tr_taken_a" if t % 2 == 0 else "tr_taken_v"], (t - 4) // 2 + 1)
                col = 0
                for src in tiles:
                    k, n = src.shape[0], src.free_size()
                    last = nc.tensor.transpose(banks[t % 4][0:n, col:col + k], src, ident[0:k, 0:k])
                    col += k
                last.then_inc(S["tr_done"], 1)
                group[0] += 1

            pe.wait_ge(S["consts_in"], 16 * 8)
            pe.wait_ge(S["tables_in"], 16 * N_TABLES)
            for g in range(5):
                tr_group([PR[0:valid[t], t, :] for t in range(4 * g, 4 * g + 4)])
            pe.wait_ge(S["x_in"], 16)
            for i in range(4):
                for kk in range(2):
                    tr_group([xs[:, i, 128 * k:128 * k + 128] for k in range(4 * kk, 4 * kk + 4)])
            pe.wait_ge(S["tab_set"], 1)
            for c in range(2):
                t = group[0]
                pe.wait_ge(S["tr_taken_a" if t % 2 == 0 else "tr_taken_v"], (t - 4) // 2 + 1)
                mm(banks[t % 4][0:16, :], tab[:, :], line[:, 512 * c:512 * c + 512], start=True, stop=True)\
                    .then_inc(S["tr_done"], 1)
                group[0] += 1

            def norm_sum(m):
                pe.wait_ge(S["sq_added"], 8 * (m + 1))
                if m == 0:
                    pe.wait_ge(S["ones_set"], 1)
                for hh in range(2):
                    last = mm(pn[:, PSO + HALF * hh:PSO + HALF * (hh + 1)], ones[:, :], sq[:, HALF * hh:HALF * (hh + 1)],
                              start=True, stop=True)
                last.then_inc(S["norm_done"], 1)

            def mod_product(q):
                where = MODS[q][2]
                use = sum(1 for m in MODS[:q] if m[2] == where)
                pe.wait_ge(S[f"mod_in_{where}"], 16 * (use + 1))
                if q >= 2:
                    pe.wait_ge(S["mod_row"], q - 1)
                for k in range(KT):
                    last = mm(mod_places(q)[0], PT[:, R_C + k:R_C + 72:8], mw[where][:, k, :], start=(k == 0), stop=(k == KT - 1))
                last.then_inc(S["mod_done"], 1)

            def mod_transpose(q):
                row, tr = mod_places(q)[1:]
                pe.wait_ge(S["mod_row"], q + 1)
                if q >= 2:
                    pe.wait_ge(S["mod_kept"], q - 1)
                for t in range(4):
                    last = nc.tensor.transpose(tr[:, NC9 * t:NC9 * t + NC9], row[:, 128 * t:128 * t + 128],
                                               ident[0:NC9, 0:NC9])
                last.then_inc(S["mod_t"], 1)

            def mod_pair(q):
                for step in (mod_product, mod_transpose):
                    step(q)
                    step(q + 1)

            def mod_boundary(q, m, extra=None):
                mod_product(q)
                norm_sum(m)
                if extra is not None:
                    extra()
                for r in range(q + 1, q + 4):
                    mod_product(r)
                    mod_transpose(r - 1)
                norm_sum(m + 1)
                mod_transpose(q + 3)

            pe.wait_ge(S["tr_taken_a"], 8)
            pe.wait_ge(S["tr_taken_v"], 7)
            mod_pair(0)
            norm_sum(0)
            mod_pair(2)

            def unit(phase, i, s, hi, lo, slot=None, waits=()):
                n = UBASE[phase] + 2 * i + s
                pe.wait_ge(S["w_lo_ready"], n + 1)
                if slot is None:
                    slot = s
                    if not (isinstance(n, int) and n < 2):
                        pe.wait_ge(S["out_taken"], n - 1)
                else:
                    pe.wait_ge(S["out_taken"], n)
                kk = KOF[phase]
                for k in range(kk):
                    for name, value in waits:
                        pe.wait_ge(S[name], value + k)
                    for w, hs in ((w_hi[s], (hi, lo)), (w_lo[s], (hi,))):
                        for h in hs:
                            for c in range(2):
                                last = mm(pu[slot][:, PSO + HALF * c:PSO + HALF * (c + 1)], w[:, k, :],
                                          h[:, k, HALF * c:HALF * (c + 1)],
                                          start=(k == 0 and w is w_hi[s] and h is hi),
                                          stop=(k == kk - 1 and w is w_lo[s]))
                last.then_inc(S["unit_done"], 1)

            def phase(name, hi, lo, waits=(), extra=None):
                def body(i, first):
                    for u in range(2):
                        unit(name, i, u, hi, lo, waits=waits if first and u == 0 else ())
                    if first and extra is not None:
                        extra()
                turns(pe, dict(UNITS)[name] // 2, body, first=True)

            def ffn(l, q):
                gates = MOD_AT[2 * l + 1] + 4
                pe.wait_ge(S["rs_ready"], 4 * l + 3)
                mod_product(gates)
                mod_product(gates + 1)

                def gate_transposes():
                    mod_transpose(gates)
                    mod_transpose(gates + 1)
                for hh in range(2):
                    if hh == 0:
                        phase(f"up{l}0", h_hi, h_lo, waits=[("hlo_ready", 9 * q + 2)], extra=gate_transposes)
                    else:
                        phase(f"up{l}1", h_hi, h_lo)
                    phase(f"down{l}{hh}", act_hi, act_lo, waits=[("act_lo_done", FH * (2 * l + hh) + 1)])

            def kept_rows(p):
                pe.wait_ge(S["up10_kept"], 44 * (p + 1))
                for k in range(5):
                    bank = pm[0] if k < 4 else pm[1]
                    last = nc.tensor.transpose(bank[0:88, 128 * (k % 4):128 * (k % 4) + 128],
                                               up10[:, 2 * k:2 * k + 2, :].rearrange("p a b -> p (a b)"), ident[:, :])
                last.then_inc(S["s_tr"], 1)

            def mix_in(i, first):
                for u in range(6):
                    unit("mix_in", 3 * i + u // 2, u % 2, h_hi, h_lo, waits=[("hlo_ready", 2)] if first and u == 0 else ())
                    if first and u == 2:
                        mod_pair(4)
            turns(pe, 4, mix_in, first=True)
            phase("mix_out", act_hi, act_lo, waits=[("mix_lo", 1)])
            pe.wait_ge(S["out_taken"], UBASE["up00"])
            pe.wait_ge(S["z10_kept"], KT)
            nc.tensor.transpose(pm[0][0:80, 0:128], z10[:, :, :].rearrange("p a b -> p (a b)"), ident[:, :])\
                .then_inc(S["s_tr"], 1)
            mod_boundary(6, 1)
            ffn(0, 1)
            pe.wait_ge(S["out_taken"], UBASE["kv"])

            def first_kept_rows():
                pe.wait_ge(S["s_taken"], 1)
                kept_rows(0)
            mod_boundary(12, 3, extra=first_kept_rows)
            phase("kv", h_hi, h_lo, waits=[("hlo_ready", 9 * 2 + 2)])

            pe.wait_ge(S["out_taken"], UBASE["q"])
            pe.wait_ge(S["s_taken"], 2)
            tiles = [okv[:, m, :] for m in range(8)] + [kT[:, m, :] for m in range(4)]
            ordered = [tiles[2 * KV_SLOTS.index(sl) + g] for sl in range(6) for g in range(2)]
            for s3 in range(3):
                for i in range(4):
                    tr_group([ordered[4 * s3 + k][:, 128 * i:128 * i + 128] for k in range(4)])
            for s3 in range(3):
                t = group[0]
                pe.wait_ge(S["tr_taken_a" if t % 2 == 0 else "tr_taken_v"], (t - 4) // 2 + 1)
                for k in range(4):
                    last = nc.tensor.transpose(banks[t % 4][0:NS, 128 * k:128 * k + 128], ordered[4 * s3 + k][:, NP:NT],
                                               ident[:, :])
                last.then_inc(S["tr_done"], 1)
                group[0] += 1
            pe.wait_ge(S["tr_taken_a"], 15)
            pe.wait_ge(S["tr_taken_v"], 15)

            def cached_pages(c):
                def page(i, first):
                    for s in range(4):
                        n = 8 * c + 4 * i + s
                        pe.wait_ge(S[f"pages_in{s}"], 64 * c + 32 * (i + 1))
                        if not (c == 0 and first and s < 2):
                            pe.wait_ge(S["page_rows"], n - 1)
                        for gp in range(2):
                            for g in range(2):
                                last = nc.tensor.transpose(pm[s % 2][:, 256 * gp + 128 * g:256 * gp + 128 * g + 128],
                                                           pgc[s][:, g, 128 * gp:128 * gp + 128], ident[:, :])
                        last.then_inc(S["page_tr"], 1)
                turns(pe, 2, page, first=(c == 0))

            def hidden(c):
                pe.wait_ge(S["pe_in"], 32 * (c + 1))
                if c == 1:
                    pe.wait_ge(S["cmp_kept"], 1)
                nc.tensor.transpose(pnb[1][:, 0:32], per_[:, :], ident[0:32, 0:32]).then_inc(S["pe_tr"], 1)
                pe.wait_ge(S["cmpw_in"], 64 * (c + 1))
                pe.wait_ge(S["rt_rest"], 3 * (c + 1))
                pe.wait_ge(S["page_rows"], 8 * (c + 1))
                for r in range(32):
                    last = mm(pn[:, 0:162], w1b[:, r, :], RT[:, :, r:2592:32], start=(r == 0), stop=(r == 31))
                last.then_inc(S["hid_done"], 1)

            cached_pages(0)
            hidden(0)
            pe.wait_ge(S["line_in"], 16)
            for r in range(28):
                x0 = 32 * (r - 15) + 481
                last = mm(pm[0][:, 16 * r:16 * r + 16], line2[:, x0:x0 + 128], tabp[:, :], start=True, stop=True)
            last.then_inc(S["cb_done"], 1)
            pe.wait_ge(S["hid_act"], 1)
            mm(pnb[1][:, 0:160], w2b[:, 0, :], hx[:, :, :], start=True, stop=True).then_inc(S["cmp_done"], 1)
            mod_pair(16)
            pe.wait_ge(S["cb_kept"], 1)
            cached_pages(1)
            hidden(1)
            mod_product(18)
            pe.wait_ge(S["hid_act"], 2)
            for gp in range(2):
                mm(pnb[1][0:16, 128 * gp:128 * gp + 128], hx[:, gp, 0:16], w2b[:, 1, :], start=True, stop=True)
                last = mm(pnb[0][0:64, 128 * gp:128 * gp + 128], hx[:, gp, 16:80], w2b[:, 1, :], start=True, stop=True)
            last.then_inc(S["cmp_done"], 1)
            mod_transpose(18)
            mod_product(19)
            mod_transpose(19)
            mod_pair(20)
            pe.wait_ge(S["cmp_kept"], 2)

            pe.wait_ge(S["hlo_ready"], 9 * 4)
            pe.wait_ge(S["wg_lo_s"], 1)
            pe.wait_ge(S["mod_kept"], 22)
            for k in range(KT):
                for w, hs in ((wg_hi, (h_hi, h_lo)), (wg_lo, (h_hi,))):
                    for h in hs:
                        for c in range(2):
                            last = mm(pu[1][0:48, PSO + HALF * c:PSO + HALF * (c + 1)], w[:, k, :],
                                      h[:, k, HALF * c:HALF * (c + 1)], start=(k == 0 and w is wg_hi and h is h_hi),
                                      stop=(k == KT - 1 and w is wg_lo))
            last.then_inc(S["g_done"], 1)

            for gp in range(2):
                def heads(it, first):
                    T = 2 * gp + it
                    for u in range(2):
                        unit("q", T, u, h_hi, h_lo, slot=0)
                    if gp == 0 and first:
                        pe.wait_ge(S["g_rt"], 1)
                        for i in range(4):
                            last = nc.tensor.transpose(pm[0][:, 48 * i:48 * i + 48], gT[:, 128 * i:128 * i + 128],
                                                       ident[0:48, 0:48])
                        last = nc.tensor.transpose(pm[0][0:NS, 192:240], gT[:, NP:NT], ident[0:48, 0:48])
                        last.then_inc(S["g_tr"], 1)
                        pe.wait_ge(S["g_kept"], 3)

                    def scores(step):
                        u, item = S_ITEMS[step]
                        nS = NSI * T + step
                        if item is None or S_ITEMS[step - 1][1] is None:
                            pe.wait_ge(S["q_in_sb"], 2 * T + u + 1)
                        if not (gp == 0 and first and step < 2):
                            pe.wait_ge(S["S_biased"], nS - 1)
                        if item is None:
                            f = step % 2
                            for i in range(4):
                                last = mm(pnb[f][:, 16 * i:16 * i + 16], qT[u][64 * f:64 * f + 64, 128 * i:128 * i + 128],
                                          kcT[64 * f:64 * f + 64, gp, 0:16], start=True, stop=True)
                        else:
                            _, f, br, i = item
                            W = 128 * (i + 1)
                            last = mm(pnb[step % 2][:, 0:W], qT[u][64 * f:64 * f + 64, 128 * i:128 * i + 128],
                                      kT[64 * f:64 * f + 64, 2 * br + gp, 0:W], start=True, stop=True)
                        last.then_inc(S["S_done"], 1)

                    def flip(step):
                        _, item = S_ITEMS[step]
                        m, f, br, i = item
                        pe.wait_ge(S["P_ready"], 32 * T + m + 1)
                        if not (gp == 0 and first and m < 2):
                            pe.wait_ge(S["PT_kept_a" if m % 2 == 0 else "PT_kept_v"], 16 * T + m // 2)
                        for j in range(i + 1):
                            last = nc.tensor.transpose(pm[m % 2][:, 128 * j:128 * j + 128],
                                                       Pb[m % 4][:, 128 * j:128 * j + 128], ident[:, :])
                        last.then_inc(S["PT_done"], 1)

                    def weigh(step):
                        _, item = S_ITEMS[step]
                        m, f, br, i = item
                        pe.wait_ge(S["PT_kept_a" if m % 2 == 0 else "PT_kept_v"], 16 * T + m // 2 + 1)
                        if not (gp == 0 and first and m < 2):
                            pe.wait_ge(S["O_kept"], 32 * T + m - 1)
                        col = (3 if br == 0 else 5) * 256 + (2 * gp + f) * 64
                        for j in range(i + 1):
                            last = mm(pu[1][:, 512 * (m % 2):512 * (m % 2) + 64], PTb[m % 2][:, 128 * j:128 * j + 128],
                                      kvt[:, j, col:col + 64], start=(j == 0), stop=(j == i))
                        last.then_inc(S["O_done"], 1)

                    for step in range(len(S_ITEMS) + 3):
                        if step < len(S_ITEMS):
                            scores(step)
                        if 0 <= step - 2 < len(S_ITEMS) and S_ITEMS[step - 2][1] is not None:
                            flip(step - 2)
                        if 0 <= step - 3 < len(S_ITEMS) and S_ITEMS[step - 3][1] is not None:
                            weigh(step - 3)
                turns(pe, 2, heads, first=(gp == 0))
            pe.wait_ge(S["O_kept"], 128)
            pe.wait_ge(S["PT_kept_a"], 64)
            pe.wait_ge(S["PT_kept_v"], 64)

            for gp in range(2):
                mm(pm[gp][:, 0:128], rep[:, :], vcp[:, 128 * gp:128 * gp + 128], start=True, stop=True)\
                    .then_inc(S["vrep_done"], 1)
            pe.wait_ge(S["c_prob"], 1)
            pe.wait_ge(S["v_blk"], 2)
            for n in range(9):
                if n < 8:
                    i, gp = divmod(n, 2)
                    if n >= 2:
                        pe.wait_ge(S["c_trk"], n - 1)
                    nc.tensor.transpose(pm[n % 2][:, 0:128], sc[:, i, 8 * gp:8 * gp + 8, :].rearrange("p e n -> p (e n)"),
                                        ident[:, :]).then_inc(S["c_tr"], 1)
                if n >= 1:
                    k = n - 1
                    pe.wait_ge(S["c_trk"], k + 1)
                    if k >= 2:
                        pe.wait_ge(S["c_added"], k - 1)
                    mm(pnb[k % 2][:, :], pcT[k % 2][:, :], vblk[:, k % 2, :], start=True, stop=True)\
                        .then_inc(S["c_out"], 1)

            def sample_keys(i, first):
                for s in range(2):
                    b = 2 * i + s
                    pe.wait_ge(S[f"sk_in{s}"], 48 * (i + 1))
                    if not (first and s == 0):
                        pe.wait_ge(S["sk_sb"], 2 * b)
                    for gp in range(2):
                        for j in range(4):
                            last = nc.tensor.transpose(pm[gp][:, 128 * j:128 * j + 128],
                                                       ld[s][:, j, 128 * gp:128 * gp + 128], ident[:, :])
                    last.then_inc(S["sk_tr"], 1)
                    pe.wait_ge(S["sk_sb"], 2 * b + 2)
                    pe.wait_ge(S["qb_set"], b + 1)
                    if not (first and s == 0):
                        pe.wait_ge(S["s_sck"], b)
                    for g in range(4):
                        gp, f = divmod(g, 2)
                        for j in range(4):
                            last = mm(pnb[f][:, 8 * j + 4 * gp:8 * j + 4 * gp + 4],
                                      ksT[64 * f:64 * f + 64, gp, 128 * j:128 * j + 128],
                                      qb[64 * f:64 * f + 64, 4 * gp:4 * gp + 4], start=True, stop=True)
                    last.then_inc(S["s_sc"], 1)
            pe.wait_ge(S["c_added"], 8)
            pe.wait_ge(S["c_trk"], 8)
            turns(pe, 4, sample_keys, first=True)
            pe.wait_ge(S["s_sck"], 8)
            pe.wait_ge(S["sk_sb"], 16)
            for g in range(4):
                gp, f = divmod(g, 2)
                rhs = qs[64 * f:64 * f + 64, 4 * gp:4 * gp + 4, :]
                bank = (pm[0], pnb[1])[f]
                for br in range(2):
                    mm(bank[0:8, 64 * br + 32 * gp:64 * br + 32 * gp + 32], kT[64 * f:64 * f + 64, 2 * br + gp, NP:NT], rhs,
                       start=True, stop=True)
                last = mm(bank[0:64, 128 + 32 * gp:128 + 32 * gp + 32], kcT[64 * f:64 * f + 64, gp, 16:80], rhs,
                          start=True, stop=True)
            mm(pnb[0][:, 0:328], tabr[:, :], srow[:, :], start=True, stop=True).then_inc(S["sn_done"], 1)
            pe.wait_ge(S["sn_kept"], 3)
            for j in range(4):
                nc.tensor.transpose(pm[1][:, 128 * j:128 * j + 128], ST[:, j, :], ident[:, :])
            for br in range(2):
                nc.tensor.transpose(pnb[1][:, 8 * br:8 * br + 8], STn[0:8, br, :], ident[0:8, 0:8])
            nc.tensor.transpose(pnb[1][:, 16:80], STn[0:64, 2, :], ident[0:64, 0:64]).then_inc(S["sS_tr"], 1)
            pe.wait_ge(S["s_p"], 1)
            for j, c0 in enumerate((0, 128, 264, 392)):
                nc.tensor.transpose(pm[0][:, 128 * j:128 * j + 128], Sa[:, c0:c0 + 128], ident[:, :])
            for j, c0 in enumerate((256, 520)):
                nc.tensor.transpose(pm[1][0:8, 128 * j:128 * j + 128], Sa[:, c0:c0 + 8], ident[:, :])
            nc.tensor.transpose(pm[1][0:64, 256:384], Sa[:, 528:592], ident[:, :]).then_inc(S["sP_tr"], 1)
            pe.wait_ge(S["sP_kept"], 3)

            def sample_values(i, first):
                for s in range(2):
                    b = 2 * i + s
                    pe.wait_ge(S[f"sv_in{s}"], 48 * (i + 1))
                    pe.wait_ge(S["pb_set"], b + 1)
                    if not (first and s == 0):
                        pe.wait_ge(S["sv_kept"], b)
                    for g in range(4):
                        gp, f = divmod(g, 2)
                        for j in range(4):
                            last = mm(pnb[0][64 * f:64 * f + 64, 4 * gp:4 * gp + 4], ld[s][:, j, 64 * g:64 * g + 64],
                                      pb[:, j, 4 * g:4 * g + 4], start=(j == 0), stop=(j == 3))
                    last.then_inc(S["sv_done"], 1)
            turns(pe, 4, sample_values, first=True)
            for g in range(4):
                gp, f = divmod(g, 2)
                out = pm[1][64 * f:64 * f + 64, 32 * gp:32 * gp + 32]
                mm(out, kvs[:, 768 + 64 * g:768 + 64 * g + 64], pTn[0:8, 0, 32 * g:32 * g + 32], start=True, stop=False)
                mm(out, kvs[:, 1280 + 64 * g:1280 + 64 * g + 64], pTn[0:8, 1, 32 * g:32 * g + 32], start=False, stop=False)
                last = mm(out, vcs[:, 64 * g:64 * g + 64], pTn[0:64, 2, 32 * g:32 * g + 32], start=False, stop=True)
            last.then_inc(S["sv_all"], 1)

            for n in range(8):
                i, kk = divmod(n, 2)
                if n >= 2:
                    pe.wait_ge(S["olo_ready"], n - 1)
                bank = (pm[0], pnb[1])[n % 2]
                for t in range(4):
                    last = nc.tensor.transpose(bank[:, 128 * t:128 * t + 128],
                                               Oacc[:, i, 512 * kk + 128 * t:512 * kk + 128 * t + 128], ident[:, :])
                last.then_inc(S["oT_tr"], 1)
            pe.wait_ge(S["olo_ready"], 9)
            phase("attn_out", h_hi, h_lo)
            pe.wait_ge(S["out_taken"], UBASE["up10"])
            mod_boundary(22, 5)
            ffn(1, 4)
            norm_sum(7)
            kept_rows(1)
            pe.wait_ge(S["s_taken"], 3)
            pe.wait_ge(S["x_updated"], 9 * 4)
            for n in range(10):
                if n >= 4:
                    pe.wait_ge(S["y_kept"], n - 3)
                for k in range(4):
                    kk = 4 * (n % 2) + k
                    if n < 8:
                        i = n // 2
                        last = nc.tensor.transpose(banks[n % 4][:, 128 * k:128 * k + 128],
                                                   x[:, kk, 128 * i:128 * i + 128], ident[:, :])
                    else:
                        last = nc.tensor.transpose(banks[n % 4][0:NS, 128 * k:128 * k + 128], x[:, kk, NP:NT], ident[:, :])
                last.then_inc(S["y_tr"], 1)

        @block.scalar
        def _(act):
            fn = nc.scalar.activation
            banks = [pnb[0], pnb[1], pm[0], pm[1]]
            ch = Chain(act, S["act_seq"])

            def split_hi(phase, i, s, first=False):
                w_wait(act, phase, i, s)
                if not first:
                    act.wait_ge(S["unit_done"], UBASE[phase] + 2 * i + s - 1)
                k = KOF[phase]
                fn(w_hi[s][:, 0:k, :], w_raw[s][:, 0:k, :], ACT.Copy).then_inc(S["w_hi_ready"], 1)

            def rows(first, last):
                for q in range(first, last):
                    out, row, _ = mod_places(q)
                    act.wait_ge(S["mod_done"], q + 1)
                    if q >= 2:
                        act.wait_ge(S["mod_t"], q - 1)
                    fn(row, out, ACT.Copy).then_inc(S["mod_row"], 1)

            def squares(m, tiles, waits, between={}):
                for k in range(KT):
                    for name, value in waits(k):
                        act.wait_ge(S[name], value)
                    if 8 * m + k >= 2:
                        act.wait_ge(S["sq_added"], 8 * m + k - 1)
                    fn(sqt[k % 2][:, :], tiles[:, k, :], ACT.Square).then_inc(S["sq_ready"], 1)
                    if k in between:
                        rows(between[k], between[k] + 1)

            def root(m):
                act.wait_ge(S["rs_ready"], m + 1)
                fn(rstd[:, :], rstd[:, :], ACT.Sqrt).then_inc(S["rstd_ready"], 1)

            def affine(q, scale, shift, gates=None):
                for k in range(KT):
                    act.wait_ge(S["t_ready"], 8 * q + k + 1)
                    if 8 * q + k >= 2:
                        act.wait_ge(S["hlo_ready"], 9 * ((8 * q + k - 2) // 8) + (8 * q + k - 2) % 8 + 2)
                    fn(hf[k % 2][:, 0:NP], nt[k % 2][:, 0:NP], ACT.Identity, bias=shift[:, k, 0:1], scale=scale[:, k, 0:1])\
                        .then_inc(S["hf_ready"], 1)
                    if gates is not None and k in (4, 7):
                        rows(gates + k // 7, gates + k // 7 + 1)

            for t in range(0, 13, 2):
                act.wait_ge(S["tr_done"], t + 1)
                bank = banks[t % 4]
                if t < 5:
                    col = 0
                    for tile in range(4 * t, 4 * t + 4):
                        n = valid[tile]
                        last = fn(PT[:, 128 * tile:128 * tile + n], bank[:, col:col + n], ACT.Copy)
                        col += n
                else:
                    i, kk = divmod(t - 5, 2)
                    last = fn(x[:, 4 * kk:4 * kk + 4, 128 * i:128 * i + 128], bank.rearrange("p (k c) -> p k c", k=4), ACT.Copy)
                last.then_inc(S["tr_taken_a"], 1)
            act.wait_ge(S["tr_done"], 15)
            fn(lrow[:, 512:1024], banks[2][0:16, :], ACT.Copy).then_inc(S["tr_taken_a"], 1)
            act.wait_ge(S["tr_taken_a"], 8)
            act.wait_ge(S["tr_taken_v"], 7)
            act.dma_start(lines_d, lrow[:, :]).then_inc(S["lines_out"], 16)
            squares(0, x, lambda k: [("prep_done", 1)] if k == 0 else [])

            rows(0, 2)
            root(0)
            rows(2, 4)
            act.wait_ge(S["lines_out"], 16)
            split_hi("mix_in", 0, 0, first=True)
            split_hi("mix_in", 0, 1, first=True)
            sh, s_, _ = site(0)
            affine(0, s_, sh)

            def mix_in(i, first, last_turn=False):
                for u in range(6):
                    j, part = 2 * i + u // 3, u % 3
                    n = 6 * i + u
                    act.wait_ge(S["unit_done"], n + 1)
                    if not (first and u < 3):
                        act.wait_ge(S["z_made" if part < 2 else "mixed"], j)
                    fn((sg, yb[0], af)[part][:, :], prod[u % 2], ACT.Copy).then_inc(S["out_taken"], 1)
                    if first and u == 2:
                        rows(4, 6)
                    if part == 2:
                        hold(act, S["mixed"], j + 1)
                        fn(act_hi[:, bass.ds(j, 1), :].rearrange("p o n -> p (o n)"), hf[0][:, :], ACT.Copy).then_inc(S["mix_hi"], 1)
                    if not last_turn or u < 4:
                        split_next(i, u)
                    else:
                        split_hi("mix_out", 0, u % 2)

            def split_next(i, u):
                s = u % 2
                k = 3 * i + u // 2 + 1
                w_wait(act, "mix_in", k, s)
                act.wait_ge(S["unit_done"], 2 * k + s - 1)
                fn(w_hi[s][:, 0:KT, :], w_raw[s][:, 0:KT, :], ACT.Copy).then_inc(S["w_hi_ready"], 1)
            act.wait_ge(S["hlo_ready"], 9)
            mix_in(0, True)
            for b in range(NS):
                act.dma_start(O["new_win_sample"][b, 0:PAST - 1].rearrange("t a g d -> t (a g d)"),
                              A["cache_win"][b, 1:PAST].rearrange("t a g d -> t (a g d)")).then_inc(S["win_out"], 16)
            for l in range(2):
                act.dma_start(O["new_ffn_conv_sample"][l, :, 0, :], A["state_ffn_conv"][l, :, 1, :]).then_inc(S["win_out"], 16)
            act.dma_start(O["new_conv_a_sample"][0, :, 0, :], A["state_conv_a"][0, :, 1, :]).then_inc(S["win_out"], 16)
            with act.Fori(1, 3) as i:
                mix_in(i, False)
            mix_in(3, False, last_turn=True)

            def out_phase(name, m, second=False, halves=0):
                if name == "attn_out":
                    split_hi(name, 0, 0)
                    split_hi(name, 0, 1)

                def body(i, first, last_turn=False):
                    for s in range(2):
                        n, k = UBASE[name] + 2 * i + s, 2 * i + s
                        act.wait_ge(S["unit_done"], n + 1)
                        if second:
                            act.wait_ge(S["half_added"], 8 * halves + k)
                            fn(nt[0][:, :], prod[s], ACT.Copy).then_inc(S["out_taken"], 1)
                        else:
                            act.sem_inc(S["passed"], 1)
                            fn(o[:, bass.ds(k, 1), :].rearrange("p a n -> p (a n)"), prod[s], ACT.Copy).then_inc(S["out_taken"], 1)
                        if not last_turn:
                            split_hi(name, i + 1, s)
                        elif name in NEXT:
                            split_hi(NEXT[name], 0, s)
                        if m is not None:
                            act.wait_ge(S["sq_added"], 8 * m + k - 1)
                            if second:
                                hold(act, S["half_added"], 8 * halves + k + 1)
                            else:
                                hold(act, S["out_taken"], n + 1)
                            fn(sqt[s][:, :], o[:, bass.ds(k, 1), :].rearrange("p a n -> p (a n)"), ACT.Square)\
                                .then_inc(S["sq_ready"], 1)
                body(0, True)
                with act.Fori(1, 3) as i:
                    body(i, False)
                body(3, False, last_turn=True)

            def up_phase(name, half):

                def body(i, first, last_turn=False):
                    for s in range(2):
                        n = UBASE[name] + 2 * i + s
                        act.wait_ge(S["unit_done"], n + 1)
                        if not (half == 0 and first):
                            act.wait_ge(S["conv_done"], 2 * (FH * half + i) - 1 + s)
                            act.wait_ge(S["up10_kept"], 2 * (FH * half + i) - 1 + s)
                        elif half == 0:
                            act.wait_ge(S["ub_zero"], 1)
                        fn(ub[s][:, 2:2 + NT], prod[s], ACT.Copy).then_inc(S["out_taken"], 1)
                        if not last_turn:
                            split_hi(name, i + 1, s)
                        else:
                            split_hi(NEXT[name], 0, s)
                    j = FH * half + i
                    act.wait_ge(S["conv_done"], 2 * j + 2)
                    fn(sg[:, :], yb[1][:, :], ACT.Silu).then_inc(S["silu_done"], 1)
                    hold(act, S["af_ready"], j + 1)
                    fn(act_hi[:, bass.ds(i, 1), :].rearrange("p o n -> p (o n)"), af[:, :], ACT.Copy)\
                        .then_inc(S["act_hi_done"], 1)
                body(0, True)
                with act.Fori(1, FH - 1) as i:
                    body(i, False)
                body(FH - 1, False, last_turn=True)

            def ffn(l, q):
                sh, s_, _ = site(2 * l + 1)
                affine(q, s_, sh, gates=MOD_AT[2 * l + 1] + 4)
                if l == 1:
                    act.wait_ge(S["ub_zero"], 2)
                up_phase(f"up{l}0", 2 * l)
                out_phase(f"down{l}0", None)
                up_phase(f"up{l}1", 2 * l + 1)
                out_phase(f"down{l}1", 4 * l + 3, second=True, halves=l)

            def history_out(l):
                act.wait_ge(S["s_tr"], 2 + l)
                if l == 1:
                    act.wait_ge(S["s_out"], 16 * 5)
                fn(st[:, 0:4, :], pm[0][0:88, :].rearrange("p (a c) -> p a c", a=4), ACT.Copy)
                fn(st[:, 4, :], pm[1][0:88, 0:128], ACT.Copy).then_inc(S["s_taken"], 1)
                act.wait_ge(S["s_taken"], 2 + l)
                act.dma_start(O["new_ffn_conv_prompt"][l, 0].rearrange("j (t c) -> (j t) c", c=128), st[:, 0, :])\
                   .then_inc(S["s_out"], 16)
                for f in range(2):
                    dst = O["new_ffn_conv_sample"][l, :, 1, :].rearrange("(a f) (t c) -> f t a c", f=2, c=128)
                    act.dma_start(dst[f], st[44 * f:44 * f + 44, 1:5, :]).then_inc(S["s_out"], 16)

            out_phase("mix_out", 1)
            act.wait_ge(S["s_tr"], 1)
            fn(st_z[:, :], pm[0][0:80, 0:128], ACT.Copy).then_inc(S["s_taken"], 1)
            act.wait_ge(S["s_taken"], 1)
            act.dma_start(O["new_conv_a_prompt"][0, 0].rearrange("j (t c) -> (j t) c", c=128), st_z[0:16, :])\
               .then_inc(S["s_out"], 16)
            act.dma_start(O["new_conv_a_sample"][0, :, 1, :].rearrange("b (t c) -> b t c", c=128), st_z[16:80, :])\
               .then_inc(S["s_out"], 16)
            rows(6, 7)
            root(1)
            squares(2, x, lambda k: [("x_updated", k + 2)], between={1: 7, 6: 8})
            rows(9, 10)
            root(2)
            ffn(0, 1)
            rows(12, 13)
            root(3)
            history_out(0)
            squares(4, x, lambda k: [("x_updated", 9 + k + 2)], between={1: 13, 6: 14})
            rows(15, 16)
            root(4)

            sh, s_, _ = site(4)
            affine(2, s_, sh)
            for c in range(6):
                for s in range(2):
                    m = 2 * c + s
                    act.wait_ge(S["unit_done"], UBASE["kv"] + m + 1)
                    dst = okv[:, m, :] if m < 8 else kT[:, m - 8, :]
                    if m == 8:
                        act.wait_ge(S["hlo_ready"], 27)
                    fn(dst, prod[s], ACT.Copy).then_inc(S["out_taken"], 1)
                    if c < 5:
                        split_hi("kv", c + 1, s)
            for n in range(15):
                t = 15 + n
                if t % 2:
                    continue
                act.wait_ge(S["tr_done"], t + 1)
                if n < 12:
                    dst, src = kvt[:, n % 4, 512 * (n // 4):512 * (n // 4) + 512], banks[t % 4]
                else:
                    dst, src = kvs[:, 512 * (n - 12):512 * (n - 12) + 512], banks[t % 4][0:NS, :]
                fn(dst, src, ACT.Copy).then_inc(S["tr_taken_a"], 1)
            act.wait_ge(S["tr_taken_a"], 15)
            act.wait_ge(S["tr_taken_v"], 15)
            act.dma_start(O["new_kv_prompt"][0].rearrange("(i p) s g d -> p i (s g d)", p=128), kvt[:, :, 0:1024])\
               .then_inc(S["kvp_out"], 16)
            act.dma_start(O["new_win_prompt"][0].rearrange("(i p) s g d -> p i (s g d)", p=128), kvt[:, :, 1024:1536])\
               .then_inc(S["kvp_out"], 16)
            act.dma_start(O["new_kv_sample"].rearrange("b o s g d -> (b o) (s g d)"), kvs[:, 0:1024]).then_inc(S["kvp_out"], 16)
            act.dma_start(O["new_win_sample"][:, PAST - 1].rearrange("b s g d -> b (s g d)"), kvs[:, 1024:1536])\
               .then_inc(S["kvp_out"], 16)

            for c in range(2):
                def page_rows(i, first):
                    for s in range(2):
                        hold(act, S["page_tr"], 8 * c + 2 * i + s + 1)
                        fn(RT[:, :, bass.ds(NP + 512 * i + 256 * s, 256)], pm[s][:, :].rearrange("p (g n) -> p g n", g=2),
                           ACT.Copy).then_inc(S["page_rows"], 1)
                if c == 1:
                    act.wait_ge(S["hid_done"], 1)
                turns(act, 4, page_rows)
                act.wait_ge(S["pe_tr"], c + 1)
                for g in range(2):
                    last = fn(RT[:, g, 2560:2592], pnb[1][:, 0:32], ACT.Copy)
                last.then_inc(S["rt_rest"], 1)
                act.wait_ge(S["hid_lin"], c + 1)
                fn(hz[:, :, :], hy[:, :, :], ACT.Tanh, scale=math.sqrt(2.0 / math.pi)).then_inc(S["hid_tanh"], 1)
                if c == 0:
                    act.wait_ge(S["cb_done"], 1)
                    for i in range(4):
                        last = fn(cb[:, i, :, :].rearrange("p e n -> p n e"),
                                  pm[0][:, 64 * i:64 * i + 256].rearrange("p (n e) -> p n e", e=16)[:, ::-1, :], ACT.Copy)
                    last.then_inc(S["cb_kept"], 1)
                else:
                    rows(18, 19)
                act.wait_ge(S["cmp_done"], c + 1)
                if c == 0:
                    fn(kcT[:, :, :], pnb[1][:, 0:160].rearrange("p (g n) -> p g n", g=2), ACT.Copy).then_inc(S["cmp_kept"], 1)
                    rows(16, 18)
                else:
                    fn(vcp[:, :], pnb[1][0:16, 0:256], ACT.Copy)
                    fn(vcs[:, :], pnb[0][0:64, 0:256], ACT.Copy).then_inc(S["cmp_kept"], 1)
                    act.wait_ge(S["gate_w_in"], 16)
                    fn(wg_hi[:, :, :], wg_raw[:, :, :], ACT.Copy).then_inc(S["wg_hi_s"], 1)
                    rows(19, 22)

            sh, s_, _ = site(2)
            affine(3, s_, sh)
            split_hi("q", 0, 0)
            split_hi("q", 0, 1)
            act.wait_ge(S["g_done"], 1)
            fn(gT[:, :], pu[1][0:48, PSO:PSO + NT], ACT.Exp, scale=-1.0).then_inc(S["g_kept"], 1)
            for gp in range(2):
                def heads(it, first, last_turn=False):
                    T = 2 * gp + it
                    for u in range(2):
                        n = UBASE["q"] + 2 * T + u
                        act.wait_ge(S["unit_done"], n + 1)
                        if not (gp == 0 and first):
                            act.wait_ge(S["S_done"], NSI * T)
                        fn(qT[u][:, :], prod[0], ACT.Copy, scale=0.125).then_inc(S["out_taken"], 1)
                        hold(act, S["out_taken"], n + 1)
                        fn(qs[:, bass.ds(2 * T + u, 1), :].rearrange("p o b -> p (o b)"), qT[u][:, NP:NT], ACT.Copy)\
                            .then_inc(S["q_in_sb"], 1)
                        if not last_turn:
                            split_hi("q", T + 1, u)
                    if gp == 0 and first:
                        act.wait_ge(S["g_tr"], 1)
                        fn(gat[:, :, :], pm[0][:, 0:192].rearrange("p (i n) -> p i n", i=4), ACT.Copy).then_inc(S["g_kept"], 1)
                        fn(gts[:, :], pm[0][0:NS, 192:240], ACT.Copy).then_inc(S["g_kept"], 1)
                        act.wait_ge(S["g_kept"], 3)
                        act.dma_start(gates_d, gts[:, :]).then_inc(S["g_sent"], 16)
                        act.wait_ge(S["g_sent"], 16)
                        act.dma_start(gr[:, :], bass.AP(gates_d.tensor, 0, [[3, 16], [48, 8], [1, 3]])).then_inc(S["g_back"], 16)

                    def expo(step):
                        m, f, br, i = S_ITEMS[step][1]
                        act.wait_ge(S["nm_ready"], 32 * T + m + 1)
                        if not (gp == 0 and first and m < 4):
                            act.wait_ge(S["PT_done"], 32 * T + m - 3)
                            if not (gp == 0 and first and m < 8):
                                act.wait_ge(S["O_kept"], 32 * T + m - 7)
                        W = 128 * (i + 1)
                        fn(Pb[m % 4][:, 0:W], Ss[m % 2][:, 0:W], ACT.Exp, bias=nm[:, m % 4:m % 4 + 1],
                           accum_out=den[:, m % 8:m % 8 + 1]).then_inc(S["P_ready"], 1)

                    def keep_t(step):
                        m, f, br, i = S_ITEMS[step][1]
                        if m % 2:
                            return
                        act.wait_ge(S["PT_done"], 32 * T + m + 1)
                        if not (gp == 0 and first and m < 2):
                            act.wait_ge(S["O_done"], 32 * T + m - 1)
                        W = 128 * (i + 1)
                        fn(PTb[0][:, 0:W], pm[0][:, 0:W], ACT.Copy).then_inc(S["PT_kept_a"], 1)

                    for step in range(len(S_ITEMS) + 2):
                        if step < len(S_ITEMS) and S_ITEMS[step][1] is not None:
                            expo(step)
                        if step >= 2 and S_ITEMS[step - 2][1] is not None:
                            keep_t(step - 2)
                heads(0, gp == 0)
                heads(1, False, last_turn=(gp == 1))

            act.wait_ge(S["c_max"], 1)
            fn(sc[:, :, :, :].rearrange("p i e n -> p (i e n)"), sc[:, :, :, :].rearrange("p i e n -> p (i e n)"), ACT.Exp)\
                .then_inc(S["c_exp"], 1)
            for n in range(8):
                act.wait_ge(S["c_tr"], n + 1)
                if n >= 2:
                    act.wait_ge(S["c_out"], n - 1)
                fn(pcT[n % 2][:, :], pm[n % 2][:, 0:128], ACT.Copy).then_inc(S["c_trk"], 1)

            def sample_keys(i, first):
                for s in range(2):
                    b = 2 * i + s
                    act.wait_ge(S["sk_tr"], b + 1)
                    if not (first and s == 0):
                        act.wait_ge(S["s_sc"], b)
                    for gp in range(2):
                        last = fn(ksT[:, gp, :], pm[gp][:, :], ACT.Copy)
                    last.then_inc(S["sk_sb"], 2)
                    hold(act, S["s_sc"], b + 1)
                    for f in range(2):
                        STv = ST[:, :, bass.ds(b, 16, step=8)].rearrange("p j (g f q) -> p j g f q", g=2, f=2)
                        last = fn(STv[:, :, :, f], pnb[f][:, 0:32].rearrange("p (j g q) -> p j g q", j=4, g=2), ACT.Copy)
                    last.then_inc(S["s_sck"], 1)
            act.wait_ge(S["c_added"], 8)
            turns(act, 4, sample_keys, first=True)
            act.wait_ge(S["sn_done"], 1)
            for f, bank in enumerate((pm[0], pnb[1])):
                STv = STn[:, :, :].rearrange("p k (g f r) -> p k g f r", g=2, f=2)
                fn(STv[0:8, 0:2, :, f], bank[0:8, 0:128].rearrange("p (k g r) -> p k g r", k=2, g=2), ACT.Copy)
                fn(STv[0:64, 2, :, f], bank[0:64, 128:192].rearrange("p (g r) -> p g r", g=2), ACT.Copy).then_inc(S["sn_kept"], 1)
            fn(bias_s[:, :], pnb[0][:, 0:328], ACT.Copy).then_inc(S["sn_kept"], 1)
            act.wait_ge(S["sS_bias"], 1)
            for br, c0, n in ((0, 0, 264), (1, 264, 264), (2, 528, 64)):
                last = fn(Sa[:, c0:c0 + n], Sa[:, c0:c0 + n], ACT.Exp, bias=smx[:, br:br + 1], accum_out=sden[:, br:br + 1])
            last.then_inc(S["s_exp"], 1)
            act.wait_ge(S["sP_tr"], 1)
            fn(pT[:, :, :], pm[0][:, :].rearrange("p (j r) -> p j r", j=4), ACT.Copy).then_inc(S["sP_kept"], 1)
            fn(pTn[0:8, 0:2, :], pm[1][0:8, 0:256].rearrange("p (k r) -> p k r", k=2), ACT.Copy).then_inc(S["sP_kept"], 1)
            fn(pTn[0:64, 2, :], pm[1][0:64, 256:384], ACT.Copy).then_inc(S["sP_kept"], 1)

            for n in range(8):
                i, kk = divmod(n, 2)
                act.wait_ge(S["oT_tr"], n + 1)
                bank = (pm[0], pnb[1])[n % 2]
                fn(h_hi[:, 4 * kk:4 * kk + 4, 128 * i:128 * i + 128], bank.rearrange("p (t c) -> p t c", t=4), ACT.Copy)\
                    .then_inc(S["oh_ready"], 1)
            act.wait_ge(S["oS_done"], 1)
            fn(h_hi[:, :, NP:NT], oS[:, :, :], ACT.Copy).then_inc(S["oh_ready"], 1)

            act.wait_ge(S["olo_ready"], 9)
            out_phase("attn_out", 5)
            rows(22, 23)
            root(5)
            squares(6, x, lambda k: [("x_updated", 18 + k + 2)], between={1: 23, 6: 24})
            rows(25, 26)
            root(6)
            ffn(1, 4)
            root(7)
            history_out(1)
            for n in range(10):
                act.wait_ge(S["y_tr"], n + 1)
                if n < 8:
                    i = n // 2
                    if i >= 2:
                        act.wait_ge(S[f"y_out{i % 2}"], 16)
                    fn(yt[i % 2][:, 512 * (n % 2):512 * (n % 2) + 512], banks[n % 4], ACT.Copy).then_inc(S["y_kept"], 1)
                else:
                    fn(yts[:, 512 * (n % 2):512 * (n % 2) + 512], banks[n % 4][0:NS, :], ACT.Copy).then_inc(S["y_kept"], 1)
            act.wait_ge(S["win_out"], 16 * 11)
            act.wait_ge(S["kvp_out"], 16 * 4)
            act.wait_ge(S["s_out"], 16 * 8)

        @block.vector
        def _(dve):
            v = nc.vector
            banks = [pnb[0], pnb[1], pm[0], pm[1]]
            ch = Chain(dve, S["dve_seq"])

            def wide(ap, n):
                return ap.unsqueeze(2).to_broadcast([ap.shape[0], ap.shape[1], n])

            v.memset(ones[:, :], 1.0).then_inc(S["ones_set"], 1)
            v.memset(tab[32:33, :], 1.0).then_inc(S["tab_set"], 1)
            dve.wait_ge(S["consts_in"], 16 * 8)
            dve.wait_ge(S["tab_set"], 1)
            v.tensor_copy(tabp[:, :].rearrange("t (g q f) -> t g q f", g=2, q=4),
                          tab[:, :].rearrange("t (g f q) -> t g q f", g=2, f=2))
            v.tensor_copy(tabr[:, :].rearrange("t (h b) -> t h b", b=NS), wide(tab[0:32, :], NS))

            for t in range(1, 15, 2):
                dve.wait_ge(S["tr_done"], t + 1)
                bank = banks[t % 4]
                if t < 5:
                    col = 0
                    for tile in range(4 * t, 4 * t + 4):
                        n = valid[tile]
                        last = v.tensor_copy(PT[:, 128 * tile:128 * tile + n], bank[:, col:col + n])
                        col += n
                elif t < 13:
                    i, kk = divmod(t - 5, 2)
                    last = v.tensor_copy(x[:, 4 * kk:4 * kk + 4, 128 * i:128 * i + 128], bank.rearrange("p (k c) -> p k c", k=4))
                else:
                    last = v.tensor_copy(lrow[:, 0:512], banks[1][0:16, :])
                last.then_inc(S["tr_taken_v"], 1)

            dve.wait_ge(S["tr_taken_a"], 7)
            dve.wait_ge(S["tr_taken_v"], 7)
            ch.link(v.tensor_copy(x[:, :, NP:NT], PTv(R_XS, 64).rearrange("p (b k) -> p k b", k=KT)))

            def history(out, state, w, n, tmp):
                st_ = state.rearrange("p (b j k) -> p j k b", b=NS, j=2)
                ch.mark(v.tensor_tensor(out, st_[:, 0], wide(w[:, 0:n], NS), ALU.mult))
                ch.link(v.tensor_tensor(tmp, st_[:, 1], wide(w[:, n:2 * n], NS), ALU.mult))
                ch.link(v.tensor_tensor(out, out, tmp, ALU.add))
            history(sca[:, :, :], PTv(R_STA, 128), PTv(R_ACW, 24), KT, ts[:, :, :])
            for l in range(2):
                history(scf[:, l], PTv(R_STF + 704 * l, 704), PTv(R_FCW + 132 * l, 132), 2 * FT,
                        nt[0][:, 0:352].rearrange("p (k b) -> p k b", b=NS))
            v.tensor_copy(st_z[0:1, 0:1], ones[0:1, 0:1]).then_inc(S["prep_done"], 1)

            def mods(first, last):
                for q in range(first, last):
                    dve.wait_ge(S["mod_t"], q + 1)
                    ft = 24 * MODS[q][0] + 4 * MODS[q][1]
                    v.tensor_tensor(modT[:, ft:ft + 4, :], mod_places(q)[2].rearrange("p (t r) -> p t r", t=4),
                                    wide(PT[:, ft:ft + 4], NC9), ALU.add).then_inc(S["mod_kept"], 1)

            def norm_scale(k, kept):
                s_ = site(k)[1]
                dve.wait_ge(S["mod_kept"], kept)
                ch.link(v.scalar_tensor_tensor(s_, s_, 1.0, wide(PTv(R_NG + 16 * k, 8) if k < 4 else PTv(R_KVG, 8), NC9),
                                               ALU.add, ALU.mult))

            def norm_gate(k, kept):
                gate = site(k)[2]
                dve.wait_ge(S["mod_kept"], kept)
                ch.link(v.tensor_tensor(gate, gate, wide(PTv(R_NG + 16 * k + 8, 8), NC9), ALU.mult))

            def mean(m):
                dve.wait_ge(S["norm_done"], m + 1)
                ch.link(v.tensor_scalar(rstd[:, :], pn[:, PSO:PSO + NT], 1.0 / D, EPS, ALU.mult, ALU.add))
                v.reciprocal(rstd[:, :], rstd[:, :]).then_inc(S["rs_ready"], 1)
                dve.wait_ge(S["rstd_ready"], m + 1)

            rs_s = rstd[:, NP:NT].unsqueeze(1).to_broadcast([128, KT, NS])

            def modulate(q, scale, shift):
                if q > 0:
                    dve.wait_ge(S["hlo_ready"], 9 * q)
                ch.link(v.tensor_tensor(ts[:, :, :], x[:, :, NP:NT], rs_s, ALU.mult))
                ch.link(v.tensor_tensor(ts[:, :, :], ts[:, :, :], scale[:, :, 1:NC9], ALU.mult))
                ch.link(v.tensor_tensor(ts[:, :, :], ts[:, :, :], shift[:, :, 1:NC9], ALU.add))
                v.tensor_copy(h_hi[:, :, NP:NT], ts[:, :, :]).then_inc(S["hhi_ready"], 1)
                for k in range(KT + 1):
                    if k < KT:
                        if 8 * q + k >= 2:
                            dve.wait_ge(S["hf_ready"], 8 * q + k - 1)
                        v.tensor_tensor(nt[k % 2][:, 0:NP], x[:, k, 0:NP], rstd[:, 0:NP], ALU.mult).then_inc(S["t_ready"], 1)
                    if k > 0:
                        dve.wait_ge(S["hf_ready"], 8 * q + k)
                        v.tensor_copy(h_hi[:, k - 1, 0:NP], hf[(k - 1) % 2][:, 0:NP]).then_inc(S["hhi_ready"], 1)

            def update(p, gate):
                ch.link(v.tensor_tensor(ts[:, :, :], o[:, :, NP:NT], rs_s, ALU.mult))
                ch.link(v.tensor_tensor(ts[:, :, :], ts[:, :, :], gate[:, :, 1:NC9], ALU.mult))
                v.tensor_tensor(x[:, :, NP:NT], x[:, :, NP:NT], ts[:, :, :], ALU.add).then_inc(S["x_updated"], 1)
                for k in range(KT):
                    ch.link(v.tensor_tensor(nt[k % 2][:, 0:NP], o[:, k, 0:NP], rstd[:, 0:NP], ALU.mult))
                    v.scalar_tensor_tensor(x[:, k, 0:NP], nt[k % 2][:, 0:NP], gate[:, k, 0:1], x[:, k, 0:NP], ALU.mult, ALU.add)\
                     .then_inc(S["x_updated"], 1)
                dve.wait_ge(S["x_updated"], 9 * (p + 1))

            def conv(y, u, w, b, history_term):
                ch.link(v.tensor_scalar(y[:, :], u[:, 2:2 + NT], w[2], b, ALU.mult, ALU.add))
                ch.mark(v.tensor_tensor(y[:, NP:NT], y[:, NP:NT], history_term, ALU.add))
                ch.link(v.scalar_tensor_tensor(y[:, 0:NP], u[:, 1:1 + NP], w[1], y[:, 0:NP], ALU.mult, ALU.add))
                return v.scalar_tensor_tensor(y[:, 0:NP], u[:, 0:NP], w[0], y[:, 0:NP], ALU.mult, ALU.add)

            mods(0, 2)
            mean(0)
            mods(2, 4)
            norm_scale(0, 4)
            sh, s_, _ = site(0)
            modulate(0, s_, sh)

            def mix(i, first):
                for e in range(2):
                    j = 2 * i + e
                    dve.wait_ge(S["out_taken"], 6 * i + 3 * e + 2)
                    if first and e == 0:
                        dve.wait_ge(S["ub_zero"], 1)
                    else:
                        dve.wait_ge(S["z10_kept"], j)
                    ch.link(v.tensor_tensor(ub[0][:, 2:2 + NT], sg[:, :], yb[0][:, :], ALU.mult))
                    v.tensor_copy(zflag[:, 0:1], ub[0][:, 2:3]).then_inc(S["z_made"], 1)
                    w = [PT[:, bass.ds(R_ACW + 8 * t + j, 1)] for t in range(3)]
                    ch.link(conv(yb[1], ub[0], w, PT[:, bass.ds(R_ACB + j, 1)],
                                 sca[:, bass.ds(j, 1), :].rearrange("p o b -> p (o b)")))
                    dve.wait_ge(S["out_taken"], 6 * i + 3 * e + 3)
                    if first and e == 0:
                        dve.wait_ge(S["hlo_ready"], 9)
                        mods(4, 6)
                    else:
                        dve.wait_ge(S["mix_lo"], j)
                    v.tensor_tensor(hf[0][:, :], yb[1][:, :], af[:, :], ALU.mult).then_inc(S["mixed"], 1)
            ch.turns(4, 10, mix, first=True)

            norm_gate(0, 6)
            mean(1)
            update(0, site(0)[2])
            mods(6, 10)
            norm_scale(1, 10)
            mean(2)

            def ffn_pairs(l, half, half_l):
                gates = MOD_AT[2 * l + 1] + 4
                def body(i, first):
                    j = FH * half + i
                    for s in range(2):
                        n = UBASE[f"up{l}{half_l}"] + 2 * i + s
                        dve.wait_ge(S["out_taken"], n + 1)
                        if not (half == 0 and first):
                            dve.wait_ge(S["silu_done" if s else "af_ready"], j)
                        ft = FH * half_l + i + FT * s
                        w = [PT[:, bass.ds(R_FCW + 132 * l + 44 * t + ft, 1)] for t in range(3)]
                        conv(yb[s], ub[s], w, PT[:, bass.ds(R_FCB + 44 * l + ft, 1)],
                             scf[:, l, bass.ds(ft, 1), :].rearrange("p o b -> p (o b)")).then_inc(S["conv_done"], 1)
                    if first and half_l == 0:
                        mods(gates, gates + 2)
                    dve.wait_ge(S["silu_done"], j + 1)
                    dve.wait_ge(S["conv_done"], 2 * j + 1)
                    if not (half == 0 and first):
                        dve.wait_ge(S["act_lo_done"], j)
                    v.tensor_tensor(af[:, :], sg[:, :], yb[0][:, :], ALU.mult).then_inc(S["af_ready"], 1)
                ch.turns(FH, 6, body, first=(half_l == 0))

            def add_halves(l):
                def body(i, first):
                    for s in range(2):
                        dve.wait_ge(S["out_taken"], UBASE[f"down{l}1"] + 2 * i + s + 1)
                        ok = o[:, bass.ds(2 * i + s, 1), :].rearrange("p a n -> p (a n)")
                        v.tensor_tensor(ok, ok, nt[0][:, :], ALU.add).then_inc(S["half_added"], 1)
                turns(dve, 4, body)

            def ffn(l, q):
                sh, s_, _ = site(2 * l + 1)
                modulate(q, s_, sh)
                ffn_pairs(l, 2 * l, 0)
                ffn_pairs(l, 2 * l + 1, 1)
                add_halves(l)

            ffn(0, 1)
            norm_gate(1, 12)
            mean(3)
            update(1, site(1)[2])
            mods(12, 16)
            norm_scale(4, 16)
            mean(4)
            sh, s_, _ = site(4)
            modulate(2, s_, sh)

            for n in range(15):
                t = 15 + n
                if t % 2 == 0:
                    continue
                dve.wait_ge(S["tr_done"], t + 1)
                if n < 12:
                    dst, src = kvt[:, n % 4, 512 * (n // 4):512 * (n // 4) + 512], banks[t % 4]
                else:
                    dst, src = kvs[:, 512 * (n - 12):512 * (n - 12) + 512], banks[t % 4][0:NS, :]
                v.tensor_copy(dst, src).then_inc(S["tr_taken_v"], 1)

            for c in range(2):
                dve.wait_ge(S["hid_done"], c + 1)
                if c == 1:
                    dve.wait_ge(S["cmp_done"], 1)
                hid = pn[:, 0:162].rearrange("p (g n) -> p g n", g=2)
                ch.link(v.tensor_copy(hemb[:, :], pn[:, 80:81]))
                ch.link(v.tensor_scalar(hx[:, :, :], hid[:, :, 0:80], hemb[:, 0:1], None, ALU.add))
                ch.link(v.tensor_tensor(hy[:, :, :], hx[:, :, :], hx[:, :, :], ALU.mult))
                ch.link(v.tensor_tensor(hy[:, :, :], hy[:, :, :], hx[:, :, :], ALU.mult))
                v.scalar_tensor_tensor(hy[:, :, :], hy[:, :, :], 0.044715, hx[:, :, :], ALU.mult, ALU.add)\
                    .then_inc(S["hid_lin"], 1)
                dve.wait_ge(S["hid_tanh"], c + 1)
                ch.link(v.tensor_scalar(hz[:, :, :], hz[:, :, :], 1.0, 0.5, ALU.add, ALU.mult))
                v.tensor_tensor(hx[:, :, :], hx[:, :, :], hz[:, :, :], ALU.mult).then_inc(S["hid_act"], 1)
                mods(*((16, 18), (18, 22))[c])

            dve.wait_ge(S["cb_kept"], 1)
            dve.wait_ge(S["wg_hi_s"], 1)
            v.tensor_tensor(wg_lo[:, :, :], wg_raw[:, :, :], wg_hi[:, :, :].bitcast(f32), ALU.subtract).then_inc(S["wg_lo_s"], 1)
            norm_scale(2, 22)
            norm_gate(2, 22)
            sh, s_, _ = site(2)
            modulate(3, s_, sh)
            dve.wait_ge(S["g_kept"], 1)
            ch.link(v.tensor_scalar_add(gT[:, :], gT[:, :], 1.0))
            v.reciprocal(gT[:, :], gT[:, :]).then_inc(S["g_rt"], 1)
            dve.wait_ge(S["g_kept"], 3)

            for gp in range(2):
                def heads(it, first):
                    T = 2 * gp + it

                    def bias(step):
                        u, item = S_ITEMS[step]
                        dve.wait_ge(S["S_done"], NSI * T + step + 1)
                        if item is None:
                            e = 8 * gp + 4 * it + 2 * u + step % 2
                            v.tensor_tensor(sc[:, :, bass.ds(e, 1), :].rearrange("p i o n -> p i (o n)"),
                                            pnb[step % 2][:, 0:64].rearrange("p (i n) -> p i n", i=4),
                                            cb[:, :, bass.ds(e, 1), :].rearrange("p i o n -> p i (o n)"), ALU.add)\
                                .then_inc(S["S_biased"], 1)
                            return
                        m, f, br, i = item
                        W = 128 * (i + 1)
                        if not (gp == 0 and first and m < 2):
                            dve.wait_ge(S["P_ready"], 32 * T + m - 1)
                        hold(dve, S[f"H_in{2 * u + f}"], 16 * (T + 1))
                        v.tensor_tensor_reduce(out=Ss[m % 2][:, 0:W], in0=pnb[step % 2][:, 0:W],
                                               in1=Hb[2 * u + f][:, 0:W][:, ::-1], scale=1.0, scalar=-3.0e38,
                                               op0=ALU.add, op1=ALU.max, accum_out=mx[:, m % 4:m % 4 + 1])\
                            .then_inc(S["S_biased"], 1)
                        dve.wait_ge(S["S_biased"], NSI * T + step + 1)
                        ins = v.tensor_scalar(nm[:, m % 4:m % 4 + 1], mx[:, m % 4:m % 4 + 1], -1.0, None, ALU.mult)
                        ins.then_inc(S["nm_ready"], 1)
                        if br == 1 and i == 0:
                            v.tensor_copy(zflag[:, 0:1], ones[:, 0:1]).then_inc(S["head_used"], 1)

                    def keep_t(step):
                        m, f, br, i = S_ITEMS[step][1]
                        if m % 2 == 0:
                            return
                        dve.wait_ge(S["PT_done"], 32 * T + m + 1)
                        if not (gp == 0 and first and m < 2):
                            dve.wait_ge(S["O_done"], 32 * T + m - 1)
                        W = 128 * (i + 1)
                        v.tensor_copy(PTb[1][:, 0:W], pm[1][:, 0:W]).then_inc(S["PT_kept_v"], 1)

                    def gather(step):
                        u = S_ITEMS[step][0]
                        m, f, br, i = S_ITEMS[step][1]
                        dve.wait_ge(S["P_ready"], 32 * T + m + 1)
                        c = cf[:, m % 4:m % 4 + 1]
                        ch.link(v.reciprocal(c, den[:, m % 8:m % 8 + 1]))
                        gcol = 3 * (8 * gp + 4 * f + 2 * it + u) + 1 + br
                        ch.link(v.tensor_tensor(c, c, gat[:, i, bass.ds(gcol, 1)], ALU.mult))
                        dve.wait_ge(S["O_done"], 32 * T + m + 1)
                        dst = Oacc[:, i, bass.ds(64 * (8 * gp + 4 * it + 2 * u + f), 64)]
                        O_ = pu[1][:, 512 * (m % 2):512 * (m % 2) + 64]
                        if br == 0:
                            ins = v.tensor_scalar(dst, O_, c, None, ALU.mult)
                        else:
                            ins = v.scalar_tensor_tensor(dst, O_, c, dst, ALU.mult, ALU.add)
                        ins.then_inc(S["O_kept"], 1)

                    for step in range(len(S_ITEMS) + 4):
                        if step < len(S_ITEMS):
                            bias(step)
                        if 2 <= step < len(S_ITEMS) + 2 and S_ITEMS[step - 2][1] is not None:
                            keep_t(step - 2)
                        if step >= 4 and S_ITEMS[step - 4][1] is not None:
                            gather(step - 4)
                ch.turns(2, 2 * 32, heads, first=(gp == 0))
            dve.wait_ge(S["O_kept"], 128)

            rows = sc[:, :, :, :].rearrange("p i e n -> p (i e) n")
            ch.link(v.tensor_reduce(cm[:, :], rows, AX.X, ALU.max))
            ch.link(v.tensor_scalar(cm[:, :], cm[:, :], FLOOR, None, ALU.max))
            v.tensor_tensor(rows, rows, wide(cm[:, :], 16), ALU.subtract).then_inc(S["c_max"], 1)
            for gp in range(2):
                dve.wait_ge(S["vrep_done"], gp + 1)
                for q in range(4):
                    e = 2 * q
                    last = v.tensor_tensor(vblk[:, gp, 128 * q:128 * q + 128].rearrange("p (f d) -> p f d", f=2),
                                           pm[gp][:, 0:128].rearrange("p (f d) -> p f d", f=2), wide(blk[:, e:e + 2], 64), ALU.mult)
                last.then_inc(S["v_blk"], 1)
            dve.wait_ge(S["c_exp"], 1)
            ch.link(v.tensor_reduce(cd[:, :], rows, AX.X, ALU.add))
            ch.link(v.tensor_scalar(cd[:, :], cd[:, :], 1.0e-30, None, ALU.max))
            ch.link(v.reciprocal(cd[:, :], cd[:, :]))
            gq = gat[:, :, :].rearrange("p i (g f q b) -> p i g q f b", g=2, f=2, q=4)
            cdv = cd[:, :].rearrange("p (i g q f) -> p i g q f", i=4, g=2, q=4)
            for i in range(4):
                for g in range(2):
                    ch.mark(v.tensor_tensor(cdv[:, i, g], cdv[:, i, g], gq[:, i, g, :, :, 0], ALU.mult))
            ch.settle()
            v.tensor_tensor(rows, rows, wide(cd[:, :], 16), ALU.mult).then_inc(S["c_prob"], 1)
            for n in range(8):
                i, g = divmod(n, 2)
                dve.wait_ge(S["c_out"], n + 1)
                dst = Oacc[:, i, 512 * g:512 * g + 512]
                v.tensor_tensor(dst, dst, pnb[n % 2], ALU.add).then_inc(S["c_added"], 1)

            def queries(i, first):
                for s in range(2):
                    b = 2 * i + s
                    if not (first and s == 0):
                        dve.wait_ge(S["s_sc"], b)
                    v.tensor_copy(qb[:, :], qs[:, :, bass.ds(b, 1)].rearrange("p t o -> p (t o)")).then_inc(S["qb_set"], 1)
            dve.wait_ge(S["c_added"], 8)
            dve.wait_ge(S["kvp_out"], 16 * 4)
            turns(dve, 4, queries, first=True)
            dve.wait_ge(S["sS_tr"], 1)
            dve.wait_ge(S["sn_kept"], 3)
            for k, c0 in enumerate((0, 264)):
                ch.mark(v.tensor_tensor(Sa[:, c0:c0 + 256], pm[1][:, 256 * k:256 * k + 256], bias_s[:, 0:256], ALU.add))
                ch.mark(v.tensor_tensor(Sa[:, c0 + 256:c0 + 264], pnb[1][:, 8 * k:8 * k + 8], bias_s[:, 256:264], ALU.add))
            ch.link(v.tensor_tensor(Sa[:, 528:592], pnb[1][:, 16:80], bias_s[:, 264:328], ALU.add))
            for c0, n, m0 in ((256, 8, 0), (520, 8, 0), (528, 64, 8)):
                ch.mark(v.tensor_tensor(Sa[:, c0:c0 + n], Sa[:, c0:c0 + n], smask[:, m0:m0 + n], ALU.add))
            ch.settle()
            for br, c0, n in ((0, 0, 264), (1, 264, 264), (2, 528, 64)):
                ch.mark(v.tensor_reduce(smx[:, br:br + 1], Sa[:, c0:c0 + n], AX.X, ALU.max))
            ch.settle()
            v.tensor_scalar(smx[:, 0:3], smx[:, 0:3], -1.0, None, ALU.mult).then_inc(S["sS_bias"], 1)
            dve.wait_ge(S["s_exp"], 1)
            dve.wait_ge(S["g_back"], 16)
            ch.link(v.reciprocal(scof[:, 0:3], sden[:, 0:3]))
            for br, gcol in ((0, 1), (1, 2), (2, 0)):
                ch.mark(v.tensor_tensor(scof[:, br:br + 1], scof[:, br:br + 1], gr[:, gcol:gcol + 1], ALU.mult))
            ch.settle()
            for br, c0, n in ((0, 0, 264), (1, 264, 264), (2, 528, 64)):
                last = v.tensor_scalar(Sa[:, c0:c0 + n], Sa[:, c0:c0 + n], scof[:, br:br + 1], None, ALU.mult)
            last.then_inc(S["s_p"], 1)
            dve.wait_ge(S["sP_kept"], 3)

            def values(i, first):
                for s in range(2):
                    b = 2 * i + s
                    if not (first and s == 0):
                        dve.wait_ge(S["sv_done"], b)
                    v.tensor_copy(pb[:, :, :], pT[:, :, bass.ds(b, 16, step=8)]).then_inc(S["pb_set"], 1)
                    dve.wait_ge(S["sv_done"], b + 1)
                    v.tensor_copy(oS[:, :, bass.ds(b, 1)].rearrange("p t o -> p (t o)"), pnb[0][:, 0:8]).then_inc(S["sv_kept"], 1)
            turns(dve, 4, values, first=True)
            dve.wait_ge(S["sv_all"], 1)
            dve.wait_ge(S["sv_kept"], 8)
            v.tensor_tensor(oS[:, :, :].rearrange("p t b -> p (t b)"), oS[:, :, :].rearrange("p t b -> p (t b)"), pm[1][:, 0:64],
                            ALU.add).then_inc(S["oS_done"], 1)

            for n in range(8):
                i, kk = divmod(n, 2)
                dve.wait_ge(S["oh_ready"], n + 1)
                bank = (pm[0], pnb[1])[n % 2].rearrange("p (t c) -> p t c", t=4)
                v.tensor_tensor(h_lo[:, 4 * kk:4 * kk + 4, 128 * i:128 * i + 128], bank,
                                h_hi[:, 4 * kk:4 * kk + 4, 128 * i:128 * i + 128].bitcast(f32), ALU.subtract)\
                    .then_inc(S["olo_ready"], 1)
            dve.wait_ge(S["oh_ready"], 9)
            dve.wait_ge(S["oS_done"], 1)
            v.tensor_tensor(h_lo[:, :, NP:NT], oS[:, :, :], h_hi[:, :, NP:NT].bitcast(f32), ALU.subtract)\
                .then_inc(S["olo_ready"], 1)

            mean(5)
            update(2, site(2)[2])
            mods(22, 26)
            norm_scale(3, 26)
            mean(6)
            ffn(1, 4)
            norm_gate(3, 28)
            mean(7)
            update(3, site(3)[2])

        @block.gpsimd
        def _(pool):
            g = nc.gpsimd

            def split_lo(phase, i, s):
                n, k = UBASE[phase] + 2 * i + s, KOF[phase]
                pool.wait_ge(S["w_hi_ready"], n + 1)
                g.tensor_tensor(w_lo[s][:, 0:k, :], w_raw[s][:, 0:k, :], w_hi[s][:, 0:k, :].bitcast(f32), ALU.subtract)\
                    .then_inc(S["w_lo_ready"], 1)

            def add_square(m, k, s, first):
                pool.wait_ge(S["sq_ready"], 8 * m + k + 1)
                if first:
                    if m > 0:
                        pool.wait_ge(S["norm_done"], m)
                    g.tensor_copy(sq[:, :], sqt[s][:, :]).then_inc(S["sq_added"], 1)
                else:
                    pool.wait_ge(S["sq_added"], 8 * m + k)
                    g.tensor_tensor(sq[:, :], sq[:, :], sqt[s][:, :], ALU.add).then_inc(S["sq_added"], 1)

            def trail(q):
                for k in range(KT + 1):
                    pool.wait_ge(S["hhi_ready"], 9 * q + k + 1)
                    if k == 0:
                        dst, full, hi = h_lo[:, :, NP:NT], ts[:, :, :], h_hi[:, :, NP:NT]
                    else:
                        dst, full, hi = h_lo[:, k - 1, 0:NP], hf[(k - 1) % 2][:, 0:NP], h_hi[:, k - 1, 0:NP]
                    g.tensor_tensor(dst, full, hi.bitcast(f32), ALU.subtract).then_inc(S["hlo_ready"], 1)

            for k in range(KT):
                add_square(0, k, k % 2, k == 0)
            split_lo("mix_in", 0, 0)
            split_lo("mix_in", 0, 1)
            trail(0)
            pool.wait_ge(S["mod_done"], 4)
            for s in range(2):
                last = g.memset(ub[s][:, 0:2], 0.0)
            last.then_inc(S["ub_zero"], 1)

            def mix(i, first, last_turn=False):
                for u in range(6):
                    j, part = 2 * i + u // 3, u % 3
                    if part == 1:
                        pool.wait_ge(S["z_made"], j + 1)
                        g.tensor_copy(z10[:, :, bass.ds(j, 1)].rearrange("p t o -> p (t o)"), ub[0][:, NP:NP + 10])\
                            .then_inc(S["z10_kept"], 1)
                    if part == 2:
                        pool.wait_ge(S["mix_hi"], j + 1)
                        g.tensor_tensor(act_lo[:, bass.ds(j, 1), :].rearrange("p o n -> p (o n)"), hf[0][:, :],
                                        act_hi[:, bass.ds(j, 1), :].rearrange("p o n -> p (o n)").bitcast(f32), ALU.subtract)\
                            .then_inc(S["mix_lo"], 1)
                    if not last_turn or u < 4:
                        s = u % 2
                        pool.wait_ge(S["w_hi_ready"], 6 * i + u + 3)
                        g.tensor_tensor(w_lo[s][:, 0:KT, :], w_raw[s][:, 0:KT, :], w_hi[s][:, 0:KT, :].bitcast(f32), ALU.subtract)\
                            .then_inc(S["w_lo_ready"], 1)
                    else:
                        split_lo("mix_out", 0, u % 2)
            mix(0, True)
            with pool.Fori(1, 3) as i:
                mix(i, False)
            mix(3, False, last_turn=True)

            def out_phase(name, m):
                if name == "attn_out":
                    split_lo(name, 0, 0)
                    split_lo(name, 0, 1)

                def body(i, first, last_turn=False):
                    for s in range(2):
                        if not last_turn:
                            split_lo(name, i + 1, s)
                        elif name in NEXT:
                            split_lo(NEXT[name], 0, s)
                        if m is not None:
                            add_square(m, 2 * i + s, s, first and s == 0)
                body(0, True)
                with pool.Fori(1, 3) as i:
                    body(i, False)
                body(3, False, last_turn=True)

            def up_phase(name, half, half_l):
                def body(i, first, last_turn=False):
                    j = FH * half + i
                    for s in range(2):
                        if not last_turn:
                            split_lo(name, i + 1, s)
                        else:
                            split_lo(NEXT[name], 0, s)
                        pool.wait_ge(S["out_taken"], UBASE[name] + 2 * i + s + 1)
                        g.tensor_copy(up10[:, :, bass.ds(FH * half_l + i + FT * s, 1)].rearrange("p t o -> p (t o)"),
                                      ub[s][:, NP:NP + 10]).then_inc(S["up10_kept"], 1)
                    pool.wait_ge(S["act_hi_done"], j + 1)
                    g.tensor_tensor(act_lo[:, bass.ds(i, 1), :].rearrange("p o n -> p (o n)"), af[:, :],
                                    act_hi[:, bass.ds(i, 1), :].rearrange("p o n -> p (o n)").bitcast(f32), ALU.subtract)\
                        .then_inc(S["act_lo_done"], 1)
                body(0, True)
                with pool.Fori(1, FH - 1) as i:
                    body(i, False)
                body(FH - 1, False, last_turn=True)

            def ffn(l, q):
                trail(q)
                up_phase(f"up{l}0", 2 * l, 0)
                out_phase(f"down{l}0", None)
                up_phase(f"up{l}1", 2 * l + 1, 1)
                out_phase(f"down{l}1", 4 * l + 3)

            out_phase("mix_out", 1)
            for k in range(KT):
                add_square(2, k, k % 2, k == 0)
            ffn(0, 1)
            for k in range(KT):
                add_square(4, k, k % 2, k == 0)
            trail(2)
            for c in range(1, 6):
                for s in range(2):
                    split_lo("kv", c, s)
            pool.wait_ge(S["unit_done"], UBASE["kv"] + 1)
            g.memset(w1b[:, :, :], 0.0)
            g.memset(w2b[:, :, :], 0.0).then_inc(S["w1_zero"], 1)
            for c in range(2):
                pool.wait_ge(S["out_taken"], UBASE["q"])
                pool.wait_ge(S["unit_done"], UBASE["q"])
                if c == 1:
                    pool.wait_ge(S["hid_done"], 1)
                for gp in range(2):
                    g.tensor_copy(RT[:, gp, 0:NP], okv[:, 2 * c + gp, 0:NP]).then_inc(S["rt_rest"], 1)
            trail(3)
            split_lo("q", 0, 0)
            split_lo("q", 0, 1)
            for T in range(3):
                for u in range(2):
                    split_lo("q", T + 1, u)
            out_phase("attn_out", 5)
            for k in range(KT):
                add_square(6, k, k % 2, k == 0)
            for s in range(2):
                last = g.memset(ub[s][:, 0:2], 0.0)
            last.then_inc(S["ub_zero"], 1)
            ffn(1, 4)


_INS = ['x_prompt', 'x_sample', 'c_prompt', 'c_sample', 'cache_kv', 'cache_win', 'state_conv_a', 'state_ffn_conv',
        'page_table', 'mod_w', 'mod_b', 'norm_g', 'a_w_in', 'a_conv_w', 'a_conv_b', 'a_w_out', 'kv_mod_w', 'kv_mod_b',
        'kv_norm_g', 'w_kv', 'cmp_pe', 'cmp_w1', 'cmp_w2', 'b_w_qg', 'b_w_out', 'rel_bias', 'ffn_w_up', 'ffn_conv_w',
        'ffn_conv_b', 'ffn_w_down']
_OUTS = [('y_prompt', (1, 512, 1024)), ('y_sample', (8, 1, 1024)), ('new_kv_prompt', (1, 512, 4, 4, 64)),
         ('new_kv_sample', (8, 1, 4, 4, 64)), ('new_win_prompt', (1, 512, 2, 4, 64)), ('new_win_sample', (8, 256, 2, 4, 64)),
         ('new_conv_a_prompt', (1, 1, 2, 1024)), ('new_conv_a_sample', (1, 8, 2, 1024)),
         ('new_ffn_conv_prompt', (2, 1, 2, 5632)), ('new_ffn_conv_sample', (2, 8, 2, 5632))]


def kernel(**inputs):
    import numpy as _np
    import concourse.bacc as _bacc
    from concourse import mybir as _mybir
    from concourse.bass_utils import run_bass_kernel_spmd as _run

    nc = _bacc.Bacc("TRN2", target_bir_lowering=False, num_devices=1)
    arrays, ins, outs = {}, {}, {}
    tables = constants()
    for name in _INS + list(tables):
        a = _np.ascontiguousarray(inputs[name] if name in inputs else tables[name])
        arrays[f"in_{name}"] = a
        ins[name] = nc.dram_tensor(f"in_{name}", a.shape, _mybir.dt.from_np(a.dtype), kind="ExternalInput").ap()
    for name, shape in _OUTS:
        outs[name] = nc.dram_tensor(f"out_{name}", shape, _mybir.dt.float32, kind="ExternalOutput").ap()
    decoder_step(nc, ins, outs)
    r = _run(nc, [arrays], core_ids=[0])
    return tuple(r.results[0][f"out_{name}"] for name, _ in _OUTS)
```

```python
import math
from contextlib import ExitStack

import numpy as np
import concourse.bass as bass
from concourse import mybir

D = 1024
NP = 512
NS = 8
NT = NP + NS
HALF = NT // 2
KT = D // 128
FF = 2816
FT = FF // 128
FH = FT // 2
NC9 = NS + 1
HD = 64
PAST = 256
EPS = 1e-6
NEG = -1.0e30
FLOOR = -1.0e29
PSO = 512 - HALF
R_MODB, R_KVG, R_ACB = 0, 112, 120
R_NG, R_ACW = 128, 192
R_FCB, R_FCW = 256, 384
R_STA, R_STF = 768, 896
R_C, R_XS = 2304, 2432
PT_TILES = 20
UNITS = [("mix_in", 24), ("mix_out", 8), ("up00", 22), ("down00", 8), ("up01", 22), ("down01", 8),
         ("kv", 12), ("q", 8), ("attn_out", 8), ("up10", 22), ("down10", 8), ("up11", 22), ("down11", 8)]
UBASE, _n = {}, 0
for _name, _c in UNITS:
    UBASE[_name] = _n
    _n += _c
KV_SLOTS = [0, 1, 3, 5, 2, 4]
MODS = ([(0, c, z) for c, z in enumerate(("z2", "z0", "z1", "z2", "z0", "z1"))]
        + [(1, c, z) for c, z in enumerate(("h0", "h1", "z0", "z1", "z0", "z1"))]
        + [(4, c, z) for c, z in enumerate(("h0", "h1", "z0", "z1"))]
        + [(2, c, z) for c, z in enumerate(("w0", "w1", "w0", "w1", "w0", "w1"))]
        + [(3, c, z) for c, z in enumerate(("z0", "z1", "h0", "h1", "z0", "z1"))])
MOD_AT = {k: [m[0] for m in MODS].index(k) for k in range(5)}


S_ITEMS, N_TABLES = [], 14
for _u in range(2):
    S_ITEMS += [(_u, None), (_u, None)]
    S_ITEMS += [(_u, (16 * _u + 8 * f + 4 * br + 3 - i, f, br, i)) for f in range(2) for br in range(2)
                for i in (3, 2, 1, 0)]


NSI = len(S_ITEMS)
STEPS = 4 * NSI
Q_STEPS = [4 * n + r for n in range(4) for r in (4, 5)] + [4 * n + r for n in range(4) for r in (22, 23)]


def place_of(step):
    T, step = divmod(step, NSI)
    return (T, step) + divmod(T, 2)


def row_item(step):
    return 0 <= step < STEPS and S_ITEMS[step % NSI][1] is not None


def bucket(d):
    if d < 16:
        return max(d, 0)
    f = np.float32(np.log(np.float32(d) / np.float32(16)))
    return min(16 + int(np.float32(f / np.float32(math.log(64)) * np.float32(16))), 31)


def constants():
    ident = np.eye(128, dtype=np.float32)
    line = np.zeros((33, 1024), np.float32)
    for x in range(1024):
        if x < 512:
            line[32, x] = NEG
        else:
            line[bucket(x - 512), x] = 1
    srow = np.zeros((32, 328), np.float32)
    for j in range(256):
        srow[bucket(256 - j), j] = 1
    srow[0, 256:264] = 1
    for b in range(8):
        for n in range(8):
            srow[bucket(256 - 32 * n - 31), 264 + 8 * b + n] = 1
    smask = np.zeros((128, 72), np.float32)
    for r in range(128):
        for b in range(8):
            if b != r % 8:
                smask[r, b] = NEG
                smask[r, 8 + 8 * b:16 + 8 * b] = NEG
    rep = np.tile(np.eye(16, dtype=np.float32), (1, 8))
    blk = np.kron(np.eye(8, dtype=np.float32), np.ones((16, 1), np.float32))
    return dict(c_ident=ident, c_line=line, c_srow=srow, c_smask=smask, c_rep=rep, c_blk=blk)


def decoder_step(nc, A, O):
    f32 = mybir.dt.float32
    f32r = mybir.dt.float32r
    i32 = mybir.dt.int32
    ALU = mybir.AluOpType
    ACT = mybir.ActivationFunctionType
    AX = mybir.AxisListType

    ctx = ExitStack()
    with ctx:
        base = (nc.sbuf_base + 63) // 64 * 64
        at = [base]

        def place(name, shape, dt=f32, offset=None):
            n = int(np.prod(shape[1:])) * 4
            if offset is None:
                offset = at[0]
                at[0] += (n + 31) // 32 * 32
            t = nc.alloc_sbuf_tensor_at(name, list(shape), dt, offset=offset)
            return t, offset

        def keep(name, *shape, dt=f32):
            return place(name, shape, dt)[0]

        x = keep("x", 128, KT, NT)
        o, o_at = place("o", (128, KT, NT))
        h_hi, h_at = place("h_hi", (128, KT, NT), f32r)
        h_lo = keep("h_lo", 128, KT, NT, dt=f32r)
        w_at = at[0]
        w_raw = [keep(f"w_raw{s}", 128, FH, 128) for s in range(2)]
        w_hi = [keep(f"w_hi{s}", 128, FH, 128, dt=f32r) for s in range(2)]
        w_lo = [keep(f"w_lo{s}", 128, FH, 128, dt=f32r) for s in range(2)]
        PT = keep("PT", 128, PT_TILES * 128)
        modT = keep("modT", 128, 4 * len(MODS), NC9)
        ident = keep("ident", 128, 128)
        ones = keep("ones", 128, 128)
        srow = keep("srow", 32, 328)
        smask = keep("smask", 128, 72)
        rep = keep("rep", 16, 128)
        blk = keep("blk", 128, 8)
        tab = keep("tab", 33, 16)
        tabr = keep("tabr", 32, 128)
        tabp = keep("tabp", 33, 16)
        sca = keep("sca", 128, KT, NS)
        scf = keep("scf", 128, 2, 2 * FT, NS)
        up10 = keep("up10", 128, 10, 2 * FT)
        z10 = keep("z10", 128, 10, KT)
        zflag = keep("zflag", 128, 1)
        hemb = keep("hemb", 128, 1)
        pti = keep("pti", 1, 16, dt=i32)
        n_at = at[0]
        rstd = keep("rstd", 128, NT)
        sq = keep("sq", 128, NT)
        sqt = [keep(f"sqt{s}", 128, NT) for s in range(2)]
        nt = [keep(f"nt{s}", 128, NT) for s in range(2)]
        hf = [keep(f"hf{s}", 128, NT) for s in range(2)]
        n_end = at[0]
        ts = keep("ts", 128, KT, NS)
        st = keep("st", 88, 5, 128)
        st_z = keep("st_z", 80, 128)
        z_at = at[0]

        def layer(start):
            pos = [start]

            def put(name, *shape, dt=f32):
                t, off = place(name, shape, dt, pos[0])
                pos[0] += (int(np.prod(shape[1:])) * 4 + 31) // 32 * 32
                assert pos[0] <= nc.sbuf_usable_end, (name, pos[0])
                return t
            put.pos = pos
            return put

        put = layer(z_at)
        act_hi = put("act_hi", 128, FH, NT, dt=f32r)
        act_lo = put("act_lo", 128, FH, NT, dt=f32r)
        ub = [put(f"ub{s}", 128, NT + 2) for s in range(2)]
        yb = [put(f"yb{s}", 128, NT) for s in range(2)]
        sg = put("sg", 128, NT)
        af = put("af", 128, NT)
        mw = {}
        for where, start, count in (("z", z_at, 3), ("h", h_at, 2), ("w", w_at, 2)):
            put = layer(start)
            for s in range(count):
                mw[f"{where}{s}"] = put(f"mw_{where}{s}", 128, KT, 512)
        put = layer(h_at)
        xs = put("xs", 128, 4, D)
        PR = put("PR", 128, PT_TILES, 128)
        line = put("line", 33, 1024)
        lrow = place("lrow", (16, 1024), f32, n_end - 4160)[0]
        put = layer(z_at)
        kT = put("kT", 128, 4, NT)
        kvt = put("kvt", 128, 4, 1536)
        kvs = put("kvs", NS, 1536)
        cb = put("cb", 128, 4, 16, 16)
        sc = put("sc", 128, 4, 16, 16)
        gat = put("gat", 128, 4, 48)
        gts = put("gts", NS, 48)
        gr = put("gr", 128, 3)
        kcT = put("kcT", 128, 2, 80)
        vcp = put("vcp", 16, 256)
        vcs = put("vcs", 64, 256)
        w2b = put("w2b", 128, 2, 128)
        a_at = put.pos[0]
        w1b = put("w1b", 128, 32, 128)
        put = layer(a_at)
        Hb = [put(f"Hb{s}", 128, 512) for s in range(4)]
        qT = [put(f"qT{s}", 128, NT) for s in range(2)]
        qs = put("qs", 128, KT, NS)
        mx = put("mx", 128, 4)
        nm = put("nm", 128, 4)
        den = put("den", 128, 8)
        cf = put("cf", 128, 4)
        g_at = put.pos[0]
        qT += [put(f"qT{s}", 128, NT) for s in range(2, 4)]
        put = layer(g_at)
        wg_hi = put("wg_hi", 128, KT, 48, dt=f32r)
        wg_lo = put("wg_lo", 128, KT, 48, dt=f32r)
        put = layer(n_at)
        Ss = [put(f"Ss{s}", 128, 512) for s in range(2)]
        Pb = [put(f"Pb{s}", 128, 512) for s in range(4)]
        PTb = [put(f"PTb{s}", 128, 512) for s in range(2)]
        assert put.pos[0] <= n_end
        put = layer(n_at + NT * 4)
        hx = put("hx", 128, 2, 80)
        hy = put("hy", 128, 2, 80)
        hz = put("hz", 128, 2, 80)
        per_ = put("per_", 32, 128)
        put = layer(h_at)
        RT = put("RT", 128, 2, 2592)
        pgc = [put(f"pgc{s}", 128, 2, 256) for s in range(4)]
        assert put.pos[0] <= h_at + 2 * KT * NT * 4
        okv = place("okv", (128, KT, NT), f32, o_at)[0]
        wg_raw = place("wg_raw", (128, KT, 48), f32, n_at + 3 * NT * 4)[0]
        line2 = place("line2", (33, 1024), f32, n_end - 4160)[0]
        gT = place("gT", (48, NT), f32, o_at)[0]
        Oacc = place("Oacc", (128, 4, D), f32, o_at)[0]
        put = layer(a_at)
        vblk = put("vblk", 128, 2, 512)
        cm = put("cm", 128, 64)
        cd = put("cd", 128, 64)
        put = layer(n_at)
        pcT = [put(f"pcT{s}", 128, 128) for s in range(2)]
        put = layer(z_at + 16512)
        vld = [put(f"vld{s}", 128, 4, 256) for s in range(4)]
        put = layer(h_at)
        kld = [put(f"kld{s}", 128, 4, 256) for s in range(4)]
        ksT = [put(f"ksT{s}", 128, 2, 512) for s in range(2)]
        Qm = put("Qm", 128, 2, NS * 128)
        assert put.pos[0] <= h_at + 2 * KT * NT * 4
        put = layer(n_at + 1216)
        Qa = put("Qa", 128, 2, 128)
        bias_s = put("bias_s", 128, 328)
        Sa = put("Sa", 128, 592)
        oR = put("oR", 128, 256)
        assert put.pos[0] <= n_end, (put.pos[0], n_end)
        put = layer(z_at + 8320 + 64)
        pTn = put("pTn", 64, 3, 128)
        oS = put("oS", 128, KT, NS)
        smx = put("smx", 128, 4)
        sden = put("sden", 128, 4)
        scof = put("scf_", 128, 4)
        put = layer(a_at)
        pTm = put("pTm", 128, 4, NS * 128)
        put = layer(z_at)
        yt = [put(f"yt{s}", 128, D) for s in range(2)]
        yts = put("yts", NS, D)

        pu = [ctx.enter_context(nc.psum_tensor(f"pu{s}", [128, 1024], f32)) for s in range(2)]
        pn = ctx.enter_context(nc.psum_tensor("pn", [128, 1024], f32))
        pm = [ctx.enter_context(nc.psum_tensor(f"pm{s}", [128, 512], f32))[:, :] for s in range(2)]
        prod = [p[:, PSO:PSO + NT] for p in pu]
        pnb = [pn[:, 0:512], pn[:, 512:1024]]

        def mod_places(q):
            k, c, _ = MODS[q]
            if k == 2 and c >= 4:
                out, tr = pu[0][:, 512 * (q % 2):512 * (q % 2) + 512], pu[1][:, 512 * (q % 2):512 * (q % 2) + 512]
            elif k in (0, 1, 3) and c >= 4:
                out, tr = pm[q % 2], pnb[q % 2]
            else:
                out, tr = pu[q % 2][:, 0:512], pu[q % 2][:, 512:1024]
            row = (nt if k in (0, 2) else hf if k == 4 or c < 4 else sqt)[q % 2][0:NC9, 0:512]
            return out[0:NC9, :], row, tr[:, 0:4 * NC9]

        lines_d = nc.dram_tensor("lines_d", [16, 1024], f32).ap()
        gates_d = nc.dram_tensor("gates_d", [8, 48], f32).ap()

        sems = {}

        def sem(name):
            if name not in sems:
                sems[name] = ctx.enter_context(nc.semaphore(name))
            return sems[name]

        def PTv(row, n):
            return PT[:, row:row + n]

        def site(k):
            b0 = 24 * k
            return modT[:, b0:b0 + 8, :], modT[:, b0 + 8:b0 + 16, :], modT[:, b0 + 16:b0 + 24, :] if k < 4 else None


        def turns(e, count, body, first=False):
            if first:
                body(0, True)
            with e.Fori(1 if first else 0, count) as i:
                body(i, False)

        def hold(e, semaphore, value):
            e.wait_ge(semaphore, value)
            e.sem_inc(S["passed"], 1)

        class Chain:

            def __init__(self, e, s):
                self.e, self.s, self.n, self.off = e, s, 0, 0

            def mark(self, ins):
                ins.then_inc(self.s, 1)
                self.n += 1

            def settle(self):
                self.e.wait_ge(self.s, self.off + self.n)

            def link(self, ins):
                self.mark(ins)
                self.settle()

            def turns(self, count, per, body, first=False):
                if first:
                    body(0, True)
                start = 1 if first else 0
                k0 = self.n
                with self.e.Fori(start, count) as i:
                    self.n, self.off = 0, k0 + (i - start) * per
                    body(i, False)
                    assert self.n == per, (self.n, per)
                self.off, self.n = 0, k0 + (count - start) * per

        names = """passed consts_in tables_in x_in tr_done tr_taken_a tr_taken_v ones_set tab_set prep_done
            lines_out mod_in_z0 mod_in_z1 mod_in_z2 mod_in_h0 mod_in_h1 mod_in_w0 mod_in_w1 mod_done mod_row mod_t mod_kept
            w_landed0 w_landed1 w_hi_ready w_lo_ready unit_done out_taken
            sq_ready sq_added norm_done rs_ready rstd_ready
            t_ready hf_ready hhi_ready hlo_ready x_updated dve_seq 
            z_made mixed mix_hi mix_lo z10_kept ub_zero
            conv_done silu_done af_ready act_hi_done act_lo_done up10_kept
            half_added s_tr s_taken s_out
            pe_in cmpw_in pages_in0 pages_in1 pages_in2 pages_in3
            w1_zero page_tr page_rows rt_rest hid_done hid_act hid_lin hid_tanh cmp_done cmp_kept pe_tr line_in
            cb_done cb_kept gate_w_in wg_hi_s wg_lo_s g_done g_tr g_kept g_sent g_back g_rt
            H_in0 H_in1 H_in2 H_in3 head_used q_in_sb 
            S_done S_biased nm_ready P_ready PT_done PT_kept_a PT_kept_v O_done O_kept
            c_max c_exp c_prob c_tr c_trk vrep_done v_blk c_out c_added
            sk_in0 sk_in1 sk_in2 sk_in3 sk_tr sk_sb q_zero q_set s_sc sn_done sS_bias s_exp s_p sP_tr sP_kept
            p_zero p_set sv_in0 sv_in1 sv_in2 sv_in3 sv_done oR_kept oR_tr oS_done oT_tr oh_ready olo_ready
            y_tr y_kept y_out0 y_out1 ys_out win_out kvp_out""".split()
        S = {n: sem(n) for n in names}

        w_mod = A["mod_w"].rearrange("l s (k p) n -> (l s) p k n", p=128)
        w_kvm = A["kv_mod_w"].rearrange("(k p) n -> p k n", p=128)
        w_ain = A["a_w_in"][0].rearrange("(k p) n -> p k n", p=128)
        w_aout = A["a_w_out"][0].rearrange("(k p) n -> p k n", p=128)
        w_up = A["ffn_w_up"].rearrange("l (k p) n -> l p k n", p=128)
        w_down = A["ffn_w_down"].rearrange("l (h k p) n -> (l h) p k n", p=128, h=2)
        w_kv = A["w_kv"].rearrange("(k p) n -> p k n", p=128)
        w_qg = A["b_w_qg"][0].rearrange("(k p) n -> p k n", p=128)
        w_bout = A["b_w_out"][0].rearrange("(g f p d) n -> f d g p n", g=2, f=2, p=4)

        block = ctx.enter_context(nc.Block())

        def w_wait(e, phase, i, s):
            e.wait_ge(S[f"w_landed{s}"], W0[phase] + WI[phase] * (i + 1))

        WI = {n: {"q": 32, "attn_out": 64}.get(n, 16) for n, _ in UNITS}
        W0, c0 = {}, 0
        for n, c in UNITS:
            W0[n] = c0
            c0 += WI[n] * (c // 2)
        NEXT = {n: m for (n, _), (m, _) in zip(UNITS, UNITS[1:]) if m not in ("q", "attn_out")}
        KOF = {n: FH if n.startswith("down") else KT for n, _ in UNITS}
        valid = [128, 88, 88, 128, 128, 8] + [128] * 12 + [72, 64]

        @block.sync
        def _(sp):
            for t, n in ((ident, "c_ident"), (srow, "c_srow"), (smask, "c_smask"), (rep, "c_rep"), (blk, "c_blk"),
                         (line, "c_line")):
                sp.dma_start(t[:, :], A[n]).then_inc(S["consts_in"], 16)
            sp.dma_start(tab[0:32, :], A["rel_bias"]).then_inc(S["consts_in"], 16)
            sp.dma_start(pti[:, :], A["page_table"].rearrange("a b -> (a b)").unsqueeze(0)).then_inc(S["consts_in"], 16)
            n_tab = 0
            for row, src in ((R_MODB, A["mod_b"].rearrange("l s (t c) -> (l s t) c", c=128)),
                             (96, A["kv_mod_b"].rearrange("(t c) -> t c", c=128)),
                             (R_KVG, A["kv_norm_g"].rearrange("(t c) -> t c", c=128)),
                             (R_ACB, A["a_conv_b"].rearrange("l (t c) -> (l t) c", c=128)),
                             (R_NG, A["norm_g"].rearrange("l s (t c) -> (l s t) c", c=128)),
                             (R_ACW, A["a_conv_w"].rearrange("l j (t c) -> (l j t) c", c=128)),
                             (R_FCB, A["ffn_conv_b"].rearrange("l (t c) -> (l t) c", c=128)),
                             (R_FCW, A["ffn_conv_w"].rearrange("l j (t c) -> (l j t) c", c=128)),
                             (R_STA, A["state_conv_a"].rearrange("l b j (t c) -> (l b j t) c", c=128)),
                             (R_STF, A["state_ffn_conv"].rearrange("l b j (t c) -> (l b j t) c", c=128)),
                             (R_C, A["c_prompt"].rearrange("b (t c) -> (b t) c", c=128)),
                             (R_C + 8, A["c_sample"].rearrange("b (t c) -> (b t) c", c=128)),
                             (R_XS, A["x_sample"].rearrange("b s (t c) -> (b s t) c", c=128))):
                n, k = src.shape[0], 0
                while k < n:
                    t, p = divmod(row + k, 128)
                    full = (n - k) // 128 if p == 0 else 0
                    if full:
                        sp.dma_start(PR[:, t:t + full, :], src[k:k + 128 * full, :].rearrange("(t p) c -> p t c", p=128))\
                          .then_inc(S["tables_in"], 16)
                        k += 128 * full
                    else:
                        m = min(128 - p, n - k)
                        sp.dma_start(PR[p:p + m, t, :], src[k:k + m, :]).then_inc(S["tables_in"], 16)
                        k += m
                    n_tab += 1
            assert n_tab == N_TABLES, n_tab
            sp.dma_start(xs[:, :, :], A["x_prompt"][0].rearrange("(i p) n -> p i n", p=128)).then_inc(S["x_in"], 16)

            def mod_weights(q):
                k, c, where = MODS[q]
                last = [p for p in range(q) if MODS[p][2] == where]
                if last:
                    sp.wait_ge(S["mod_done"], last[-1] + 1)
                src = w_kvm if k == 4 else w_mod[k]
                sp.dma_start(mw[where][:, :, :], src[:, :, 512 * c:512 * c + 512]).then_inc(S[f"mod_in_{where}"], 16)

            for q in range(3):
                mod_weights(q)

            def weights(phase, i, s, src, first=False):
                if not first:
                    hold(sp, S["w_lo_ready"], UBASE[phase] + 2 * i + s - 1)
                k = KOF[phase]
                sp.dma_start(w_raw[s][:, 0:k, :], src).then_inc(S[f"w_landed{s}"], 16)

            def mix_in_w(i, first, units=range(6)):
                for u in units:
                    part = (1, 2, 0)[u % 3]
                    col = part * D + (2 * i + u // 3) * 128
                    if not (first and u < 2):
                        hold(sp, S["w_lo_ready"], 6 * i + u - 1)
                    sp.dma_start(w_raw[u % 2][:, 0:KT, :], w_ain[:, :, bass.ds(col, 128)]).then_inc(S[f"w_landed{u % 2}"], 16)
            mix_in_w(0, True, units=range(2))
            for q in range(3, 6):
                mod_weights(q)
            mix_in_w(0, True, units=range(2, 6))
            with sp.Fori(1, 4) as i:
                mix_in_w(i, False)

            def out_w(phase, view):
                def body(i, first):
                    for s in range(2):
                        weights(phase, i, s, view[:, :, bass.ds(256 * i + 128 * s, 128)])
                turns(sp, 4, body)

            def up_w(phase, l, hh, between=None):
                def body(i, first):
                    for s in range(2):
                        weights(phase, i, s, w_up[l, :, :, bass.ds((hh * FH + i) * 128 + s * FF, 128)])
                body(0, True)
                if between is not None:
                    between()
                with sp.Fori(1, FH) as i:
                    body(i, False)

            def ffn_w(l, between):
                for hh in range(2):
                    up_w(f"up{l}{hh}", l, hh, between if hh == 0 else None)
                    out_w(f"down{l}{hh}", w_down[2 * l + hh])

            out_w("mix_out", w_aout)
            sp.wait_ge(S["unit_done"], UBASE["mix_out"])
            for q in range(6, 8):
                mod_weights(q)

            def mods_ffn0():
                sp.wait_ge(S["unit_done"], UBASE["up00"])
                for q in range(8, 12):
                    mod_weights(q)
            ffn_w(0, mods_ffn0)
            sp.wait_ge(S["unit_done"], UBASE["down01"])
            for q in range(12, 14):
                mod_weights(q)
            for c, slot in enumerate(KV_SLOTS):
                if c == 1:
                    sp.wait_ge(S["unit_done"], UBASE["kv"])
                    for q in range(14, 16):
                        mod_weights(q)
                for s in range(2):
                    weights("kv", c, s, w_kv[:, :, 256 * slot + 128 * s:256 * slot + 128 * s + 128])

            sp.wait_ge(S["unit_done"], UBASE["q"])
            for c in range(2):
                def cached(i, first):
                    for s in range(4):
                        if not (first and c == 0):
                            hold(sp, S["page_tr"], 8 * c + 4 * i + s - 3)
                        for g in range(2):
                            v = sp.value_load(pti[0:1, bass.ds(8 * i + 2 * s + g, 1)], min_val=0, max_val=19)
                            src = A["cache_kv"][bass.ds(v, 1), :, c].rearrange("o p g d -> (o p) (g d)")
                            sp.dma_start(pgc[s][:, g, :], src).then_inc(S[f"pages_in{s}"], 16)
                turns(sp, 2, cached, first=(c == 0))
                if c == 0:
                    sp.wait_ge(S["w1_zero"], 1)
                else:
                    sp.wait_ge(S["hid_done"], 1)
                    sp.wait_ge(S["cmp_done"], 1)
                for f in range(2):
                    sp.dma_start(w1b[64 * f:64 * f + 64, :, 64 * f:64 * f + 64],
                                 A["cmp_w1"][c].rearrange("(r d) n -> d r n", d=64)).then_inc(S["cmpw_in"], 16)
                    sp.dma_start(w2b[64 * f:64 * f + 64, c, 64 * f:64 * f + 64], A["cmp_w2"][c]).then_inc(S["cmpw_in"], 16)
                    sp.dma_start(per_[:, 64 * f:64 * f + 64], A["cmp_pe"][c]).then_inc(S["pe_in"], 16)
                if c == 0:
                    sp.dma_start(line2[:, :], A["c_line"]).then_inc(S["line_in"], 16)
                    sp.dma_start(wg_raw[:, :, :], w_qg[:, :, 1024:1072]).then_inc(S["gate_w_in"], 16)
                for q in ((16, 17), (18, 19))[c]:
                    mod_weights(q)
            sp.wait_ge(S["mod_done"], 20)
            sp.wait_ge(S["lines_out"], 16)
            def q_weights(T):
                gp, it = divmod(T, 2)
                for u in range(2):
                    sp.wait_ge(S["w_lo_ready"], UBASE["q"] + 2 * T + u - 1)
                    for f in range(2):
                        col = (8 * gp + 4 * f + 2 * it + u) * 64
                        sp.dma_start(w_raw[u][:, 0:KT, 64 * f:64 * f + 64], w_qg[:, :, col:col + 64])\
                          .then_inc(S[f"w_landed{u}"], 16)

            def bias_lines(T):
                gp, it = divmod(T, 2)
                for u in range(2):
                    for f in range(2):
                        k = 2 * u + f
                        if T > 0:
                            sp.wait_ge(S["head_used"], 4 * T + k - 3)
                        row = 8 * gp + 4 * f + 2 * it + u
                        src = bass.AP(lines_d.tensor, row * 1024 + 385, [[1, 128], [1, 512]])
                        sp.dma_start(Hb[k][:, :], src).then_inc(S[f"H_in{k}"], 16)
            for T in range(4):
                if T == 0:
                    q_weights(0)
                elif T == 1:
                    q_weights(2)
                elif T == 2:
                    q_weights(3)
                bias_lines(T)
                if T == 0:
                    q_weights(1)
            sp.wait_ge(S["unit_done"], UBASE["attn_out"])
            for q in range(20, 22):
                mod_weights(q)

            sp.wait_ge(S["unit_done"], UBASE["attn_out"])
            for part, done, ld in (("k", "sk_tr", kld), ("v", "sv_done", vld)):
                kv = 0 if part == "k" else 1
                if part == "v":
                    sp.wait_ge(S["O_kept"], 128)
                    sp.wait_ge(S["kvp_out"], 16 * 4)

                def cached_rows(i, first):
                    for s in range(4):
                        if not first:
                            hold(sp, S[done], 4 * i + s - 3)
                        for g in range(2):
                            v = sp.value_load(pti[0:1, bass.ds(8 * i + 2 * s + g, 1)], min_val=0, max_val=19)
                            src = A["cache_kv"][bass.ds(v, 1), :, 2 + kv].rearrange("o p g d -> (o p) (g d)")
                            sp.dma_start(ld[s][:, g, :], src).then_inc(S[f"s{part}_in{s}"], 16)
                        src = A["cache_win"][bass.ds(4 * i + s, 1), :, kv].rearrange("o (g p) h d -> (o p) g (h d)", p=128)
                        sp.dma_start(ld[s][:, 2:4, :], src).then_inc(S[f"s{part}_in{s}"], 16)
                turns(sp, 2, cached_rows, first=True)

            sp.wait_ge(S["mod_done"], 22)

            def bout(i, first):
                for s in range(2):
                    hold(sp, S["w_lo_ready"], UBASE["attn_out"] + 2 * i + s - 1)
                    for f in range(2):
                        for g in range(2):
                            sp.dma_start(w_raw[s][64 * f:64 * f + 64, 4 * g:4 * g + 4, :],
                                         w_bout[f][:, g, :, bass.ds(256 * i + 128 * s, 128)]).then_inc(S[f"w_landed{s}"], 16)
            turns(sp, 4, bout)
            sp.wait_ge(S["unit_done"], UBASE["attn_out"] + 1)
            for q in range(22, 24):
                mod_weights(q)

            def mods_ffn1():
                sp.wait_ge(S["unit_done"], UBASE["up10"])
                for q in range(24, 28):
                    mod_weights(q)
            ffn_w(1, mods_ffn1)

            for i in range(4):
                hold(sp, S["y_kept"], 2 * i + 2)
                sp.dma_start(O["y_prompt"][0, 128 * i:128 * i + 128, :], yt[i % 2][:, :]).then_inc(S[f"y_out{i % 2}"], 16)
            sp.wait_ge(S["y_kept"], 10)
            sp.dma_start(O["y_sample"].rearrange("b s n -> (b s) n"), yts[:, :]).then_inc(S["ys_out"], 16)
            sp.wait_ge(S["y_out0"], 32)
            sp.wait_ge(S["y_out1"], 32)
            sp.wait_ge(S["ys_out"], 16)

        @block.tensor
        def _(pe):
            mm = nc.tensor.matmul
            banks = [pnb[0], pnb[1], pm[0], pm[1]]
            group = [0]

            def tr_group(tiles):
                t = group[0]
                if t >= 4:
                    pe.wait_ge(S["tr_taken_a" if t % 2 == 0 else "tr_taken_v"], (t - 4) // 2 + 1)
                col = 0
                for src in tiles:
                    k, n = src.shape[0], src.free_size()
                    last = nc.tensor.transpose(banks[t % 4][0:n, col:col + k], src, ident[0:k, 0:k])
                    col += k
                last.then_inc(S["tr_done"], 1)
                group[0] += 1

            pe.wait_ge(S["consts_in"], 16 * 8)
            pe.wait_ge(S["tables_in"], 16 * N_TABLES)
            for g in range(5):
                tr_group([PR[0:valid[t], t, :] for t in range(4 * g, 4 * g + 4)])
            pe.wait_ge(S["x_in"], 16)
            for i in range(4):
                for kk in range(2):
                    tr_group([xs[:, i, 128 * k:128 * k + 128] for k in range(4 * kk, 4 * kk + 4)])
            pe.wait_ge(S["tab_set"], 1)
            for c in range(2):
                t = group[0]
                pe.wait_ge(S["tr_taken_a" if t % 2 == 0 else "tr_taken_v"], (t - 4) // 2 + 1)
                mm(banks[t % 4][0:16, :], tab[:, :], line[:, 512 * c:512 * c + 512], start=True, stop=True)\
                    .then_inc(S["tr_done"], 1)
                group[0] += 1

            def norm_sum(m):
                pe.wait_ge(S["sq_added"], 8 * (m + 1))
                if m == 0:
                    pe.wait_ge(S["ones_set"], 1)
                for hh in range(2):
                    last = mm(pn[:, PSO + HALF * hh:PSO + HALF * (hh + 1)], ones[:, :], sq[:, HALF * hh:HALF * (hh + 1)],
                              start=True, stop=True)
                last.then_inc(S["norm_done"], 1)

            def mod_product(q, tiles=range(KT)):
                where = MODS[q][2]
                use = sum(1 for m in MODS[:q] if m[2] == where)
                pe.wait_ge(S[f"mod_in_{where}"], 16 * (use + 1))
                if q >= 2:
                    pe.wait_ge(S["mod_row"], q - 1)
                for k in tiles:
                    last = mm(mod_places(q)[0], PT[:, R_C + k:R_C + 72:8], mw[where][:, k, :], start=(k == 0), stop=(k == KT - 1))
                if k == KT - 1:
                    last.then_inc(S["mod_done"], 1)

            def mod_transpose(q):
                row, tr = mod_places(q)[1:]
                pe.wait_ge(S["mod_row"], q + 1)
                if q >= 2:
                    pe.wait_ge(S["mod_kept"], q - 1)
                for t in range(4):
                    last = nc.tensor.transpose(tr[:, NC9 * t:NC9 * t + NC9], row[:, 128 * t:128 * t + 128],
                                               ident[0:NC9, 0:NC9])
                last.then_inc(S["mod_t"], 1)

            def mod_pair(q):
                for step in (mod_product, mod_transpose):
                    step(q)
                    step(q + 1)

            def mod_boundary(q, m, extra=None):
                mod_product(q, range(KT // 2))
                norm_sum(m)
                mod_product(q, range(KT // 2, KT))
                if extra is not None:
                    extra()
                for r in range(q + 1, q + 3):
                    mod_product(r)
                    mod_transpose(r - 1)
                norm_sum(m + 1)
                mod_transpose(q + 2)
                mod_product(q + 3)
                mod_transpose(q + 3)

            pe.wait_ge(S["tr_taken_a"], 8)
            pe.wait_ge(S["tr_taken_v"], 7)
            mod_pair(0)
            norm_sum(0)
            mod_pair(2)

            def unit(phase, i, s, hi, lo, slot=None, waits=()):
                n = UBASE[phase] + 2 * i + s
                pe.wait_ge(S["w_lo_ready"], n + 1)
                if slot is None:
                    slot = s
                    if not (isinstance(n, int) and n < 2):
                        pe.wait_ge(S["out_taken"], n - 1)
                else:
                    pe.wait_ge(S["out_taken"], n)
                kk = KOF[phase]
                for k in range(kk):
                    for name, value in waits:
                        pe.wait_ge(S[name], value + k)
                    for w, hs in ((w_hi[s], (hi, lo)), (w_lo[s], (hi,))):
                        for h in hs:
                            for c in range(2):
                                last = mm(pu[slot][:, PSO + HALF * c:PSO + HALF * (c + 1)], w[:, k, :],
                                          h[:, k, HALF * c:HALF * (c + 1)],
                                          start=(k == 0 and w is w_hi[s] and h is hi),
                                          stop=(k == kk - 1 and w is w_lo[s]))
                last.then_inc(S["unit_done"], 1)

            def phase(name, hi, lo, waits=(), extra=None):
                def body(i, first):
                    for u in range(2):
                        unit(name, i, u, hi, lo, waits=waits if first and u == 0 else ())
                    if first and extra is not None:
                        extra()
                turns(pe, dict(UNITS)[name] // 2, body, first=True)

            def ffn(l, q):
                gates = MOD_AT[2 * l + 1] + 4
                pe.wait_ge(S["rs_ready"], 4 * l + 3)
                mod_product(gates)
                mod_product(gates + 1)

                def gate_transposes():
                    mod_transpose(gates)
                    mod_transpose(gates + 1)
                for hh in range(2):
                    if hh == 0:
                        phase(f"up{l}0", h_hi, h_lo, waits=[("hlo_ready", 9 * q + 2)], extra=gate_transposes)
                    else:
                        phase(f"up{l}1", h_hi, h_lo)
                    phase(f"down{l}{hh}", act_hi, act_lo, waits=[("act_lo_done", FH * (2 * l + hh) + 1)])

            def kept_rows(p):
                pe.wait_ge(S["up10_kept"], 44 * (p + 1))
                for k in range(5):
                    bank = pm[0] if k < 4 else pm[1]
                    last = nc.tensor.transpose(bank[0:88, 128 * (k % 4):128 * (k % 4) + 128],
                                               up10[:, 2 * k:2 * k + 2, :].rearrange("p a b -> p (a b)"), ident[:, :])
                last.then_inc(S["s_tr"], 1)

            def mix_in(i, first):
                for u in range(6):
                    unit("mix_in", 3 * i + u // 2, u % 2, h_hi, h_lo, waits=[("hlo_ready", 2)] if first and u == 0 else ())
                    if first and u == 2:
                        mod_pair(4)
            turns(pe, 4, mix_in, first=True)
            phase("mix_out", act_hi, act_lo, waits=[("mix_lo", 1)])
            pe.wait_ge(S["out_taken"], UBASE["up00"])
            pe.wait_ge(S["z10_kept"], KT)
            nc.tensor.transpose(pm[0][0:80, 0:128], z10[:, :, :].rearrange("p a b -> p (a b)"), ident[:, :])\
                .then_inc(S["s_tr"], 1)
            mod_boundary(6, 1)
            ffn(0, 1)
            pe.wait_ge(S["out_taken"], UBASE["kv"])

            def first_kept_rows():
                pe.wait_ge(S["s_taken"], 1)
                kept_rows(0)
            mod_boundary(12, 3, extra=first_kept_rows)
            phase("kv", h_hi, h_lo, waits=[("hlo_ready", 9 * 2 + 2)])

            pe.wait_ge(S["out_taken"], UBASE["q"])
            pe.wait_ge(S["s_taken"], 2)
            tiles = [okv[:, m, :] for m in range(8)] + [kT[:, m, :] for m in range(4)]
            ordered = [tiles[2 * KV_SLOTS.index(sl) + g] for sl in range(6) for g in range(2)]
            for s3 in range(3):
                for i in range(4):
                    tr_group([ordered[4 * s3 + k][:, 128 * i:128 * i + 128] for k in range(4)])
            for s3 in range(3):
                t = group[0]
                pe.wait_ge(S["tr_taken_a" if t % 2 == 0 else "tr_taken_v"], (t - 4) // 2 + 1)
                for k in range(4):
                    last = nc.tensor.transpose(banks[t % 4][0:NS, 128 * k:128 * k + 128], ordered[4 * s3 + k][:, NP:NT],
                                               ident[:, :])
                last.then_inc(S["tr_done"], 1)
                group[0] += 1
            pe.wait_ge(S["tr_taken_a"], 15)
            pe.wait_ge(S["tr_taken_v"], 15)

            def cached_pages(c):
                def page(i, first):
                    for s in range(4):
                        n = 8 * c + 4 * i + s
                        pe.wait_ge(S[f"pages_in{s}"], 64 * c + 32 * (i + 1))
                        if not (c == 0 and first and s < 2):
                            pe.wait_ge(S["page_rows"], n - 1)
                        for gp in range(2):
                            for g in range(2):
                                last = nc.tensor.transpose(pm[s % 2][:, 256 * gp + 128 * g:256 * gp + 128 * g + 128],
                                                           pgc[s][:, g, 128 * gp:128 * gp + 128], ident[:, :])
                        last.then_inc(S["page_tr"], 1)
                turns(pe, 2, page, first=(c == 0))

            def hidden(c):
                pe.wait_ge(S["pe_in"], 32 * (c + 1))
                if c == 1:
                    pe.wait_ge(S["cmp_kept"], 1)
                nc.tensor.transpose(pnb[1][:, 0:32], per_[:, :], ident[0:32, 0:32]).then_inc(S["pe_tr"], 1)
                pe.wait_ge(S["cmpw_in"], 64 * (c + 1))
                pe.wait_ge(S["rt_rest"], 3 * (c + 1))
                pe.wait_ge(S["page_rows"], 8 * (c + 1))
                for r in range(32):
                    last = mm(pn[:, 0:162], w1b[:, r, :], RT[:, :, r:2592:32], start=(r == 0), stop=(r == 31))
                last.then_inc(S["hid_done"], 1)

            cached_pages(0)
            hidden(0)
            pe.wait_ge(S["line_in"], 16)
            for r in range(28):
                x0 = 32 * (r - 15) + 481
                last = mm(pm[0][:, 16 * r:16 * r + 16], line2[:, x0:x0 + 128], tabp[:, :], start=True, stop=True)
            last.then_inc(S["cb_done"], 1)
            pe.wait_ge(S["hid_act"], 1)
            mm(pnb[1][:, 0:160], w2b[:, 0, :], hx[:, :, :], start=True, stop=True).then_inc(S["cmp_done"], 1)
            mod_pair(16)
            pe.wait_ge(S["cb_kept"], 1)
            cached_pages(1)
            hidden(1)
            mod_product(18)
            pe.wait_ge(S["hid_act"], 2)
            for gp in range(2):
                mm(pnb[1][0:16, 128 * gp:128 * gp + 128], hx[:, gp, 0:16], w2b[:, 1, :], start=True, stop=True)
                last = mm(pnb[0][0:64, 128 * gp:128 * gp + 128], hx[:, gp, 16:80], w2b[:, 1, :], start=True, stop=True)
            last.then_inc(S["cmp_done"], 1)
            mod_transpose(18)
            mod_product(19)
            mod_transpose(19)
            pe.wait_ge(S["cmp_kept"], 2)

            pe.wait_ge(S["hlo_ready"], 9 * 4)
            pe.wait_ge(S["wg_lo_s"], 1)
            pe.wait_ge(S["mod_kept"], 20)
            for k in range(KT):
                for w, hs in ((wg_hi, (h_hi, h_lo)), (wg_lo, (h_hi,))):
                    for h in hs:
                        for c in range(2):
                            last = mm(pu[1][0:48, PSO + HALF * c:PSO + HALF * (c + 1)], w[:, k, :],
                                      h[:, k, HALF * c:HALF * (c + 1)], start=(k == 0 and w is wg_hi and h is h_hi),
                                      stop=(k == KT - 1 and w is wg_lo))
            last.then_inc(S["g_done"], 1)

            for u in range(2):
                unit("q", 0, u, h_hi, h_lo, slot=0)
            pe.wait_ge(S["g_rt"], 1)
            for i in range(4):
                nc.tensor.transpose(pm[0][:, 48 * i:48 * i + 48], gT[:, 128 * i:128 * i + 128], ident[0:48, 0:48])
            nc.tensor.transpose(pm[0][0:NS, 192:240], gT[:, NP:NT], ident[0:48, 0:48]).then_inc(S["g_tr"], 1)
            pe.wait_ge(S["g_kept"], 3)

            def query_part(T, u, k):
                n = UBASE["q"] + 2 * T + u
                if k == 0:
                    pe.wait_ge(S["w_lo_ready"], n + 1)
                    pe.wait_ge(S["out_taken"], n)
                for w, hs in ((w_hi[u], (h_hi, h_lo)), (w_lo[u], (h_hi,))):
                    for h in hs:
                        for c in range(2):
                            last = mm(pu[0][:, PSO + HALF * c:PSO + HALF * (c + 1)], w[:, k, :],
                                      h[:, k, HALF * c:HALF * (c + 1)], start=(k == 0 and w is w_hi[u] and h is h_hi),
                                      stop=(k == KT - 1 and w is w_lo[u]))
                if k == KT - 1:
                    last.then_inc(S["unit_done"], 1)


            def scores(step):
                T, step, gp, it = place_of(step)
                q_now = qT[2 * it:2 * it + 2]
                u, item = S_ITEMS[step]
                nS = NSI * T + step
                if item is None or S_ITEMS[step - 1][1] is None:
                    pe.wait_ge(S["q_in_sb"], 2 * T + u + 1)
                if not (T == 0 and step < 2):
                    pe.wait_ge(S["S_biased"], nS - 1)
                if item is None:
                    f = step % 2
                    for i in range(4):
                        last = mm(pnb[f][:, 16 * i:16 * i + 16], q_now[u][64 * f:64 * f + 64, 128 * i:128 * i + 128],
                                  kcT[64 * f:64 * f + 64, gp, 0:16], start=True, stop=True)
                else:
                    _, f, br, i = item
                    W = 128 * (i + 1)
                    last = mm(pnb[step % 2][:, 0:W], q_now[u][64 * f:64 * f + 64, 128 * i:128 * i + 128],
                              kT[64 * f:64 * f + 64, 2 * br + gp, 0:W], start=True, stop=True)
                last.then_inc(S["S_done"], 1)

            def flip(step):
                T, step, gp, it = place_of(step)
                _, item = S_ITEMS[step]
                m, f, br, i = item
                pe.wait_ge(S["P_ready"], 32 * T + m + 1)
                if not (T == 0 and m < 2):
                    pe.wait_ge(S["PT_kept_a" if m % 2 == 0 else "PT_kept_v"], 16 * T + m // 2)
                for j in range(i + 1):
                    last = nc.tensor.transpose(pm[m % 2][:, 128 * j:128 * j + 128],
                                               Pb[m % 4][:, 128 * j:128 * j + 128], ident[:, :])
                last.then_inc(S["PT_done"], 1)

            def weigh(step):
                T, step, gp, it = place_of(step)
                _, item = S_ITEMS[step]
                m, f, br, i = item
                pe.wait_ge(S["PT_kept_a" if m % 2 == 0 else "PT_kept_v"], 16 * T + m // 2 + 1)
                if not (T == 0 and m < 2):
                    pe.wait_ge(S["O_kept"], 32 * T + m - 1)
                col = (3 if br == 0 else 5) * 256 + (2 * gp + f) * 64
                for j in range(i + 1):
                    last = mm(pu[1][:, 512 * (m % 2):512 * (m % 2) + 64], PTb[m % 2][:, 128 * j:128 * j + 128],
                              kvt[:, j, col:col + 64], start=(j == 0), stop=(j == i))
                last.then_inc(S["O_done"], 1)

            for step in range(STEPS + 3):
                if step < STEPS:
                    scores(step)
                if row_item(step - 2):
                    flip(step - 2)
                if row_item(step - 3):
                    weigh(step - 3)
                T, r = divmod(step, NSI)
                if T < 3 and r in Q_STEPS:
                    query_part(T + 1, *divmod(Q_STEPS.index(r), KT))
            pe.wait_ge(S["O_kept"], 128)
            pe.wait_ge(S["PT_kept_a"], 64)
            pe.wait_ge(S["PT_kept_v"], 64)

            for gp in range(2):
                mm(pnb[gp][:, 0:128], rep[:, :], vcp[:, 128 * gp:128 * gp + 128], start=True, stop=True)\
                    .then_inc(S["vrep_done"], 1)

            pe.wait_ge(S["out_taken"], UBASE["attn_out"])
            mod_pair(20)
            kbanks = [pm, [pu[0][:, 0:512], pu[0][:, 512:1024]]]
            s_old, s_new = pu[1][:, 0:512], pu[1][:, 512:1024]

            def key_transposes(b):
                pe.wait_ge(S[f"sk_in{b % 4}"], 48 * (b // 4 + 1))
                if b >= 2:
                    pe.wait_ge(S["sk_sb"], b - 1)
                elif b == 1:
                    pe.wait_ge(S["mod_row"], 22)
                for gp in range(2):
                    for j in range(4):
                        last = nc.tensor.transpose(kbanks[b % 2][gp][:, 128 * j:128 * j + 128],
                                                   kld[b % 4][:, j, 128 * gp:128 * gp + 128], ident[:, :])
                last.then_inc(S["sk_tr"], 1)

            for b in range(NS + 1):
                if b < NS:
                    key_transposes(b)
                if b >= 1:
                    if b == 1:
                        pe.wait_ge(S["q_set"], 1)
                        pe.wait_ge(S["mod_kept"], 22)
                    pe.wait_ge(S["sk_sb"], b)
                    for gp in range(2):
                        last = mm(s_old, Qm[:, gp, 128 * (b - 1):128 * b], ksT[(b - 1) % 2][:, gp, :],
                                  start=(b == 1 and gp == 0), stop=(b == NS and gp == 1))
                    last.then_inc(S["s_sc"], 1)
            for c0, rhs in ((0, lambda gp: kT[:, gp, NP:NT]), (8, lambda gp: kT[:, 2 + gp, NP:NT]),
                            (16, lambda gp: kcT[:, gp, 16:80])):
                n = 64 if c0 == 16 else 8
                for gp in range(2):
                    mm(s_new[:, c0:c0 + n], Qa[:, gp, :], rhs(gp), start=(gp == 0), stop=(gp == 1))
            mm(s_new[:, 80:408], tabr[:, :], srow[:, :], start=True, stop=True).then_inc(S["sn_done"], 1)

            pe.wait_ge(S["c_prob"], 1)
            pe.wait_ge(S["v_blk"], 2)
            pe.wait_ge(S["sk_sb"], NS)
            for n in range(9):
                if n < 8:
                    i, gp = divmod(n, 2)
                    if n >= 2:
                        pe.wait_ge(S["c_trk"], n - 1)
                    nc.tensor.transpose(pm[n % 2][:, 0:128], sc[:, i, 8 * gp:8 * gp + 8, :].rearrange("p e n -> p (e n)"),
                                        ident[:, :]).then_inc(S["c_tr"], 1)
                if n >= 1:
                    k = n - 1
                    pe.wait_ge(S["c_trk"], k + 1)
                    if k >= 2:
                        pe.wait_ge(S["c_added"], k - 1)
                    mm(pnb[k % 2][:, :], pcT[k % 2][:, :], vblk[:, k % 2, :], start=True, stop=True)\
                        .then_inc(S["c_out"], 1)

            pe.wait_ge(S["c_added"], 8)
            pe.wait_ge(S["c_trk"], 8)
            pe.wait_ge(S["s_p"], 1)
            for j, c0 in enumerate((0, 128, 264, 392)):
                nc.tensor.transpose(pm[0][:, 128 * j:128 * j + 128], Sa[:, c0:c0 + 128], ident[:, :])
            for j, c0 in enumerate((256, 520)):
                nc.tensor.transpose(pm[1][0:8, 128 * j:128 * j + 128], Sa[:, c0:c0 + 8], ident[:, :])
            nc.tensor.transpose(pm[1][0:64, 256:384], Sa[:, 528:592], ident[:, :]).then_inc(S["sP_tr"], 1)
            pe.wait_ge(S["p_set"], 1)
            o_all = pnb[0][:, 0:256]
            for b in range(NS):
                pe.wait_ge(S[f"sv_in{b % 4}"], 48 * (b // 4 + 1))
                for j in range(4):
                    last = mm(o_all, pTm[:, j, 128 * b:128 * b + 128], vld[b % 4][:, j, :], start=(b == 0 and j == 0), stop=False)
                last.then_inc(S["sv_done"], 1)
            pe.wait_ge(S["sP_kept"], 2)
            mm(o_all, pTn[0:8, 0, :], kvs[:, 768:1024], start=False, stop=False)
            mm(o_all, pTn[0:8, 1, :], kvs[:, 1280:1536], start=False, stop=False)
            mm(o_all, pTn[0:64, 2, :], vcs[:, :], start=False, stop=True).then_inc(S["sv_done"], 1)
            pe.wait_ge(S["oR_kept"], 1)
            for gp in range(2):
                last = nc.tensor.transpose(pm[1][:, 128 * gp:128 * gp + 128], oR[:, 128 * gp:128 * gp + 128], ident[:, :])
            last.then_inc(S["oR_tr"], 1)

            for n in range(8):
                i, kk = divmod(n, 2)
                if n == 0:
                    pe.wait_ge(S["p_set"], 1)
                if n >= 2:
                    pe.wait_ge(S["olo_ready"], n - 1)
                bank = (pm[0], pnb[1])[n % 2]
                for t in range(4):
                    last = nc.tensor.transpose(bank[:, 128 * t:128 * t + 128],
                                               Oacc[:, i, 512 * kk + 128 * t:512 * kk + 128 * t + 128], ident[:, :])
                last.then_inc(S["oT_tr"], 1)
            pe.wait_ge(S["olo_ready"], 9)
            phase("attn_out", h_hi, h_lo)
            pe.wait_ge(S["out_taken"], UBASE["up10"])
            mod_boundary(22, 5)
            ffn(1, 4)
            norm_sum(7)
            kept_rows(1)
            pe.wait_ge(S["s_taken"], 3)
            pe.wait_ge(S["x_updated"], 9 * 4)
            for n in range(10):
                if n >= 4:
                    pe.wait_ge(S["y_kept"], n - 3)
                for k in range(4):
                    kk = 4 * (n % 2) + k
                    if n < 8:
                        i = n // 2
                        last = nc.tensor.transpose(banks[n % 4][:, 128 * k:128 * k + 128],
                                                   x[:, kk, 128 * i:128 * i + 128], ident[:, :])
                    else:
                        last = nc.tensor.transpose(banks[n % 4][0:NS, 128 * k:128 * k + 128], x[:, kk, NP:NT], ident[:, :])
                last.then_inc(S["y_tr"], 1)

        @block.scalar
        def _(act):
            fn = nc.scalar.activation
            banks = [pnb[0], pnb[1], pm[0], pm[1]]

            def split_hi(phase, i, s, first=False):
                w_wait(act, phase, i, s)
                if not first:
                    act.wait_ge(S["unit_done"], UBASE[phase] + 2 * i + s - 1)
                k = KOF[phase]
                fn(w_hi[s][:, 0:k, :], w_raw[s][:, 0:k, :], ACT.Copy).then_inc(S["w_hi_ready"], 1)

            def rows(first, last):
                for q in range(first, last):
                    out, row, _ = mod_places(q)
                    act.wait_ge(S["mod_done"], q + 1)
                    if q >= 2:
                        act.wait_ge(S["mod_t"], q - 1)
                    fn(row, out, ACT.Copy).then_inc(S["mod_row"], 1)

            def squares(m, tiles, waits, between={}):
                for k in range(KT):
                    for name, value in waits(k):
                        act.wait_ge(S[name], value)
                    if 8 * m + k >= 2:
                        act.wait_ge(S["sq_added"], 8 * m + k - 1)
                    fn(sqt[k % 2][:, :], tiles[:, k, :], ACT.Square).then_inc(S["sq_ready"], 1)
                    if k in between:
                        rows(between[k], between[k] + 1)

            def root(m):
                act.wait_ge(S["rs_ready"], m + 1)
                fn(rstd[:, :], rstd[:, :], ACT.Sqrt).then_inc(S["rstd_ready"], 1)

            def affine(q, scale, shift, gates=None):
                for k in range(KT):
                    act.wait_ge(S["t_ready"], 8 * q + k + 1)
                    if 8 * q + k >= 2:
                        act.wait_ge(S["hlo_ready"], 9 * ((8 * q + k - 2) // 8) + (8 * q + k - 2) % 8 + 2)
                    fn(hf[k % 2][:, 0:NP], nt[k % 2][:, 0:NP], ACT.Identity, bias=shift[:, k, 0:1], scale=scale[:, k, 0:1])\
                        .then_inc(S["hf_ready"], 1)
                    if gates is not None and k in (4, 7):
                        rows(gates + k // 7, gates + k // 7 + 1)

            for t in range(0, 13, 2):
                act.wait_ge(S["tr_done"], t + 1)
                bank = banks[t % 4]
                if t < 5:
                    col = 0
                    for tile in range(4 * t, 4 * t + 4):
                        n = valid[tile]
                        last = fn(PT[:, 128 * tile:128 * tile + n], bank[:, col:col + n], ACT.Copy)
                        col += n
                else:
                    i, kk = divmod(t - 5, 2)
                    last = fn(x[:, 4 * kk:4 * kk + 4, 128 * i:128 * i + 128], bank.rearrange("p (k c) -> p k c", k=4), ACT.Copy)
                last.then_inc(S["tr_taken_a"], 1)
            act.wait_ge(S["tr_done"], 15)
            fn(lrow[:, 512:1024], banks[2][0:16, :], ACT.Copy).then_inc(S["tr_taken_a"], 1)
            act.wait_ge(S["tr_taken_a"], 8)
            act.wait_ge(S["tr_taken_v"], 7)
            act.dma_start(lines_d, lrow[:, :]).then_inc(S["lines_out"], 16)
            squares(0, x, lambda k: [("prep_done", 1)] if k == 0 else [])

            rows(0, 2)
            root(0)
            rows(2, 4)
            act.wait_ge(S["lines_out"], 16)
            split_hi("mix_in", 0, 0, first=True)
            split_hi("mix_in", 0, 1, first=True)
            sh, s_, _ = site(0)
            affine(0, s_, sh)

            def mix_in(i, first, last_turn=False):
                for u in range(6):
                    j, part = 2 * i + u // 3, u % 3
                    n = 6 * i + u
                    act.wait_ge(S["unit_done"], n + 1)
                    if not (first and u < 3):
                        act.wait_ge(S["z_made" if part < 2 else "mixed"], j)
                    fn((sg, yb[0], af)[part][:, :], prod[u % 2], ACT.Copy).then_inc(S["out_taken"], 1)
                    if first and u == 2:
                        rows(4, 6)
                    if part == 2:
                        hold(act, S["mixed"], j + 1)
                        fn(act_hi[:, bass.ds(j, 1), :].rearrange("p o n -> p (o n)"), hf[0][:, :], ACT.Copy).then_inc(S["mix_hi"], 1)
                    if not last_turn or u < 4:
                        split_next(i, u)
                    else:
                        split_hi("mix_out", 0, u % 2)

            def split_next(i, u):
                s = u % 2
                k = 3 * i + u // 2 + 1
                w_wait(act, "mix_in", k, s)
                act.wait_ge(S["unit_done"], 2 * k + s - 1)
                fn(w_hi[s][:, 0:KT, :], w_raw[s][:, 0:KT, :], ACT.Copy).then_inc(S["w_hi_ready"], 1)
            act.wait_ge(S["hlo_ready"], 9)
            mix_in(0, True)
            for b in range(NS):
                act.dma_start(O["new_win_sample"][b, 0:PAST - 1].rearrange("t a g d -> t (a g d)"),
                              A["cache_win"][b, 1:PAST].rearrange("t a g d -> t (a g d)")).then_inc(S["win_out"], 16)
            for l in range(2):
                act.dma_start(O["new_ffn_conv_sample"][l, :, 0, :], A["state_ffn_conv"][l, :, 1, :]).then_inc(S["win_out"], 16)
            act.dma_start(O["new_conv_a_sample"][0, :, 0, :], A["state_conv_a"][0, :, 1, :]).then_inc(S["win_out"], 16)
            with act.Fori(1, 3) as i:
                mix_in(i, False)
            mix_in(3, False, last_turn=True)

            def out_phase(name, m, second=False, halves=0):
                if name == "attn_out":
                    split_hi(name, 0, 0)
                    split_hi(name, 0, 1)

                def body(i, first, last_turn=False):
                    for s in range(2):
                        n, k = UBASE[name] + 2 * i + s, 2 * i + s
                        act.wait_ge(S["unit_done"], n + 1)
                        if second:
                            act.wait_ge(S["half_added"], 8 * halves + k)
                            fn(nt[0][:, :], prod[s], ACT.Copy).then_inc(S["out_taken"], 1)
                        else:
                            act.sem_inc(S["passed"], 1)
                            fn(o[:, bass.ds(k, 1), :].rearrange("p a n -> p (a n)"), prod[s], ACT.Copy).then_inc(S["out_taken"], 1)
                        if not last_turn:
                            split_hi(name, i + 1, s)
                        elif m is None and name in NEXT:
                            split_hi(NEXT[name], 0, s)
                        if m is not None:
                            act.wait_ge(S["sq_added"], 8 * m + k - 1)
                            if second:
                                hold(act, S["half_added"], 8 * halves + k + 1)
                            else:
                                hold(act, S["out_taken"], n + 1)
                            fn(sqt[s][:, :], o[:, bass.ds(k, 1), :].rearrange("p a n -> p (a n)"), ACT.Square)\
                                .then_inc(S["sq_ready"], 1)
                    if last_turn and m is not None and name in NEXT:
                        for s in range(2):
                            split_hi(NEXT[name], 0, s)
                body(0, True)
                with act.Fori(1, 3) as i:
                    body(i, False)
                body(3, False, last_turn=True)

            def up_phase(name, half):

                def body(i, first, last_turn=False):
                    for s in range(2):
                        n = UBASE[name] + 2 * i + s
                        act.wait_ge(S["unit_done"], n + 1)
                        if not (half == 0 and first):
                            act.wait_ge(S["conv_done"], 2 * (FH * half + i) - 1 + s)
                            act.wait_ge(S["up10_kept"], 2 * (FH * half + i) - 1 + s)
                        elif half == 0:
                            act.wait_ge(S["ub_zero"], 1)
                        fn(ub[s][:, 2:2 + NT], prod[s], ACT.Copy).then_inc(S["out_taken"], 1)
                        if not last_turn:
                            split_hi(name, i + 1, s)
                        else:
                            split_hi(NEXT[name], 0, s)
                    j = FH * half + i
                    act.wait_ge(S["conv_done"], 2 * j + 2)
                    fn(sg[:, :], yb[1][:, :], ACT.Silu).then_inc(S["silu_done"], 1)
                    hold(act, S["af_ready"], j + 1)
                    fn(act_hi[:, bass.ds(i, 1), :].rearrange("p o n -> p (o n)"), af[:, :], ACT.Copy)\
                        .then_inc(S["act_hi_done"], 1)
                body(0, True)
                with act.Fori(1, FH - 1) as i:
                    body(i, False)
                body(FH - 1, False, last_turn=True)

            def ffn(l, q):
                sh, s_, _ = site(2 * l + 1)
                affine(q, s_, sh, gates=MOD_AT[2 * l + 1] + 4)
                if l == 1:
                    act.wait_ge(S["ub_zero"], 2)
                up_phase(f"up{l}0", 2 * l)
                out_phase(f"down{l}0", None)
                up_phase(f"up{l}1", 2 * l + 1)
                out_phase(f"down{l}1", 4 * l + 3, second=True, halves=l)

            def history_out(l):
                act.wait_ge(S["s_tr"], 2 + l)
                if l == 1:
                    act.wait_ge(S["s_out"], 16 * 5)
                fn(st[:, 0:4, :], pm[0][0:88, :].rearrange("p (a c) -> p a c", a=4), ACT.Copy)
                fn(st[:, 4, :], pm[1][0:88, 0:128], ACT.Copy).then_inc(S["s_taken"], 1)
                act.wait_ge(S["s_taken"], 2 + l)
                act.dma_start(O["new_ffn_conv_prompt"][l, 0].rearrange("j (t c) -> (j t) c", c=128), st[:, 0, :])\
                   .then_inc(S["s_out"], 16)
                for f in range(2):
                    dst = O["new_ffn_conv_sample"][l, :, 1, :].rearrange("(a f) (t c) -> f t a c", f=2, c=128)
                    act.dma_start(dst[f], st[44 * f:44 * f + 44, 1:5, :]).then_inc(S["s_out"], 16)

            out_phase("mix_out", 1)
            act.wait_ge(S["s_tr"], 1)
            fn(st_z[:, :], pm[0][0:80, 0:128], ACT.Copy).then_inc(S["s_taken"], 1)
            act.wait_ge(S["s_taken"], 1)
            act.dma_start(O["new_conv_a_prompt"][0, 0].rearrange("j (t c) -> (j t) c", c=128), st_z[0:16, :])\
               .then_inc(S["s_out"], 16)
            act.dma_start(O["new_conv_a_sample"][0, :, 1, :].rearrange("b (t c) -> b t c", c=128), st_z[16:80, :])\
               .then_inc(S["s_out"], 16)
            root(1)
            rows(6, 7)
            squares(2, x, lambda k: [("x_updated", k + 2)], between={1: 7, 6: 8})
            root(2)
            rows(9, 10)
            ffn(0, 1)
            root(3)
            rows(12, 13)
            history_out(0)
            squares(4, x, lambda k: [("x_updated", 9 + k + 2)], between={1: 13, 6: 14})
            root(4)
            rows(15, 16)

            sh, s_, _ = site(4)
            affine(2, s_, sh)
            for c in range(6):
                for s in range(2):
                    m = 2 * c + s
                    act.wait_ge(S["unit_done"], UBASE["kv"] + m + 1)
                    dst = okv[:, m, :] if m < 8 else kT[:, m - 8, :]
                    if m == 8:
                        act.wait_ge(S["hlo_ready"], 27)
                    fn(dst, prod[s], ACT.Copy).then_inc(S["out_taken"], 1)
                    if c < 5:
                        split_hi("kv", c + 1, s)
            for n in range(15):
                t = 15 + n
                if t % 2:
                    continue
                act.wait_ge(S["tr_done"], t + 1)
                if n < 12:
                    dst, src = kvt[:, n % 4, 512 * (n // 4):512 * (n // 4) + 512], banks[t % 4]
                else:
                    dst, src = kvs[:, 512 * (n - 12):512 * (n - 12) + 512], banks[t % 4][0:NS, :]
                fn(dst, src, ACT.Copy).then_inc(S["tr_taken_a"], 1)
            act.wait_ge(S["tr_taken_a"], 15)
            act.wait_ge(S["tr_taken_v"], 15)
            act.dma_start(O["new_kv_prompt"][0].rearrange("(i p) s g d -> p i (s g d)", p=128), kvt[:, :, 0:1024])\
               .then_inc(S["kvp_out"], 16)
            act.dma_start(O["new_win_prompt"][0].rearrange("(i p) s g d -> p i (s g d)", p=128), kvt[:, :, 1024:1536])\
               .then_inc(S["kvp_out"], 16)
            act.dma_start(O["new_kv_sample"].rearrange("b o s g d -> (b o) (s g d)"), kvs[:, 0:1024]).then_inc(S["kvp_out"], 16)
            act.dma_start(O["new_win_sample"][:, PAST - 1].rearrange("b s g d -> b (s g d)"), kvs[:, 1024:1536])\
               .then_inc(S["kvp_out"], 16)

            for c in range(2):
                def page_rows(i, first):
                    for s in range(2):
                        hold(act, S["page_tr"], 8 * c + 2 * i + s + 1)
                        fn(RT[:, :, bass.ds(NP + 512 * i + 256 * s, 256)], pm[s][:, :].rearrange("p (g n) -> p g n", g=2),
                           ACT.Copy).then_inc(S["page_rows"], 1)
                if c == 1:
                    act.wait_ge(S["hid_done"], 1)
                turns(act, 4, page_rows)
                act.wait_ge(S["pe_tr"], c + 1)
                for g in range(2):
                    last = fn(RT[:, g, 2560:2592], pnb[1][:, 0:32], ACT.Copy)
                last.then_inc(S["rt_rest"], 1)
                act.wait_ge(S["hid_lin"], c + 1)
                fn(hz[:, :, :], hy[:, :, :], ACT.Tanh, scale=math.sqrt(2.0 / math.pi)).then_inc(S["hid_tanh"], 1)
                if c == 0:
                    act.wait_ge(S["cb_done"], 1)
                    for i in range(4):
                        last = fn(cb[:, i, :, :].rearrange("p e n -> p n e"),
                                  pm[0][:, 64 * i:64 * i + 256].rearrange("p (n e) -> p n e", e=16)[:, ::-1, :], ACT.Copy)
                    last.then_inc(S["cb_kept"], 1)
                else:
                    rows(18, 19)
                act.wait_ge(S["cmp_done"], c + 1)
                if c == 0:
                    fn(kcT[:, :, :], pnb[1][:, 0:160].rearrange("p (g n) -> p g n", g=2), ACT.Copy).then_inc(S["cmp_kept"], 1)
                    rows(16, 18)
                else:
                    fn(vcp[:, :], pnb[1][0:16, 0:256], ACT.Copy)
                    fn(vcs[:, :], pnb[0][0:64, 0:256], ACT.Copy).then_inc(S["cmp_kept"], 1)
                    act.wait_ge(S["gate_w_in"], 16)
                    fn(wg_hi[:, :, :], wg_raw[:, :, :], ACT.Copy).then_inc(S["wg_hi_s"], 1)
                    rows(19, 20)

            sh, s_, _ = site(2)
            affine(3, s_, sh)
            split_hi("q", 0, 0)
            split_hi("q", 0, 1)
            act.wait_ge(S["g_done"], 1)
            fn(gT[:, :], pu[1][0:48, PSO:PSO + NT], ACT.Exp, scale=-1.0).then_inc(S["g_kept"], 1)
            def queries(T, u):
                n = UBASE["q"] + 2 * T + u
                q_tile = qT[2 * (T % 2) + u]
                act.wait_ge(S["unit_done"], n + 1)
                if T >= 2:
                    act.wait_ge(S["S_done"], NSI * (T - 1))
                fn(q_tile[:, :], prod[0], ACT.Copy, scale=0.125).then_inc(S["out_taken"], 1)
                act.wait_ge(S["out_taken"], n + 1)
                fn(qs[:, 2 * T + u, :], q_tile[:, NP:NT], ACT.Copy).then_inc(S["q_in_sb"], 1)
                if T < 3:
                    split_hi("q", T + 1, u)

            queries(0, 0)
            queries(0, 1)
            act.wait_ge(S["g_tr"], 1)
            fn(gat[:, :, :], pm[0][:, 0:192].rearrange("p (i n) -> p i n", i=4), ACT.Copy).then_inc(S["g_kept"], 1)
            fn(gts[:, :], pm[0][0:NS, 192:240], ACT.Copy).then_inc(S["g_kept"], 1)
            act.wait_ge(S["g_kept"], 3)
            act.dma_start(gates_d, gts[:, :]).then_inc(S["g_sent"], 16)

            def expo(step):
                T, step, gp, it = place_of(step)
                m, f, br, i = S_ITEMS[step][1]
                act.wait_ge(S["nm_ready"], 32 * T + m + 1)
                if not (T == 0 and m < 4):
                    act.wait_ge(S["PT_done"], 32 * T + m - 3)
                    if not (T == 0 and m < 8):
                        act.wait_ge(S["O_kept"], 32 * T + m - 7)
                W = 128 * (i + 1)
                fn(Pb[m % 4][:, 0:W], Ss[m % 2][:, 0:W], ACT.Exp, bias=nm[:, m % 4:m % 4 + 1],
                   accum_out=den[:, m % 8:m % 8 + 1]).then_inc(S["P_ready"], 1)

            def keep_t(step):
                T, step, gp, it = place_of(step)
                m, f, br, i = S_ITEMS[step][1]
                if m % 2:
                    return
                act.wait_ge(S["PT_done"], 32 * T + m + 1)
                if not (T == 0 and m < 2):
                    act.wait_ge(S["O_done"], 32 * T + m - 1)
                W = 128 * (i + 1)
                fn(PTb[0][:, 0:W], pm[0][:, 0:W], ACT.Copy).then_inc(S["PT_kept_a"], 1)

            for step in range(STEPS + 2):
                if row_item(step):
                    expo(step)
                if row_item(step - 2):
                    keep_t(step - 2)
                T, r = divmod(step, NSI)
                if T < 3 and r in (18, NSI - 1):
                    queries(T + 1, r // (NSI - 1))
                if step == 15:
                    act.wait_ge(S["g_sent"], 16)
                    act.dma_start(gr[:, :], bass.AP(gates_d.tensor, 0, [[3, 16], [48, 8], [1, 3]]))\
                       .then_inc(S["g_back"], 16)
            rows(20, 22)

            act.wait_ge(S["c_max"], 1)
            fn(sc[:, :, :, :].rearrange("p i e n -> p (i e n)"), sc[:, :, :, :].rearrange("p i e n -> p (i e n)"), ACT.Exp)\
                .then_inc(S["c_exp"], 1)
            for b in range(NS):
                act.wait_ge(S["sk_tr"], b + 1)
                if b >= 2:
                    act.wait_ge(S["s_sc"], b - 1)
                for gp in range(2):
                    last = fn(ksT[b % 2][:, gp, :], (pm[gp], pu[0][:, 512 * gp:512 * gp + 512])[b % 2], ACT.Copy)
                last.then_inc(S["sk_sb"], 1)
            for n in range(8):
                act.wait_ge(S["c_tr"], n + 1)
                if n >= 2:
                    act.wait_ge(S["c_out"], n - 1)
                fn(pcT[n % 2][:, :], pm[n % 2][:, 0:128], ACT.Copy).then_inc(S["c_trk"], 1)
            act.wait_ge(S["sS_bias"], 1)
            for br, c0, n in ((0, 0, 264), (1, 264, 264), (2, 528, 64)):
                last = fn(Sa[:, c0:c0 + n], Sa[:, c0:c0 + n], ACT.Exp, bias=smx[:, br:br + 1], accum_out=sden[:, br:br + 1])
            last.then_inc(S["s_exp"], 1)
            act.wait_ge(S["sP_tr"], 1)
            fn(pTn[0:8, 0:2, :], pm[1][0:8, 0:256].rearrange("p (k r) -> p k r", k=2), ACT.Copy).then_inc(S["sP_kept"], 1)
            fn(pTn[0:64, 2, :], pm[1][0:64, 256:384], ACT.Copy).then_inc(S["sP_kept"], 1)
            act.wait_ge(S["sv_done"], NS + 1)
            fn(oR[:, :], pnb[0][:, 0:256], ACT.Copy).then_inc(S["oR_kept"], 1)
            act.wait_ge(S["oR_tr"], 1)
            for gp in range(2):
                for f in range(2):
                    r0 = 128 * gp + 32 * (2 * gp + f)
                    last = fn(oS[64 * f:64 * f + 64, 4 * gp:4 * gp + 4, :].rearrange("p q b -> p (q b)"),
                              pm[1][64 * f:64 * f + 64, r0:r0 + 32], ACT.Copy)
            last.then_inc(S["oS_done"], 1)

            for n in range(8):
                i, kk = divmod(n, 2)
                act.wait_ge(S["oT_tr"], n + 1)
                bank = (pm[0], pnb[1])[n % 2]
                fn(h_hi[:, 4 * kk:4 * kk + 4, 128 * i:128 * i + 128], bank.rearrange("p (t c) -> p t c", t=4), ACT.Copy)\
                    .then_inc(S["oh_ready"], 1)
            act.wait_ge(S["oS_done"], 1)
            fn(h_hi[:, :, NP:NT], oS[:, :, :], ACT.Copy).then_inc(S["oh_ready"], 1)

            act.wait_ge(S["olo_ready"], 9)
            out_phase("attn_out", 5)
            root(5)
            rows(22, 23)
            squares(6, x, lambda k: [("x_updated", 18 + k + 2)], between={1: 23, 6: 24})
            root(6)
            rows(25, 26)
            ffn(1, 4)
            root(7)
            history_out(1)
            for n in range(10):
                act.wait_ge(S["y_tr"], n + 1)
                if n < 8:
                    i = n // 2
                    if i >= 2:
                        act.wait_ge(S[f"y_out{i % 2}"], 16)
                    fn(yt[i % 2][:, 512 * (n % 2):512 * (n % 2) + 512], banks[n % 4], ACT.Copy).then_inc(S["y_kept"], 1)
                else:
                    fn(yts[:, 512 * (n % 2):512 * (n % 2) + 512], banks[n % 4][0:NS, :], ACT.Copy).then_inc(S["y_kept"], 1)
            act.wait_ge(S["win_out"], 16 * 11)
            act.wait_ge(S["kvp_out"], 16 * 4)
            act.wait_ge(S["s_out"], 16 * 8)

        @block.vector
        def _(dve):
            v = nc.vector
            banks = [pnb[0], pnb[1], pm[0], pm[1]]
            ch = Chain(dve, S["dve_seq"])

            def wide(ap, n):
                return ap.unsqueeze(2).to_broadcast([ap.shape[0], ap.shape[1], n])

            v.memset(ones[:, :], 1.0).then_inc(S["ones_set"], 1)
            v.memset(tab[32:33, :], 1.0).then_inc(S["tab_set"], 1)
            dve.wait_ge(S["consts_in"], 16 * 8)
            dve.wait_ge(S["tab_set"], 1)
            v.tensor_copy(tabp[:, :].rearrange("t (g q f) -> t g q f", g=2, q=4),
                          tab[:, :].rearrange("t (g f q) -> t g q f", g=2, f=2))
            v.tensor_copy(tabr[:, :].rearrange("t (h b) -> t h b", b=NS), wide(tab[0:32, :], NS))

            for t in range(1, 15, 2):
                dve.wait_ge(S["tr_done"], t + 1)
                bank = banks[t % 4]
                if t < 5:
                    col = 0
                    for tile in range(4 * t, 4 * t + 4):
                        n = valid[tile]
                        last = v.tensor_copy(PT[:, 128 * tile:128 * tile + n], bank[:, col:col + n])
                        col += n
                elif t < 13:
                    i, kk = divmod(t - 5, 2)
                    last = v.tensor_copy(x[:, 4 * kk:4 * kk + 4, 128 * i:128 * i + 128], bank.rearrange("p (k c) -> p k c", k=4))
                else:
                    last = v.tensor_copy(lrow[:, 0:512], banks[1][0:16, :])
                last.then_inc(S["tr_taken_v"], 1)

            dve.wait_ge(S["tr_taken_a"], 7)
            dve.wait_ge(S["tr_taken_v"], 7)
            ch.link(v.tensor_copy(x[:, :, NP:NT], PTv(R_XS, 64).rearrange("p (b k) -> p k b", k=KT)))

            def history(out, state, w, n, tmp):
                st_ = state.rearrange("p (b j k) -> p j k b", b=NS, j=2)
                ch.mark(v.tensor_tensor(out, st_[:, 0], wide(w[:, 0:n], NS), ALU.mult))
                ch.link(v.tensor_tensor(tmp, st_[:, 1], wide(w[:, n:2 * n], NS), ALU.mult))
                ch.link(v.tensor_tensor(out, out, tmp, ALU.add))
            history(sca[:, :, :], PTv(R_STA, 128), PTv(R_ACW, 24), KT, ts[:, :, :])
            for l in range(2):
                history(scf[:, l], PTv(R_STF + 704 * l, 704), PTv(R_FCW + 132 * l, 132), 2 * FT,
                        nt[0][:, 0:352].rearrange("p (k b) -> p k b", b=NS))
            v.tensor_copy(st_z[0:1, 0:1], ones[0:1, 0:1]).then_inc(S["prep_done"], 1)

            def mods(first, last):
                for q in range(first, last):
                    dve.wait_ge(S["mod_t"], q + 1)
                    ft = 24 * MODS[q][0] + 4 * MODS[q][1]
                    v.tensor_tensor(modT[:, ft:ft + 4, :], mod_places(q)[2].rearrange("p (t r) -> p t r", t=4),
                                    wide(PT[:, ft:ft + 4], NC9), ALU.add).then_inc(S["mod_kept"], 1)

            def norm_scale(k, kept):
                s_ = site(k)[1]
                dve.wait_ge(S["mod_kept"], kept)
                ch.link(v.scalar_tensor_tensor(s_, s_, 1.0, wide(PTv(R_NG + 16 * k, 8) if k < 4 else PTv(R_KVG, 8), NC9),
                                               ALU.add, ALU.mult))

            def norm_gate(k, kept):
                gate = site(k)[2]
                dve.wait_ge(S["mod_kept"], kept)
                ch.link(v.tensor_tensor(gate, gate, wide(PTv(R_NG + 16 * k + 8, 8), NC9), ALU.mult))

            def mean(m):
                dve.wait_ge(S["norm_done"], m + 1)
                ch.link(v.tensor_scalar(rstd[:, :], pn[:, PSO:PSO + NT], 1.0 / D, EPS, ALU.mult, ALU.add))
                v.reciprocal(rstd[:, :], rstd[:, :]).then_inc(S["rs_ready"], 1)
                dve.wait_ge(S["rstd_ready"], m + 1)

            rs_s = rstd[:, NP:NT].unsqueeze(1).to_broadcast([128, KT, NS])

            def modulate(q, scale, shift):
                if q > 0:
                    dve.wait_ge(S["hlo_ready"], 9 * q)
                ch.link(v.tensor_tensor(ts[:, :, :], x[:, :, NP:NT], rs_s, ALU.mult))
                ch.link(v.tensor_tensor(ts[:, :, :], ts[:, :, :], scale[:, :, 1:NC9], ALU.mult))
                ch.link(v.tensor_tensor(ts[:, :, :], ts[:, :, :], shift[:, :, 1:NC9], ALU.add))
                v.tensor_copy(h_hi[:, :, NP:NT], ts[:, :, :]).then_inc(S["hhi_ready"], 1)
                for k in range(KT + 1):
                    if k < KT:
                        if 8 * q + k >= 2:
                            dve.wait_ge(S["hf_ready"], 8 * q + k - 1)
                        v.tensor_tensor(nt[k % 2][:, 0:NP], x[:, k, 0:NP], rstd[:, 0:NP], ALU.mult).then_inc(S["t_ready"], 1)
                    if k > 0:
                        dve.wait_ge(S["hf_ready"], 8 * q + k)
                        v.tensor_copy(h_hi[:, k - 1, 0:NP], hf[(k - 1) % 2][:, 0:NP]).then_inc(S["hhi_ready"], 1)

            def update(p, gate):
                ch.link(v.tensor_tensor(ts[:, :, :], o[:, :, NP:NT], rs_s, ALU.mult))
                ch.link(v.tensor_tensor(ts[:, :, :], ts[:, :, :], gate[:, :, 1:NC9], ALU.mult))
                v.tensor_tensor(x[:, :, NP:NT], x[:, :, NP:NT], ts[:, :, :], ALU.add).then_inc(S["x_updated"], 1)
                for k in range(KT):
                    ch.link(v.tensor_tensor(nt[k % 2][:, 0:NP], o[:, k, 0:NP], rstd[:, 0:NP], ALU.mult))
                    v.scalar_tensor_tensor(x[:, k, 0:NP], nt[k % 2][:, 0:NP], gate[:, k, 0:1], x[:, k, 0:NP], ALU.mult, ALU.add)\
                     .then_inc(S["x_updated"], 1)
                dve.wait_ge(S["x_updated"], 9 * (p + 1))

            def conv(y, u, w, b, history_term):
                ch.link(v.tensor_scalar(y[:, :], u[:, 2:2 + NT], w[2], b, ALU.mult, ALU.add))
                ch.mark(v.tensor_tensor(y[:, NP:NT], y[:, NP:NT], history_term, ALU.add))
                ch.link(v.scalar_tensor_tensor(y[:, 0:NP], u[:, 1:1 + NP], w[1], y[:, 0:NP], ALU.mult, ALU.add))
                return v.scalar_tensor_tensor(y[:, 0:NP], u[:, 0:NP], w[0], y[:, 0:NP], ALU.mult, ALU.add)

            mods(0, 2)
            mean(0)
            mods(2, 4)
            norm_scale(0, 4)
            sh, s_, _ = site(0)
            modulate(0, s_, sh)

            def mix(i, first):
                for e in range(2):
                    j = 2 * i + e
                    dve.wait_ge(S["out_taken"], 6 * i + 3 * e + 2)
                    if first and e == 0:
                        dve.wait_ge(S["ub_zero"], 1)
                    else:
                        dve.wait_ge(S["z10_kept"], j)
                    ch.link(v.tensor_tensor(ub[0][:, 2:2 + NT], sg[:, :], yb[0][:, :], ALU.mult))
                    v.tensor_copy(zflag[:, 0:1], ub[0][:, 2:3]).then_inc(S["z_made"], 1)
                    w = [PT[:, bass.ds(R_ACW + 8 * t + j, 1)] for t in range(3)]
                    ch.link(conv(yb[1], ub[0], w, PT[:, bass.ds(R_ACB + j, 1)],
                                 sca[:, bass.ds(j, 1), :].rearrange("p o b -> p (o b)")))
                    dve.wait_ge(S["out_taken"], 6 * i + 3 * e + 3)
                    if first and e == 0:
                        dve.wait_ge(S["hlo_ready"], 9)
                        mods(4, 6)
                    else:
                        dve.wait_ge(S["mix_lo"], j)
                    v.tensor_tensor(hf[0][:, :], yb[1][:, :], af[:, :], ALU.mult).then_inc(S["mixed"], 1)
            ch.turns(4, 10, mix, first=True)

            norm_gate(0, 6)
            mean(1)
            update(0, site(0)[2])
            mods(6, 9)
            mean(2)
            mods(9, 10)
            norm_scale(1, 10)

            def ffn_pairs(l, half, half_l):
                gates = MOD_AT[2 * l + 1] + 4
                def body(i, first):
                    j = FH * half + i
                    for s in range(2):
                        n = UBASE[f"up{l}{half_l}"] + 2 * i + s
                        dve.wait_ge(S["out_taken"], n + 1)
                        if not (half == 0 and first):
                            dve.wait_ge(S["silu_done" if s else "af_ready"], j)
                        ft = FH * half_l + i + FT * s
                        w = [PT[:, bass.ds(R_FCW + 132 * l + 44 * t + ft, 1)] for t in range(3)]
                        conv(yb[s], ub[s], w, PT[:, bass.ds(R_FCB + 44 * l + ft, 1)],
                             scf[:, l, bass.ds(ft, 1), :].rearrange("p o b -> p (o b)")).then_inc(S["conv_done"], 1)
                    if first and half_l == 0:
                        mods(gates, gates + 2)
                    dve.wait_ge(S["silu_done"], j + 1)
                    dve.wait_ge(S["conv_done"], 2 * j + 1)
                    if not (half == 0 and first):
                        dve.wait_ge(S["act_lo_done"], j)
                    v.tensor_tensor(af[:, :], sg[:, :], yb[0][:, :], ALU.mult).then_inc(S["af_ready"], 1)
                ch.turns(FH, 6, body, first=(half_l == 0))

            def add_halves(l):
                def body(i, first):
                    for s in range(2):
                        dve.wait_ge(S["out_taken"], UBASE[f"down{l}1"] + 2 * i + s + 1)
                        ok = o[:, bass.ds(2 * i + s, 1), :].rearrange("p a n -> p (a n)")
                        v.tensor_tensor(ok, ok, nt[0][:, :], ALU.add).then_inc(S["half_added"], 1)
                turns(dve, 4, body)

            def ffn(l, q):
                sh, s_, _ = site(2 * l + 1)
                modulate(q, s_, sh)
                ffn_pairs(l, 2 * l, 0)
                ffn_pairs(l, 2 * l + 1, 1)
                add_halves(l)

            ffn(0, 1)
            norm_gate(1, 12)
            mean(3)
            update(1, site(1)[2])
            mods(12, 15)
            mean(4)
            mods(15, 16)
            norm_scale(4, 16)
            sh, s_, _ = site(4)
            modulate(2, s_, sh)

            for n in range(15):
                t = 15 + n
                if t % 2 == 0:
                    continue
                dve.wait_ge(S["tr_done"], t + 1)
                if n < 12:
                    dst, src = kvt[:, n % 4, 512 * (n // 4):512 * (n // 4) + 512], banks[t % 4]
                else:
                    dst, src = kvs[:, 512 * (n - 12):512 * (n - 12) + 512], banks[t % 4][0:NS, :]
                v.tensor_copy(dst, src).then_inc(S["tr_taken_v"], 1)

            for c in range(2):
                dve.wait_ge(S["hid_done"], c + 1)
                if c == 1:
                    dve.wait_ge(S["cmp_done"], 1)
                hid = pn[:, 0:162].rearrange("p (g n) -> p g n", g=2)
                ch.link(v.tensor_copy(hemb[:, :], pn[:, 80:81]))
                ch.link(v.tensor_scalar(hx[:, :, :], hid[:, :, 0:80], hemb[:, 0:1], None, ALU.add))
                ch.link(v.tensor_tensor(hy[:, :, :], hx[:, :, :], hx[:, :, :], ALU.mult))
                ch.link(v.tensor_tensor(hy[:, :, :], hy[:, :, :], hx[:, :, :], ALU.mult))
                v.scalar_tensor_tensor(hy[:, :, :], hy[:, :, :], 0.044715, hx[:, :, :], ALU.mult, ALU.add)\
                    .then_inc(S["hid_lin"], 1)
                dve.wait_ge(S["hid_tanh"], c + 1)
                ch.link(v.tensor_scalar(hz[:, :, :], hz[:, :, :], 1.0, 0.5, ALU.add, ALU.mult))
                v.tensor_tensor(hx[:, :, :], hx[:, :, :], hz[:, :, :], ALU.mult).then_inc(S["hid_act"], 1)
                mods(*((16, 18), (18, 20))[c])

            dve.wait_ge(S["cb_kept"], 1)
            dve.wait_ge(S["wg_hi_s"], 1)
            v.tensor_tensor(wg_lo[:, :, :], wg_raw[:, :, :], wg_hi[:, :, :].bitcast(f32), ALU.subtract).then_inc(S["wg_lo_s"], 1)
            norm_scale(2, 20)
            sh, s_, _ = site(2)
            modulate(3, s_, sh)
            dve.wait_ge(S["g_kept"], 1)
            ch.link(v.tensor_scalar_add(gT[:, :], gT[:, :], 1.0))
            v.reciprocal(gT[:, :], gT[:, :]).then_inc(S["g_rt"], 1)
            dve.wait_ge(S["g_kept"], 3)

            def bias(step):
                T, step, gp, it = place_of(step)
                u, item = S_ITEMS[step]
                dve.wait_ge(S["S_done"], NSI * T + step + 1)
                if item is None:
                    e = 8 * gp + 4 * it + 2 * u + step % 2
                    v.tensor_tensor(sc[:, :, bass.ds(e, 1), :].rearrange("p i o n -> p i (o n)"),
                                    pnb[step % 2][:, 0:64].rearrange("p (i n) -> p i n", i=4),
                                    cb[:, :, bass.ds(e, 1), :].rearrange("p i o n -> p i (o n)"), ALU.add)\
                        .then_inc(S["S_biased"], 1)
                    return
                m, f, br, i = item
                W = 128 * (i + 1)
                if not (T == 0 and m < 2):
                    dve.wait_ge(S["P_ready"], 32 * T + m - 1)
                dve.wait_ge(S[f"H_in{2 * u + f}"], 16 * (T + 1))
                v.tensor_tensor_reduce(out=Ss[m % 2][:, 0:W], in0=pnb[step % 2][:, 0:W],
                                       in1=Hb[2 * u + f][:, 0:W][:, ::-1], scale=1.0, scalar=-3.0e38,
                                       op0=ALU.add, op1=ALU.max, accum_out=mx[:, m % 4:m % 4 + 1])\
                    .then_inc(S["S_biased"], 1)
                dve.wait_ge(S["S_biased"], NSI * T + step + 1)
                ins = v.tensor_scalar(nm[:, m % 4:m % 4 + 1], mx[:, m % 4:m % 4 + 1], -1.0, None, ALU.mult)
                ins.then_inc(S["nm_ready"], 1)
                if br == 1 and i == 0:
                    v.tensor_copy(zflag[:, 0:1], ones[:, 0:1]).then_inc(S["head_used"], 1)

            def keep_t(step):
                T, step, gp, it = place_of(step)
                m, f, br, i = S_ITEMS[step][1]
                if m % 2 == 0:
                    return
                dve.wait_ge(S["PT_done"], 32 * T + m + 1)
                if not (T == 0 and m < 2):
                    dve.wait_ge(S["O_done"], 32 * T + m - 1)
                W = 128 * (i + 1)
                v.tensor_copy(PTb[1][:, 0:W], pm[1][:, 0:W]).then_inc(S["PT_kept_v"], 1)

            def gather(step):
                T, step, gp, it = place_of(step)
                u = S_ITEMS[step][0]
                m, f, br, i = S_ITEMS[step][1]
                dve.wait_ge(S["P_ready"], 32 * T + m + 1)
                c = cf[:, m % 4:m % 4 + 1]
                ch.link(v.reciprocal(c, den[:, m % 8:m % 8 + 1]))
                gcol = 3 * (8 * gp + 4 * f + 2 * it + u) + 1 + br
                ch.link(v.tensor_tensor(c, c, gat[:, i, bass.ds(gcol, 1)], ALU.mult))
                dve.wait_ge(S["O_done"], 32 * T + m + 1)
                dst = Oacc[:, i, bass.ds(64 * (8 * gp + 4 * it + 2 * u + f), 64)]
                O_ = pu[1][:, 512 * (m % 2):512 * (m % 2) + 64]
                if br == 0:
                    ins = v.tensor_scalar(dst, O_, c, None, ALU.mult)
                else:
                    ins = v.scalar_tensor_tensor(dst, O_, c, dst, ALU.mult, ALU.add)
                ins.then_inc(S["O_kept"], 1)

            for step in range(STEPS + 4):
                if step < STEPS:
                    bias(step)
                if row_item(step - 2):
                    keep_t(step - 2)
                if row_item(step - 4):
                    gather(step - 4)
            dve.wait_ge(S["O_kept"], 128)

            def sample_queries():
                dve.wait_ge(S["q_in_sb"], 8)
                dve.wait_ge(S["q_zero"], 1)
                for gp in range(2):
                    for f in range(2):
                        half, c0 = slice(64 * f, 64 * f + 64), 32 * (2 * gp + f)
                        v.tensor_copy(Qa[half, gp, c0:c0 + 32], qs[half, 4 * gp:4 * gp + 4, :].rearrange("p q b -> p (q b)"))
                        for q in range(4):
                            c1 = c0 + 8 * q
                            last = v.tensor_copy(Qm[half, gp, c1:c1 + 7 * 129 + 1:129], qs[half, 4 * gp + q, :])
                last.then_inc(S["q_set"], 1)

            rows = sc[:, :, :, :].rearrange("p i e n -> p (i e) n")
            ch.link(v.tensor_reduce(cm[:, :], rows, AX.X, ALU.max))
            ch.link(v.tensor_scalar(cm[:, :], cm[:, :], FLOOR, None, ALU.max))
            v.tensor_tensor(rows, rows, wide(cm[:, :], 16), ALU.subtract).then_inc(S["c_max"], 1)
            sample_queries()
            mods(20, 22)
            for gp in range(2):
                dve.wait_ge(S["vrep_done"], gp + 1)
                for q in range(4):
                    e = 2 * q
                    last = v.tensor_tensor(vblk[:, gp, 128 * q:128 * q + 128].rearrange("p (f d) -> p f d", f=2),
                                           pnb[gp][:, 0:128].rearrange("p (f d) -> p f d", f=2), wide(blk[:, e:e + 2], 64), ALU.mult)
                last.then_inc(S["v_blk"], 1)
            dve.wait_ge(S["c_exp"], 1)
            ch.link(v.tensor_reduce(cd[:, :], rows, AX.X, ALU.add))
            ch.link(v.tensor_scalar(cd[:, :], cd[:, :], 1.0e-30, None, ALU.max))
            ch.link(v.reciprocal(cd[:, :], cd[:, :]))
            gq = gat[:, :, :].rearrange("p i (g f q b) -> p i g q f b", g=2, f=2, q=4)
            cdv = cd[:, :].rearrange("p (i g q f) -> p i g q f", i=4, g=2, q=4)
            for i in range(4):
                for g in range(2):
                    ch.mark(v.tensor_tensor(cdv[:, i, g], cdv[:, i, g], gq[:, i, g, :, :, 0], ALU.mult))
            ch.settle()
            v.tensor_tensor(rows, rows, wide(cd[:, :], 16), ALU.mult).then_inc(S["c_prob"], 1)
            for n in range(8):
                i, g = divmod(n, 2)
                dve.wait_ge(S["c_out"], n + 1)
                dst = Oacc[:, i, 512 * g:512 * g + 512]
                v.tensor_tensor(dst, dst, pnb[n % 2], ALU.add).then_inc(S["c_added"], 1)

            dve.wait_ge(S["kvp_out"], 16 * 4)
            dve.wait_ge(S["sn_done"], 1)
            s_old, s_new = pu[1][:, 0:512], pu[1][:, 512:1024]
            ch.link(v.tensor_copy(bias_s[:, :], s_new[:, 80:408]))
            for k, c0 in enumerate((0, 264)):
                ch.mark(v.tensor_tensor(Sa[:, c0:c0 + 256], s_old[:, 256 * k:256 * k + 256], bias_s[:, 0:256], ALU.add))
                ch.mark(v.tensor_tensor(Sa[:, c0 + 256:c0 + 264], s_new[:, 8 * k:8 * k + 8], bias_s[:, 256:264], ALU.add))
            ch.link(v.tensor_tensor(Sa[:, 528:592], s_new[:, 16:80], bias_s[:, 264:328], ALU.add))
            for c0, n, m0 in ((256, 8, 0), (520, 8, 0), (528, 64, 8)):
                ch.mark(v.tensor_tensor(Sa[:, c0:c0 + n], Sa[:, c0:c0 + n], smask[:, m0:m0 + n], ALU.add))
            ch.settle()
            for br, c0, n in ((0, 0, 264), (1, 264, 264), (2, 528, 64)):
                ch.mark(v.tensor_reduce(smx[:, br:br + 1], Sa[:, c0:c0 + n], AX.X, ALU.max))
            ch.settle()
            v.tensor_scalar(smx[:, 0:3], smx[:, 0:3], -1.0, None, ALU.mult).then_inc(S["sS_bias"], 1)
            dve.wait_ge(S["s_exp"], 1)
            dve.wait_ge(S["g_back"], 16)
            ch.link(v.reciprocal(scof[:, 0:3], sden[:, 0:3]))
            for br, gcol in ((0, 1), (1, 2), (2, 0)):
                ch.mark(v.tensor_tensor(scof[:, br:br + 1], scof[:, br:br + 1], gr[:, gcol:gcol + 1], ALU.mult))
            ch.settle()
            for br, c0, n in ((0, 0, 264), (1, 264, 264), (2, 528, 64)):
                last = v.tensor_scalar(Sa[:, c0:c0 + n], Sa[:, c0:c0 + n], scof[:, br:br + 1], None, ALU.mult)
            last.then_inc(S["s_p"], 1)
            dve.wait_ge(S["sP_tr"], 1)
            dve.wait_ge(S["p_zero"], 1)
            for b in range(NS):
                last = v.tensor_copy(pTm[:, :, 128 * b + b:128 * b + 128:8],
                                     pm[0][:, :].rearrange("p (j r) -> p j r", j=4)[:, :, b:128:8])
            last.then_inc(S["p_set"], 1)

            for n in range(8):
                i, kk = divmod(n, 2)
                dve.wait_ge(S["oh_ready"], n + 1)
                bank = (pm[0], pnb[1])[n % 2].rearrange("p (t c) -> p t c", t=4)
                v.tensor_tensor(h_lo[:, 4 * kk:4 * kk + 4, 128 * i:128 * i + 128], bank,
                                h_hi[:, 4 * kk:4 * kk + 4, 128 * i:128 * i + 128].bitcast(f32), ALU.subtract)\
                    .then_inc(S["olo_ready"], 1)
            dve.wait_ge(S["oh_ready"], 9)
            dve.wait_ge(S["oS_done"], 1)
            v.tensor_tensor(h_lo[:, :, NP:NT], oS[:, :, :], h_hi[:, :, NP:NT].bitcast(f32), ALU.subtract)\
                .then_inc(S["olo_ready"], 1)

            norm_gate(2, 22)
            mean(5)
            update(2, site(2)[2])
            mods(22, 25)
            mean(6)
            mods(25, 26)
            norm_scale(3, 26)
            ffn(1, 4)
            norm_gate(3, 28)
            mean(7)
            update(3, site(3)[2])

        @block.gpsimd
        def _(pool):
            g = nc.gpsimd

            def split_lo(phase, i, s):
                n, k = UBASE[phase] + 2 * i + s, KOF[phase]
                pool.wait_ge(S["w_hi_ready"], n + 1)
                g.tensor_tensor(w_lo[s][:, 0:k, :], w_raw[s][:, 0:k, :], w_hi[s][:, 0:k, :].bitcast(f32), ALU.subtract)\
                    .then_inc(S["w_lo_ready"], 1)

            def add_square(m, k, s, first):
                pool.wait_ge(S["sq_ready"], 8 * m + k + 1)
                if first:
                    if m > 0:
                        pool.wait_ge(S["norm_done"], m)
                    g.tensor_copy(sq[:, :], sqt[s][:, :]).then_inc(S["sq_added"], 1)
                else:
                    pool.wait_ge(S["sq_added"], 8 * m + k)
                    g.tensor_tensor(sq[:, :], sq[:, :], sqt[s][:, :], ALU.add).then_inc(S["sq_added"], 1)

            def trail(q):
                for k in range(KT + 1):
                    pool.wait_ge(S["hhi_ready"], 9 * q + k + 1)
                    if k == 0:
                        dst, full, hi = h_lo[:, :, NP:NT], ts[:, :, :], h_hi[:, :, NP:NT]
                    else:
                        dst, full, hi = h_lo[:, k - 1, 0:NP], hf[(k - 1) % 2][:, 0:NP], h_hi[:, k - 1, 0:NP]
                    g.tensor_tensor(dst, full, hi.bitcast(f32), ALU.subtract).then_inc(S["hlo_ready"], 1)

            for k in range(KT):
                add_square(0, k, k % 2, k == 0)
            split_lo("mix_in", 0, 0)
            split_lo("mix_in", 0, 1)
            trail(0)
            pool.wait_ge(S["mod_done"], 4)
            for s in range(2):
                last = g.memset(ub[s][:, 0:2], 0.0)
            last.then_inc(S["ub_zero"], 1)

            def mix(i, first, last_turn=False):
                for u in range(6):
                    j, part = 2 * i + u // 3, u % 3
                    if part == 1:
                        pool.wait_ge(S["z_made"], j + 1)
                        g.tensor_copy(z10[:, :, bass.ds(j, 1)].rearrange("p t o -> p (t o)"), ub[0][:, NP:NP + 10])\
                            .then_inc(S["z10_kept"], 1)
                    if part == 2:
                        pool.wait_ge(S["mix_hi"], j + 1)
                        g.tensor_tensor(act_lo[:, bass.ds(j, 1), :].rearrange("p o n -> p (o n)"), hf[0][:, :],
                                        act_hi[:, bass.ds(j, 1), :].rearrange("p o n -> p (o n)").bitcast(f32), ALU.subtract)\
                            .then_inc(S["mix_lo"], 1)
                    if not last_turn or u < 4:
                        s = u % 2
                        pool.wait_ge(S["w_hi_ready"], 6 * i + u + 3)
                        g.tensor_tensor(w_lo[s][:, 0:KT, :], w_raw[s][:, 0:KT, :], w_hi[s][:, 0:KT, :].bitcast(f32), ALU.subtract)\
                            .then_inc(S["w_lo_ready"], 1)
                    else:
                        split_lo("mix_out", 0, u % 2)
            mix(0, True)
            with pool.Fori(1, 3) as i:
                mix(i, False)
            mix(3, False, last_turn=True)

            def out_phase(name, m):
                if name == "attn_out":
                    split_lo(name, 0, 0)
                    split_lo(name, 0, 1)

                def body(i, first, last_turn=False):
                    for s in range(2):
                        if not last_turn:
                            split_lo(name, i + 1, s)
                        elif m is None and name in NEXT:
                            split_lo(NEXT[name], 0, s)
                        if m is not None:
                            add_square(m, 2 * i + s, s, first and s == 0)
                    if last_turn and m is not None and name in NEXT:
                        for s in range(2):
                            split_lo(NEXT[name], 0, s)
                body(0, True)
                with pool.Fori(1, 3) as i:
                    body(i, False)
                body(3, False, last_turn=True)

            def up_phase(name, half, half_l):
                def body(i, first, last_turn=False):
                    j = FH * half + i
                    for s in range(2):
                        if not last_turn:
                            split_lo(name, i + 1, s)
                        else:
                            split_lo(NEXT[name], 0, s)
                        pool.wait_ge(S["out_taken"], UBASE[name] + 2 * i + s + 1)
                        g.tensor_copy(up10[:, :, bass.ds(FH * half_l + i + FT * s, 1)].rearrange("p t o -> p (t o)"),
                                      ub[s][:, NP:NP + 10]).then_inc(S["up10_kept"], 1)
                    pool.wait_ge(S["act_hi_done"], j + 1)
                    g.tensor_tensor(act_lo[:, bass.ds(i, 1), :].rearrange("p o n -> p (o n)"), af[:, :],
                                    act_hi[:, bass.ds(i, 1), :].rearrange("p o n -> p (o n)").bitcast(f32), ALU.subtract)\
                        .then_inc(S["act_lo_done"], 1)
                body(0, True)
                with pool.Fori(1, FH - 1) as i:
                    body(i, False)
                body(FH - 1, False, last_turn=True)

            def ffn(l, q):
                trail(q)
                up_phase(f"up{l}0", 2 * l, 0)
                out_phase(f"down{l}0", None)
                up_phase(f"up{l}1", 2 * l + 1, 1)
                out_phase(f"down{l}1", 4 * l + 3)

            out_phase("mix_out", 1)
            for k in range(KT):
                add_square(2, k, k % 2, k == 0)
            ffn(0, 1)
            for k in range(KT):
                add_square(4, k, k % 2, k == 0)
            trail(2)
            for c in range(1, 6):
                for s in range(2):
                    split_lo("kv", c, s)
            pool.wait_ge(S["unit_done"], UBASE["kv"] + 1)
            g.memset(w1b[:, :, :], 0.0)
            g.memset(w2b[:, :, :], 0.0).then_inc(S["w1_zero"], 1)
            for c in range(2):
                pool.wait_ge(S["out_taken"], UBASE["q"])
                pool.wait_ge(S["unit_done"], UBASE["q"])
                if c == 1:
                    pool.wait_ge(S["hid_done"], 1)
                for gp in range(2):
                    g.tensor_copy(RT[:, gp, 0:NP], okv[:, 2 * c + gp, 0:NP]).then_inc(S["rt_rest"], 1)
            trail(3)
            split_lo("q", 0, 0)
            split_lo("q", 0, 1)
            for T in range(3):
                for u in range(2):
                    split_lo("q", T + 1, u)
            pool.wait_ge(S["unit_done"], UBASE["attn_out"])
            g.memset(Qm[:, :, :], 0.0)
            pool.wait_ge(S["O_kept"], 128)
            g.memset(Qa[:, :, :], 0.0).then_inc(S["q_zero"], 1)
            pool.wait_ge(S["q_set"], 1)
            pool.wait_ge(S["c_out"], 8)
            g.memset(pTm[:, :, :], 0.0).then_inc(S["p_zero"], 1)
            out_phase("attn_out", 5)
            for k in range(KT):
                add_square(6, k, k % 2, k == 0)
            for s in range(2):
                last = g.memset(ub[s][:, 0:2], 0.0)
            last.then_inc(S["ub_zero"], 1)
            ffn(1, 4)


_INS = ['x_prompt', 'x_sample', 'c_prompt', 'c_sample', 'cache_kv', 'cache_win', 'state_conv_a', 'state_ffn_conv',
        'page_table', 'mod_w', 'mod_b', 'norm_g', 'a_w_in', 'a_conv_w', 'a_conv_b', 'a_w_out', 'kv_mod_w', 'kv_mod_b',
        'kv_norm_g', 'w_kv', 'cmp_pe', 'cmp_w1', 'cmp_w2', 'b_w_qg', 'b_w_out', 'rel_bias', 'ffn_w_up', 'ffn_conv_w',
        'ffn_conv_b', 'ffn_w_down']
_OUTS = [('y_prompt', (1, 512, 1024)), ('y_sample', (8, 1, 1024)), ('new_kv_prompt', (1, 512, 4, 4, 64)),
         ('new_kv_sample', (8, 1, 4, 4, 64)), ('new_win_prompt', (1, 512, 2, 4, 64)), ('new_win_sample', (8, 256, 2, 4, 64)),
         ('new_conv_a_prompt', (1, 1, 2, 1024)), ('new_conv_a_sample', (1, 8, 2, 1024)),
         ('new_ffn_conv_prompt', (2, 1, 2, 5632)), ('new_ffn_conv_sample', (2, 8, 2, 5632))]


def kernel(**inputs):
    import numpy as _np
    import concourse.bacc as _bacc
    from concourse import mybir as _mybir
    from concourse.bass_utils import run_bass_kernel_spmd as _run

    nc = _bacc.Bacc("TRN2", target_bir_lowering=False, num_devices=1)
    arrays, ins, outs = {}, {}, {}
    tables = constants()
    for name in _INS + list(tables):
        a = _np.ascontiguousarray(inputs[name] if name in inputs else tables[name])
        arrays[f"in_{name}"] = a
        ins[name] = nc.dram_tensor(f"in_{name}", a.shape, _mybir.dt.from_np(a.dtype), kind="ExternalInput").ap()
    for name, shape in _OUTS:
        outs[name] = nc.dram_tensor(f"out_{name}", shape, _mybir.dt.float32, kind="ExternalOutput").ap()
    decoder_step(nc, ins, outs)
    r = _run(nc, [arrays], core_ids=[0])
    return tuple(r.results[0][f"out_{name}"] for name, _ in _OUTS)
```
